# Optimizing a Trainium2 kernel written in Bass

```python
import jax, jax.numpy as jnp
from jax import lax
import numpy as np

D_MODEL = 1024
BATCH = 1
SEQ = 512
DEPTH = 2

N_A_LAYERS = DEPTH // 2
N_B_LAYERS = DEPTH - N_A_LAYERS
MLSTM_HEADS = 8
MLSTM_QK_DIM = D_MODEL // 2 // MLSTM_HEADS
MLSTM_V_DIM = D_MODEL // MLSTM_HEADS
MLSTM_CHUNK = 64
MLSTM_SPLITS = [MLSTM_HEADS * MLSTM_QK_DIM, MLSTM_HEADS * MLSTM_QK_DIM, MLSTM_HEADS * MLSTM_V_DIM,
                MLSTM_HEADS * MLSTM_V_DIM, MLSTM_HEADS, MLSTM_HEADS]
MLSTM_IN = sum(MLSTM_SPLITS)
FOX_HEADS = 16
FOX_HEAD_DIM = D_MODEL // FOX_HEADS
FOX_BLOCK = 128
D_FF = 2816
CONV_WIDTH = 3
EPS = 1e-6


def rmsnorm(x, w):
    xf = x.astype(jnp.float32)
    y = xf * lax.rsqrt(jnp.mean(xf * xf, axis=-1, keepdims=True) + EPS)
    return (y * w.astype(jnp.float32)).astype(x.dtype)

def mlstm_mixer(h, w_in, b_gate, w_head_norm, w_out):
    B, S, _ = h.shape
    H, DK, DV, L = MLSTM_HEADS, MLSTM_QK_DIM, MLSTM_V_DIM, MLSTM_CHUNK
    NC = S // L
    proj = h @ w_in
    idx = list(np.cumsum(MLSTM_SPLITS)[:-1])
    q, k, v, o, ig, fg = jnp.split(proj, idx, axis=-1)
    f32 = jnp.float32
    ig = ig.astype(f32) + b_gate[:H].astype(f32)
    lf = jax.nn.log_sigmoid(fg.astype(f32) + b_gate[H:].astype(f32))

    def to_chunks(t, d):
        return t.astype(f32).reshape(B, NC, L, H, d).transpose(1, 0, 3, 2, 4)

    qc = to_chunks(q, DK) * (DK ** -0.5)
    kc = to_chunks(k, DK)
    vc = to_chunks(v, DV)
    ic = ig.reshape(B, NC, L, H).transpose(1, 0, 3, 2)
    fc = lf.reshape(B, NC, L, H).transpose(1, 0, 3, 2)
    causal = jnp.tril(jnp.ones((L, L), dtype=bool))

    def step(carry, inp):
        C, n, m = carry
        qt, kt, vt, it, ft = inp
        b = jnp.cumsum(ft, axis=-1)
        dmat = jnp.where(causal, b[..., :, None] - b[..., None, :] + it[..., None, :], -jnp.inf)
        m_inter = b + m[..., None]
        m_t = jnp.maximum(m_inter, jnp.max(dmat, axis=-1))
        s = jnp.einsum('bhtd,bhsd->bhts', qt, kt) * jnp.exp(dmat - m_t[..., None])
        w_inter = jnp.exp(m_inter - m_t)
        num = jnp.einsum('bhts,bhse->bhte', s, vt) + w_inter[..., None] * jnp.einsum('bhtd,bhde->bhte', qt, C)
        den = jnp.sum(s, axis=-1) + w_inter * jnp.einsum('bhtd,bhd->bht', qt, n)
        ht = num / jnp.maximum(jnp.abs(den), jnp.exp(-m_t))[..., None]
        b_last = b[..., -1]
        g = b_last[..., None] - b + it
        m_new = jnp.maximum(b_last + m, jnp.max(g, axis=-1))
        decay = jnp.exp(b_last + m - m_new)
        wk = jnp.exp(g - m_new[..., None])
        C_new = decay[..., None, None] * C + jnp.einsum('bhs,bhsd,bhse->bhde', wk, kt, vt)
        n_new = decay[..., None] * n + jnp.einsum('bhs,bhsd->bhd', wk, kt)
        return (C_new, n_new, m_new), ht

    init = (jnp.zeros((B, H, DK, DV), f32), jnp.zeros((B, H, DK), f32), jnp.zeros((B, H), f32))
    _, hs = lax.scan(step, init, (qc, kc, vc, ic, fc))
    hs = hs.transpose(1, 0, 3, 2, 4).reshape(B, S, H, DV)
    hs = hs * lax.rsqrt(jnp.mean(hs * hs, axis=-1, keepdims=True) + EPS)
    hs = hs.reshape(B, S, H * DV) * w_head_norm.astype(f32)
    hs = hs * jax.nn.sigmoid(o.astype(f32))
    return hs.astype(h.dtype) @ w_out

def shared_kv(x, kv_norm, kv_w, kv_b_f):
    B, S, _ = x.shape
    h = rmsnorm(x, kv_norm)
    proj = h @ kv_w
    k, v, f = jnp.split(proj, [D_MODEL, 2 * D_MODEL], axis=-1)
    k = k.reshape(B, S, FOX_HEADS, FOX_HEAD_DIM)
    v = v.reshape(B, S, FOX_HEADS, FOX_HEAD_DIM)
    log_f = jax.nn.log_sigmoid(f.astype(jnp.float32) + kv_b_f.astype(jnp.float32))
    c = jnp.cumsum(log_f, axis=1).transpose(0, 2, 1)
    return k, v, c

def fox_mixer(h, w_qg, w_out, k, v, c):
    B, S, _ = h.shape
    H, DH, BLK = FOX_HEADS, FOX_HEAD_DIM, FOX_BLOCK
    NQ = S // BLK
    proj = h @ w_qg
    q, g = jnp.split(proj, [D_MODEL], axis=-1)
    q = q.reshape(B, S, H, DH) * (DH ** -0.5)
    qb = q.reshape(B, NQ, BLK, H, DH).transpose(1, 0, 2, 3, 4)
    cb = c.reshape(B, H, NQ, BLK).transpose(2, 0, 1, 3)
    starts = jnp.arange(NQ) * BLK
    key_pos = jnp.arange(S)

    def block(args):
        qi, ci, st = args
        logits = jnp.einsum('bqhd,bkhd->bhqk', qi, k).astype(jnp.float32)
        logits = logits + (ci[..., :, None] - c[..., None, :])
        qpos = st + jnp.arange(BLK)
        mask = key_pos[None, :] <= qpos[:, None]
        logits = jnp.where(mask, logits, -jnp.inf)
        p = jax.nn.softmax(logits, axis=-1)
        return jnp.einsum('bhqk,bkhd->bqhd', p.astype(v.dtype), v)

    o = lax.map(block, (qb, cb, starts))
    o = o.transpose(1, 0, 2, 3, 4).reshape(B, S, D_MODEL)
    o = o * jax.nn.sigmoid(g)
    return o @ w_out

def conv_ffn(h, w_up, conv_w, conv_b, w_down):
    S = h.shape[1]
    u = h @ w_up
    up = jnp.pad(u, ((0, 0), (CONV_WIDTH - 1, 0), (0, 0)))
    y = conv_b
    for j in range(CONV_WIDTH):
        y = y + conv_w[j] * up[:, j:j + S]
    gate, val = jnp.split(y, 2, axis=-1)
    return (jax.nn.gelu(gate, approximate=True) * val) @ w_down

def first_inputs(seed: int = 0) -> dict:
    key = jax.random.key(seed)
    ks = jax.random.split(key, 24)
    D, H = D_MODEL, MLSTM_HEADS
    f32 = jnp.float32

    def nrm(k, shape, scale):
        return jax.random.normal(k, shape, f32) * scale

    def gain(k, shape):
        return 1.0 + 0.05 * jax.random.normal(k, shape, f32)

    x = jax.random.normal(ks[0], (BATCH, SEQ, D), f32)
    norm_mix_pre = gain(ks[1], (DEPTH, D))
    norm_mix_post = gain(ks[2], (DEPTH, D))
    norm_ffn_pre = gain(ks[3], (DEPTH, D))
    norm_ffn_post = gain(ks[4], (DEPTH, D))
    mlstm_w_in = nrm(ks[5], (N_A_LAYERS, D, MLSTM_IN), D ** -0.5)
    mlstm_b_gate = jnp.concatenate([
        nrm(ks[6], (N_A_LAYERS, H), 0.1),
        jax.random.uniform(ks[7], (N_A_LAYERS, H), f32, minval=3.0, maxval=6.0)], axis=-1)
    mlstm_norm = gain(ks[8], (N_A_LAYERS, H * MLSTM_V_DIM))
    mlstm_w_out = nrm(ks[9], (N_A_LAYERS, H * MLSTM_V_DIM, D), (H * MLSTM_V_DIM) ** -0.5)
    kv_norm = gain(ks[10], (D,))
    kv_w = nrm(ks[11], (D, 2 * D + FOX_HEADS), D ** -0.5)
    kv_b_f = jax.random.uniform(ks[12], (FOX_HEADS,), f32, minval=1.0, maxval=6.0)
    fox_w_qg = nrm(ks[13], (N_B_LAYERS, D, 2 * D), D ** -0.5)
    fox_w_out = nrm(ks[14], (N_B_LAYERS, D, D), D ** -0.5)
    ffn_w_up = nrm(ks[15], (DEPTH, D, 2 * D_FF), D ** -0.5)
    ffn_conv_w = nrm(ks[16], (DEPTH, CONV_WIDTH, 2 * D_FF), CONV_WIDTH ** -0.5)
    ffn_conv_b = nrm(ks[17], (DEPTH, 2 * D_FF), 0.02)
    ffn_w_down = nrm(ks[18], (DEPTH, D_FF, D), D_FF ** -0.5)
    return {'x': x, 'norm_mix_pre': norm_mix_pre, 'norm_mix_post': norm_mix_post,
            'norm_ffn_pre': norm_ffn_pre, 'norm_ffn_post': norm_ffn_post,
            'mlstm_w_in': mlstm_w_in, 'mlstm_b_gate': mlstm_b_gate, 'mlstm_norm': mlstm_norm,
            'mlstm_w_out': mlstm_w_out, 'kv_norm': kv_norm, 'kv_w': kv_w, 'kv_b_f': kv_b_f,
            'fox_w_qg': fox_w_qg, 'fox_w_out': fox_w_out, 'ffn_w_up': ffn_w_up,
            'ffn_conv_w': ffn_conv_w, 'ffn_conv_b': ffn_conv_b, 'ffn_w_down': ffn_w_down}

def first_block(x, norm_mix_pre, norm_mix_post, norm_ffn_pre, norm_ffn_post, mlstm_w_in, mlstm_b_gate,
              mlstm_norm, mlstm_w_out, kv_norm, kv_w, kv_b_f, fox_w_qg, fox_w_out, ffn_w_up,
              ffn_conv_w, ffn_conv_b, ffn_w_down):
    k_sh = v_sh = c_sh = None
    for layer in range(DEPTH):
        h = rmsnorm(x, norm_mix_pre[layer])
        if layer < N_A_LAYERS:
            y = mlstm_mixer(h, mlstm_w_in[layer], mlstm_b_gate[layer], mlstm_norm[layer], mlstm_w_out[layer])
        else:
            j = layer - N_A_LAYERS
            y = fox_mixer(h, fox_w_qg[j], fox_w_out[j], k_sh, v_sh, c_sh)
        x = x + rmsnorm(y, norm_mix_post[layer])
        h = rmsnorm(x, norm_ffn_pre[layer])
        y = conv_ffn(h, ffn_w_up[layer], ffn_conv_w[layer], ffn_conv_b[layer], ffn_w_down[layer])
        x = x + rmsnorm(y, norm_ffn_post[layer])
        if layer == N_A_LAYERS - 1:
            k_sh, v_sh, c_sh = shared_kv(x, kv_norm, kv_w, kv_b_f)
    return x


GRID_W = 64
CTX_LEN = 256
CHUNK = 128
A_GROUPS = 4
A_W = D_MODEL // 2
A_GROUP_DIM = A_W // A_GROUPS
B_HEAD_DIM = 64
B_W = D_MODEL // 2
B_HEADS = B_W // B_HEAD_DIM
WIN_H = 8
WIN_W = 16
MIX_IN = 2 * A_W + 3 * B_W
MIX_OUT = A_W + B_W
CONV_K = 31
CONV_W = D_MODEL
FFN = 4 * D_MODEL
N_EVEN = (DEPTH + 1) // 2
N_ODD = DEPTH // 2
NEG = -1e30


def rmsnorm_2(x, g):
    x32 = x.astype(jnp.float32)
    y = x32 * lax.rsqrt(jnp.mean(x32 * x32, axis=-1, keepdims=True) + EPS)
    return (y * g.astype(jnp.float32)).astype(x.dtype)

def layernorm(x, g, b=None):
    x32 = x.astype(jnp.float32)
    mu = jnp.mean(x32, axis=-1, keepdims=True)
    var = jnp.mean(jnp.square(x32 - mu), axis=-1, keepdims=True)
    y = (x32 - mu) * lax.rsqrt(var + EPS) * g.astype(jnp.float32)
    if b is not None:
        y = y + b.astype(jnp.float32)
    return y.astype(x.dtype)

def modulate(h, shift, scale):
    return h * (1 + scale) + shift

def split_heads(t):
    return t.reshape(*t.shape[:-1], B_HEADS, B_HEAD_DIM)

def spatial_gating(z, ln_v_g, w_sp, b_sp):
    u, g = jnp.split(jax.nn.gelu(z), 2, axis=-1)
    bsz, length, _ = g.shape
    g = g.reshape(bsz, length // CHUNK, CHUNK, A_GROUPS, A_GROUP_DIM)
    g = layernorm(g, ln_v_g.reshape(A_GROUPS, A_GROUP_DIM))
    s = jnp.einsum('gpq,bnqgc->bnpgc', w_sp, g) + b_sp.T[:, :, None]
    return u * s.reshape(bsz, length, A_W)

def neighborhood_attention(q, k, v, k_ctx, v_ctx, rpb):
    bsz, seq, nh, dh = q.shape
    rows_n = seq // GRID_W
    kh = min(WIN_H, rows_n)
    kw = WIN_W
    qg = q.reshape(bsz, rows_n, GRID_W, nh, dh)
    kg = k.reshape(bsz, rows_n, GRID_W, nh, dh)
    vg = v.reshape(bsz, rows_n, GRID_W, nh, dh)
    rows = jnp.arange(rows_n)
    row_idx = jnp.clip(rows - kh // 2, 0, rows_n - kh)[:, None] + jnp.arange(kh)
    k_band = kg[:, row_idx]
    v_band = vg[:, row_idx]
    cols = jnp.arange(GRID_W)
    col_start = jnp.clip(cols - kw // 2, 0, GRID_W - kw)
    col_mask = (cols[None, :] >= col_start[:, None]) & (cols[None, :] < col_start[:, None] + kw)
    dr = row_idx - rows[:, None] + WIN_H - 1
    dc = jnp.clip(cols[None, :] - cols[:, None] + WIN_W - 1, 0, 2 * WIN_W - 2)
    bias = rpb[:, dr[:, None, :, None], dc[None, :, None, :]].astype(jnp.float32)
    scale = dh ** -0.5
    s_loc = jnp.einsum('brqhd,brkwhd->bhrqkw', qg, k_band).astype(jnp.float32) * scale + bias[None]
    s_loc = jnp.where(col_mask[:, None, :], s_loc, NEG)
    s_ctx = jnp.einsum('brqhd,bchd->bhrqc', qg, k_ctx).astype(jnp.float32) * scale
    n_loc = kh * GRID_W
    s = jnp.concatenate([s_loc.reshape(bsz, nh, rows_n, GRID_W, n_loc), s_ctx], axis=-1)
    p = jax.nn.softmax(s, axis=-1).astype(v.dtype)
    p_loc = p[..., :n_loc].reshape(bsz, nh, rows_n, GRID_W, kh, GRID_W)
    p_ctx = p[..., n_loc:]
    out = (jnp.einsum('bhrqkw,brkwhd->brqhd', p_loc, v_band)
           + jnp.einsum('bhrqc,bchd->brqhd', p_ctx, v_ctx))
    return out.reshape(bsz, seq, nh * dh)

def context_attention(q, k, v):
    s = jnp.einsum('bqhd,bkhd->bhqk', q, k).astype(jnp.float32) * (q.shape[-1] ** -0.5)
    p = jax.nn.softmax(s, axis=-1).astype(v.dtype)
    out = jnp.einsum('bhqk,bkhd->bqhd', p, v)
    return out.reshape(*out.shape[:2], -1)

def even_mixer(h, hc, w_in, w_out, ln_v_g, w_sp, b_sp, rpb, ctx_out):
    cuts = [2 * A_W, 2 * A_W + B_W, 2 * A_W + 2 * B_W]
    if ctx_out:
        zc, qc, kc, vc = jnp.split(hc @ w_in, cuts, axis=-1)
    else:
        kc, vc = jnp.split(hc @ w_in[:, cuts[1]:], 2, axis=-1)
    kc, vc = split_heads(kc), split_heads(vc)
    z, q, k, v = jnp.split(h @ w_in, cuts, axis=-1)
    a = spatial_gating(z, ln_v_g, w_sp, b_sp)
    b = neighborhood_attention(split_heads(q), split_heads(k), split_heads(v), kc, vc, rpb)
    y = jnp.concatenate([a, b], axis=-1) @ w_out
    yc = None
    if ctx_out:
        ac = spatial_gating(zc, ln_v_g, w_sp, b_sp)
        bc = context_attention(split_heads(qc), kc, vc)
        yc = jnp.concatenate([ac, bc], axis=-1) @ w_out
    return y, yc

def conformer_conv(h, w_pw1, b_pw1, w_dw, b_dw, ln_g, ln_b, w_pw2, b_pw2):
    a, gate = jnp.split(h @ w_pw1 + b_pw1, 2, axis=-1)
    y = a * jax.nn.sigmoid(gate)
    y = lax.conv_general_dilated(y, w_dw[:, None, :], window_strides=(1,),
                                 padding=[(CONV_K // 2, CONV_K // 2)],
                                 dimension_numbers=('NWC', 'WIO', 'NWC'),
                                 feature_group_count=CONV_W) + b_dw
    y = jax.nn.silu(layernorm(y, ln_g, ln_b))
    return y @ w_pw2 + b_pw2

def sq_relu_mlp(h, w1, w2):
    return jnp.square(jax.nn.relu(h @ w1)) @ w2

def second_inputs(seed: int = 0) -> dict:
    key = jax.random.key(seed)
    ks = jax.random.split(key, 24)
    f32 = jnp.float32
    nrm = lambda k, shape, s: jax.random.normal(k, shape, f32) * s
    D = D_MODEL
    return {
        "x": nrm(ks[0], (BATCH, SEQ, D), 1.0),
        "c": nrm(ks[1], (BATCH, D), 1.0),
        "ctx": nrm(ks[2], (BATCH, CTX_LEN, D), 1.0),
        "c_ctx": nrm(ks[3], (D,), 1.0),
        "w_mod": nrm(ks[4], (DEPTH, D, 6 * D), 0.5 * D ** -0.5),
        "b_mod": nrm(ks[5], (DEPTH, 6 * D), 0.02),
        "norm_g": 1.0 + nrm(ks[6], (DEPTH, 2, D), 0.05),
        "w_in": nrm(ks[7], (N_EVEN, D, MIX_IN), D ** -0.5),
        "w_out": nrm(ks[8], (N_EVEN, MIX_OUT, D), MIX_OUT ** -0.5),
        "ln_v_g": 1.0 + nrm(ks[9], (N_EVEN, A_W), 0.05),
        "w_sp": nrm(ks[10], (N_EVEN, A_GROUPS, CHUNK, CHUNK), CHUNK ** -0.5),
        "b_sp": 1.0 + nrm(ks[11], (N_EVEN, A_GROUPS, CHUNK), 0.1),
        "rpb": nrm(ks[12], (N_EVEN, B_HEADS, 2 * WIN_H - 1, 2 * WIN_W - 1), 0.1),
        "w_pw1": nrm(ks[13], (N_ODD, D, 2 * CONV_W), D ** -0.5),
        "b_pw1": nrm(ks[14], (N_ODD, 2 * CONV_W), 0.02),
        "w_dw": nrm(ks[15], (N_ODD, CONV_K, CONV_W), CONV_K ** -0.5),
        "b_dw": nrm(ks[16], (N_ODD, CONV_W), 0.02),
        "ln_c_g": 1.0 + nrm(ks[17], (N_ODD, CONV_W), 0.05),
        "ln_c_b": nrm(ks[18], (N_ODD, CONV_W), 0.02),
        "w_pw2": nrm(ks[19], (N_ODD, CONV_W, D), CONV_W ** -0.5),
        "b_pw2": nrm(ks[20], (N_ODD, D), 0.02),
        "w_ff1": nrm(ks[21], (DEPTH, D, FFN), D ** -0.5),
        "w_ff2": nrm(ks[22], (DEPTH, FFN, D), FFN ** -0.5),
        "final_g": 1.0 + nrm(ks[23], (D,), 0.05),
    }

def second_block(x, c, ctx, c_ctx, w_mod, b_mod, norm_g, w_in, w_out, ln_v_g, w_sp, b_sp, rpb,
              w_pw1, b_pw1, w_dw, b_dw, ln_c_g, ln_c_b, w_pw2, b_pw2, w_ff1, w_ff2, final_g):
    last_reader = ((DEPTH - 1) // 2) * 2
    sc_c = jax.nn.silu(c)
    sc_ctx = jax.nn.silu(c_ctx)
    for l in range(DEPTH):
        m = (sc_c @ w_mod[l] + b_mod[l])[:, None, :]
        sh1, s1, g1, sh2, s2, g2 = jnp.split(m, 6, axis=-1)
        mc = sc_ctx @ w_mod[l] + b_mod[l]
        csh1, cs1, cg1, csh2, cs2, cg2 = jnp.split(mc, 6, axis=-1)
        ctx_out = l < last_reader
        h = modulate(rmsnorm_2(x, norm_g[l, 0]), sh1, s1)
        if l % 2 == 0:
            i = l // 2
            hc = modulate(rmsnorm_2(ctx, norm_g[l, 0]), csh1, cs1)
            y, yc = even_mixer(h, hc, w_in[i], w_out[i], ln_v_g[i], w_sp[i], b_sp[i], rpb[i], ctx_out)
        else:
            i = l // 2
            conv = lambda t: conformer_conv(t, w_pw1[i], b_pw1[i], w_dw[i], b_dw[i],
                                            ln_c_g[i], ln_c_b[i], w_pw2[i], b_pw2[i])
            y = conv(h)
            yc = conv(modulate(rmsnorm_2(ctx, norm_g[l, 0]), csh1, cs1)) if ctx_out else None
        x = x + g1 * y
        x = x + g2 * sq_relu_mlp(modulate(rmsnorm_2(x, norm_g[l, 1]), sh2, s2), w_ff1[l], w_ff2[l])
        if ctx_out:
            ctx = ctx + cg1 * yc
            ctx = ctx + cg2 * sq_relu_mlp(modulate(rmsnorm_2(ctx, norm_g[l, 1]), csh2, cs2), w_ff1[l], w_ff2[l])
    return rmsnorm_2(x, final_g)


def setup_inputs(seed=0):
    out = dict(first_inputs(seed))
    for name, value in second_inputs(seed + 1).items():
        if name != "x":
            out[name + "_2"] = value
    return out


def reference(
    x, norm_mix_pre, norm_mix_post, norm_ffn_pre, norm_ffn_post, mlstm_w_in, mlstm_b_gate,
    mlstm_norm, mlstm_w_out, kv_norm, kv_w, kv_b_f, fox_w_qg, fox_w_out, ffn_w_up, ffn_conv_w,
    ffn_conv_b, ffn_w_down, c_2, ctx_2, c_ctx_2, w_mod_2, b_mod_2, norm_g_2, w_in_2, w_out_2,
    ln_v_g_2, w_sp_2, b_sp_2, rpb_2, w_pw1_2, b_pw1_2, w_dw_2, b_dw_2, ln_c_g_2, ln_c_b_2,
    w_pw2_2, b_pw2_2, w_ff1_2, w_ff2_2, final_g_2,
):
    x = first_block(
        x, norm_mix_pre, norm_mix_post, norm_ffn_pre, norm_ffn_post, mlstm_w_in, mlstm_b_gate,
        mlstm_norm, mlstm_w_out, kv_norm, kv_w, kv_b_f, fox_w_qg, fox_w_out, ffn_w_up,
        ffn_conv_w, ffn_conv_b, ffn_w_down,
    )
    return second_block(
        x, c_2, ctx_2, c_ctx_2, w_mod_2, b_mod_2, norm_g_2, w_in_2, w_out_2, ln_v_g_2, w_sp_2,
        b_sp_2, rpb_2, w_pw1_2, b_pw1_2, w_dw_2, b_dw_2, ln_c_g_2, ln_c_b_2, w_pw2_2, b_pw2_2,
        w_ff1_2, w_ff2_2, final_g_2,
    )


_drawn_inputs = setup_inputs


def setup_inputs(seed=0):
    import zlib

    import numpy as np

    out = dict(_drawn_inputs(seed))
    spreads = {}
    factors = {'ctx_2': 7.063,
     'c_ctx_2': 3.069,
     'norm_g_2': 3.366,
     'ln_v_g_2': 8.0,
     'b_sp_2': 7.914,
     'rpb_2': 64.0,
     'b_pw1_2': 35.934,
     'b_dw_2': 26.412,
     'ln_c_g_2': 41.724,
     'ln_c_b_2': 64.0,
     'b_pw2_2': 64.0}
    for name, (base, spread) in spreads.items():
        noise = np.random.default_rng([zlib.crc32(name.encode()), seed]).standard_normal(out[name].shape)
        drawn = base * np.exp(spread * noise) if base else spread * noise
        out[name] = __import__('jax').numpy.asarray(drawn.astype(out[name].dtype))
    for name, factor in factors.items():
        out[name] = (out[name] * factor).astype(out[name].dtype)
    return out
```

```python
from contextlib import ExitStack

import concourse.bass as bass
from concourse import mybir

ALU = mybir.AluOpType
ACT = mybir.ActivationFunctionType
AX = mybir.AxisListType
F32 = mybir.dt.float32
F32R = mybir.dt.float32r

P = 128
T = 512
TB = T // P
D = 1024
DT = D // P
CTX = 256
EPS = 1e-6
NEG = -1e30
FF1 = 2816
FF1_T = FF1 // P
FF2 = 4096
SLOTS = 4
KC = 4
GC = 256
CONV_K = 31
PAD = CONV_K // 2


def ds(a, n):
    return bass.ds(a, n)


VECTORS = [
    ("norm_mix_pre", 16), ("norm_mix_post", 16), ("norm_ffn_pre", 16), ("norm_ffn_post", 16),
    ("mlstm_norm", 8), ("kv_norm", 8), ("ffn_conv_w", 264), ("ffn_conv_b", 88), ("norm_g_2", 32),
    ("ln_v_g_2", 4), ("b_pw1_2", 16), ("w_dw_2", 248), ("b_dw_2", 8), ("ln_c_g_2", 8), ("ln_c_b_2", 8),
    ("b_pw2_2", 8), ("final_g_2", 8), ("b_mod_2", 96), ("c_2", 8), ("c_ctx_2", 8), ("b_sp_2", 4),
]
ROW = {}
_n = 0
for _name, _rows in VECTORS:
    ROW[_name] = _n
    _n += _rows
VROWS = _n
VBLOCKS = -(-VROWS // P)


def vector_dmas():
    found = []
    for name, count in VECTORS:
        n = 0
        while n < count:
            r = ROW[name] + n
            m = min(count - n, P - r % P)
            found.append((name, n, r, m))
            n += m
    return found


VECTOR_DMAS = len(vector_dmas())


def linear_plan():
    stages = [("m_q", 2, 8), ("m_k", 2, 8), ("m_v", 4, 8), ("m_o", 4, 8), ("m_out", 4, 8)]

    def ffn1(layer):
        for part, n in enumerate((8, 8, 6)):
            stages.append((f"f{layer}_up{part}", n, 8))
            stages.append((f"f{layer}_down{part}", 4, n))

    def ffn2(layer):
        for part in range(4):
            stages.append((f"s{layer}_up{part}", 4, 8))
            stages.append((f"s{layer}_down{part}", 4, 8))

    ffn1(0)
    stages.extend([("kv_k", 4, 8), ("kv_v", 4, 8), ("x_q", 4, 8), ("x_g", 4, 8), ("x_out", 4, 8)])
    ffn1(1)
    stages.extend([("c_k", 2, 8), ("c_v", 2, 8), ("n_u", 2, 8), ("n_g", 2, 8), ("n_q", 2, 8), ("n_k", 2, 8),
                   ("n_v", 2, 8), ("n_out", 4, 8)])
    ffn2(0)
    stages.extend([("p_1", 8, 8), ("p_2", 4, 8)])
    ffn2(1)
    plan, c, g = {}, 0, 0
    for name, n, k in stages:
        plan[name] = dict(name=name, groups=n, ktiles=k, chunk=c, group=g)
        c += 2 * n
        g += n
    return plan, c


FILLS = ["pre0", "mlstm", "ffn0", "kv", "pre1", "fox", "ffn1", "ctx", "even", "mix", "mlp0", "odd", "conf", "mlp1"]
FILL = {name: 8 * i for i, name in enumerate(FILLS)}
NORMS = ["pre0", "post0", "ffn0", "fpost0", "kv", "pre1", "post1", "ffn1", "fpost1", "ctx", "even", "mlp0",
         "odd", "conf", "mlp1", "final"]
NORM = {name: i for i, name in enumerate(NORMS)}
RESIDS = {"post0": 8, "fpost0": 16, "post1": 24, "fpost1": 32}
READY = {name: 8 * i for i, name in enumerate(f for f in FILLS if f not in ("fox", "mix", "conf"))}
HIDDEN = {"f0": 0, "f1": 22, "s0": 44, "s1": 60}


def build(nc, a, out, consts):
    plan, chunks = linear_plan()
    with ExitStack() as ctx:
        arena = ctx.enter_context(nc.sbuf_tensor("arena", [P, 212736 // 4], F32))
        origin = 16512

        def at(name, offset, shape, dt=F32):
            return nc.alloc_sbuf_tensor_at(name, shape, dt, offset=origin + offset)

        def sem(name):
            return ctx.enter_context(nc.semaphore(name))

        K = 1024
        X = at("X", 0, [P, DT, T])
        Y = at("Y", 16 * K, [P, DT, T])
        H_hi = at("H_hi", 32 * K, [P, DT, T], F32R)
        H_lo = at("H_lo", 48 * K, [P, DT, T], F32R)
        raw = at("raw", 64 * K, [P, SLOTS, KC * GC])
        w_hi = at("w_hi", 80 * K, [P, SLOTS, KC * GC], F32R)
        w_lo = at("w_lo", 96 * K, [P, SLOTS, KC * GC], F32R)
        hid_hi = at("hid_hi", 112 * K, [P, DT, T], F32R)
        hid_lo = at("hid_lo", 128 * K, [P, DT, T], F32R)
        mod_acc = at("mod_acc", 144 * K, [P, 6 * D])
        ctx_acc = at("ctx_acc", 168 * K, [P, 2 * D])
        mod_w = at("mod_w", 176 * K, [P, 2, 4, 256])
        VT = at("VT", 184 * K, [P, VBLOCKS * P])
        S = at("S", 188 * K, [P, 4, T])
        SQ = at("SQ", 196 * K, [P, 2, T])
        Dg = at("Dg", 200 * K, [P, TB, P])
        o = [202 * K]

        def small(name, shape, dt=F32):
            n = 4
            for s in shape[1:]:
                n *= s
            t = at(name, o[0], shape, dt)
            o[0] += -(-n // 32) * 32
            return t

        ident = small("ident", [P, P])
        mask_ts = small("mask_ts", [P, P])
        mask_st = small("mask_st", [P, P])
        ones = small("ones", [P, P])
        eps = small("eps", [P, 1])
        sd = small("sd", [P, TB])
        rs = small("rs", [P, TB])
        gates_T = small("gates_T", [P, 3, TB, 8])
        c_T = small("c_T", [P, TB, 16])
        stat = small("stat", [P, 8, 8])
        n1 = small("n1", [P, 8, 4])
        n2 = small("n2", [P, 8, 4])
        n3 = small("n3", [P, 8, 4])
        mx = small("mx", [P, 2, 4])
        rsum = small("rsum", [P, 2, 4])
        cs = small("cs", [P, 16])
        mod = small("mod", [P, 48])
        cmod = small("cmod", [P, 16])
        gain1 = small("gain1", [P, 8])
        gain2 = small("gain2", [P, 8])
        cgain = small("cgain", [P, 8])
        gb = small("gb", [P, 8])
        bn = small("bn", [P, 16, 2])
        b_m = small("b_m", [8, 2])
        b_x = small("b_x", [16, 1])
        tok = small("tok", [P, 48])
        mod_t = small("mod_t", [P, 256])
        assert o[0] <= 212736, o[0]

        x_tm = at("x_tm", 16 * K, [P, TB, D])
        v_rows = at("v_rows", 112 * K, [P, VBLOCKS, P])
        gw_raw = at("gw_raw", 16 * K, [P, DT, P])
        gw_hi = at("gw_hi", 20 * K, [P, DT, P], F32R)
        gw_lo = at("gw_lo", 24 * K, [P, DT, P], F32R)
        mQ = at("mQ", 112 * K, [P, 4, T])
        mK = at("mK", 120 * K, [P, 4, T])
        mV = at("mV", 128 * K, [P, TB, D])
        xK = at("xK", 112 * K, [P, DT, T])
        xV = at("xV", 128 * K, [P, TB, D])
        xQ = at("xQ", 144 * K, [P, DT, T])
        att = at("att", 32 * K, [P, 8192])
        Kp = att[:, 0:768]
        Qp = att[:, 768:1280]
        Vp = att[:, 1280:2304]
        N0 = att[:, 2304:2816]
        N1 = att[:, 2816:3328]
        Lg = att[:, 3328:4864].rearrange("p (b n) -> p b n", b=2)
        PT = att[:, 4864:7936].rearrange("p (s n) -> p s n", s=6)
        rows = att[:, 0:8192].rearrange("p (j n) -> p j n", n=T)

        ctx_tm = at("ctx_tm", 16 * K, [P, 2, D])
        ct = at("ct", 24 * K, [P, DT, CTX])
        g_tm = at("g_tm", 24 * K, [P, TB, 512])
        nK = at("nK", 112 * K, [P, 4, T])
        nV = at("nV", 120 * K, [P, TB, 512])
        cK = at("cK", 128 * K, [P, 4, CTX])
        cV = at("cV", 132 * K, [P, 2, 512])
        nQ = at("nQ", 136 * K, [P, 4, T])
        tbias = at("tbias", 144 * K, [P, 8, 14, 64])
        sel = at("sel", 32 * K, [64, 2, 16 * P])
        rp = at("rp", 48 * K, [120, 64])
        rm = at("rm", 49 * K, [64, 8, 14])
        yp = at("yp", 112 * K, [P, DT, T + 2 * PAD])

        G = ctx.enter_context(nc.psum_tensor("G", [P, 4, 512], F32))
        M = ctx.enter_context(nc.psum_tensor("M", [P, 4, 512], F32))

        raw_landed = [sem(f"raw_landed{i}") for i in range(SLOTS)]
        hi_done = sem("hi_done")
        lo_done = sem("lo_done")
        chunk_used = sem("chunk_used")
        freed_a = sem("freed_a")
        freed_d = sem("freed_d")
        h_ready = sem("h_ready")
        h_hi = sem("h_hi")
        h_lo = sem("h_lo")
        n_sq = sem("n_sq")
        n_ss = sem("n_ss")
        n_sd = sem("n_sd")
        n_rc = sem("n_rc")
        n_dg = sem("n_dg")
        n_bc = sem("n_bc")
        r_t = sem("r_t")
        x_ready = sem("x_ready")
        x_dma = sem("x_dma")
        v_dma = sem("v_dma")
        c_dma = sem("c_dma")
        cs_ready = sem("cs_ready")
        pool_c = sem("pool_c")
        mod_landed = [sem(f"mod_landed{i}") for i in range(2)]
        mod_done = sem("mod_done")
        mod_s = sem("mod_s")
        mod_ok = sem("mod_ok")
        aux_free = sem("aux_free")
        chain_d = sem("chain_d")
        sel_dma = [sem(f"sel_dma{i}") for i in range(2)]
        setup_p = sem("setup_p")
        setup_t = sem("setup_t")
        setup_c = sem("setup_c")
        g_dma = sem("g_dma")
        g_zero = sem("g_zero")
        g_hi = sem("g_hi")
        g_lo = sem("g_lo")
        g_mm = sem("g_mm")
        f_a = sem("f_a")
        f_d = sem("f_d")
        f_g = sem("f_g")
        f_m = sem("f_m")
        hid_h = sem("hid_h")
        hid_l = sem("hid_l")
        row_a = sem("row_a")
        row_d = sem("row_d")
        row_t = sem("row_t")
        row_c = sem("row_c")
        ml = {k: sem(f"ml_{k}") for k in ("stg", "dg", "bc", "n0", "n1", "s", "e", "p", "num", "sq", "ss", "st",
                                          "y", "nar")}
        fx = {k: sem(f"fx_{k}") for k in ("stg", "dg", "bc", "n0", "s", "m", "e", "p", "t", "pt", "o", "y")}
        na = {k: sem(f"na_{k}") for k in ("stg", "s", "m", "e", "p", "t", "pt", "o", "y")}
        (rp_dma, tb_t, tb_r, tb_b, tb_mm, tb_e, ctx_dma, ct_t, ct_c, wsp_dma, sg_t, sg_w, sg_dg, sg_bc, sg_b, sg_v,
         sg_r, sg_n, sg_m, glu_a, cv_d, cv_s, cv_r, cv_dg, cv_bc, cv_m, cv_t, cv_y, fin_t, fin_m, fin_c) = [
            sem(k) for k in ("rp_dma tb_t tb_r tb_b tb_mm tb_e ctx_dma ct_t ct_c wsp_dma sg_t sg_w sg_dg sg_bc sg_b "
                             "sg_v sg_r sg_n sg_m glu_a cv_d cv_s cv_r cv_dg cv_bc cv_m cv_t cv_y fin_t fin_m "
                             "fin_c").split()]
        TOKENS = [(freed_a, 2), (freed_d, 2), (hid_l, 1), (tb_mm, 2), (tb_e, 4), (ml["p"], 4), (fx["t"], 2),
                  (fx["pt"], 2), (na["e"], 2), (na["t"], 2)]
        TOKENS += [(ml[k], 1) for k in ("n0", "n1", "bc", "y", "sq", "st", "ss", "num", "e")]
        TOKENS += [(fx[k], 1) for k in ("n0", "bc", "y", "o")]
        TOKENS += [(na[k], 1) for k in ("pt", "y", "o")]
        done = sem("done")

        block = ctx.enter_context(nc.Block())
        vt = lambda name, t: VT[:, ROW[name] + t:ROW[name] + t + 1]

        by = {}
        read_a = read_d = 0
        for name, st in plan.items():
            kind = "A"
            if "down" in name and (name[0] == "s" or not name.endswith("down0")):
                kind = "D"
            if name[0] == "f" and "up" in name or name in ("n_out", "p_1", "p_2"):
                kind = "D"
            st["by"] = kind
            st["freed"] = read_a if kind == "A" else read_d
            if kind == "A":
                read_a += st["groups"]
            else:
                read_d += st["groups"]
            st["totals"] = (read_a, read_d)
        order = list(plan)
        for prev, name in zip([None] + order, order):
            plan[name]["before"] = plan[prev]["totals"] if prev else (0, 0)
        used_after = lambda name: 4 + 2 * (plan[name]["group"] + plan[name]["groups"])

        ident4 = ident[:].unsqueeze(1).to_broadcast([P, TB, P])

        def h_ready_wait(eng, name, t):
            eng.wait_ge(h_ready, READY[name] + t + 1)

        def fill_act(act, name, ready, shift, after, n=T):
            if after:
                act.wait_ge(chunk_used, after)
            for t in range(DT):
                h_ready_wait(act, name, t)
                if shift:
                    ins = act.activation(H_hi[:, t, 0:n], S[:, t % 4, 0:n], ACT.Identity, bias=shift(t))
                else:
                    ins = act.activation(H_hi[:, t, 0:n], S[:, t % 4, 0:n], ACT.Copy)
                ins.then_inc(h_hi, 1)

        def fill_dve(dve, name, produce, shift, after, n=T):
            def low(t):
                dve.wait_ge(h_hi, FILL[name] + t + 1)
                if shift:
                    ins = dve.scalar_tensor_tensor(H_lo[:, t, 0:n], S[:, t % 4, 0:n], shift(t), H_hi[:, t, 0:n],
                                                   ALU.add, ALU.subtract)
                else:
                    ins = dve.tensor_tensor(H_lo[:, t, 0:n], S[:, t % 4, 0:n], H_hi[:, t, 0:n], ALU.subtract)
                ins.then_inc(h_lo, 1)

            if after:
                dve.wait_ge(chunk_used, after)
            for t in range(DT):
                if FILL[name] + t - 3 > 0:
                    dve.wait_ge(h_lo, FILL[name] + t - 3)
                produce(t, S[:, t % 4, 0:n]).then_inc(h_ready, 1)
                if t:
                    low(t - 1)
            low(7)

        def split_act(act, name, ready, src):
            for t in range(DT):
                ready(t)
                act.activation(H_hi[:, t, :], src[:, t, :], ACT.Copy).then_inc(h_hi, 1)

        def split_dve(dve, name, src):
            for t in range(DT):
                dve.wait_ge(h_hi, FILL[name] + t + 1)
                dve.tensor_tensor(H_lo[:, t, :], src[:, t, :], H_hi[:, t, :], ALU.subtract).then_inc(h_lo, 1)

        def norm_act(act, name, src, ready, blocks=TB):
            i, n = NORM[name], blocks * P
            for t in range(DT):
                ready(t)
                if 8 * i + t - 1 > 0:
                    act.wait_ge(n_ss, 8 * i + t - 1)
                act.activation(SQ[:, t % 2, 0:n], src[:, t, 0:n], ACT.Square).then_inc(n_sq, 1)
            act.wait_ge(n_ss, 8 * i + 8)
            if i:
                act.wait_ge(n_dg, i)
            act.activation(sd[:, 0:blocks], M[:, 0, 0:blocks], ACT.Sqrt, bias=eps[:, 0:1],
                           scale=1.0 / D).then_inc(n_sd, 1)

        def norm_dve(dve, name, blocks=TB):
            i = NORM[name]
            dve.wait_ge(n_sd, i + 1)
            if i:
                dve.wait_ge(n_bc, i)
            dve.reciprocal(rs[:, 0:blocks], sd[:, 0:blocks]).then_inc(n_rc, 1)
            dve.wait_ge(n_rc, i + 1)
            dve.tensor_tensor(Dg[:, 0:blocks, :], ident[:].unsqueeze(1).to_broadcast([P, blocks, P]),
                              rs[:, 0:blocks].unsqueeze(2).to_broadcast([P, blocks, P]), ALU.mult).then_inc(n_dg, 1)
            dve.wait_ge(n_bc, i + 1)
            return M[:, 1, 0:blocks * P]

        def pre_dve(dve, name, src, gain, shift, after, blocks=TB):
            row = norm_dve(dve, name, blocks)
            n = blocks * P
            fill_dve(dve, name, lambda t, dst: dve.scalar_tensor_tensor(dst, src[:, t, 0:n], gain(t), row, ALU.mult,
                                                                        ALU.mult), shift, after, n)

        def residual_dve(dve, name, gain):
            row = norm_dve(dve, name)
            b = RESIDS[name]
            def add(t):
                dve.wait_ge(r_t, b - 8 + t + 1)
                dve.tensor_tensor(X[:, t, :], X[:, t, :], S[:, t % 4, :], ALU.add).then_inc(x_ready, 1)

            for t in range(DT):
                if t >= 4:
                    dve.wait_ge(x_ready, b + t - 3)
                dve.scalar_tensor_tensor(S[:, t % 4, :], Y[:, t, :], gain(t), row, ALU.mult, ALU.mult).then_inc(r_t, 1)
                if t:
                    add(t - 1)
            add(7)

        def split_hi(act, chunk, i, j):
            act.wait_ge(raw_landed[j], i * 32 + 32 * (chunk // 4 + 1))
            act.wait_ge(chunk_used, i * 4 + (chunk + j + 1))
            act.activation(w_hi[:, j, :], raw[:, j, :], ACT.Copy).then_inc(hi_done, 1)

        def split_lo(dve, chunk, i, j):
            dve.wait_ge(hi_done, i * 4 + (chunk + j + 1))
            dve.tensor_tensor(w_lo[:, j, :], raw[:, j, :], w_hi[:, j, :], ALU.subtract).then_inc(lo_done, 1)

        def groups(eng, name, split, evacuate):
            st = plan[name]

            def body(i, more):
                for p in range(2):
                    if more:
                        split(eng, st["chunk"] + 4, i, 2 * p)
                        split(eng, st["chunk"] + 4, i, 2 * p + 1)
                    if evacuate:
                        eng.wait_ge(chunk_used, i * 4 + (2 * st["group"] + 2 * p + 6))
                        evacuate(i, p, i * 2 + p)

            n = st["groups"] // 2
            if name == order[-1]:
                for i in range(n):
                    body(i, i < n - 1)
            else:
                with eng.Fori(0, n) as i:
                    body(i, True)

        def two(tile, g):
            return tile[:, ds(g * 2, 2), :]

        def gate_weights_act(act, n):
            act.wait_ge(g_dma, 32 if n == 0 else 48)
            act.activation(gw_hi[:], gw_raw[:], ACT.Copy).then_inc(g_hi, 1)

        def gate_weights_dve(dve, n):
            dve.wait_ge(g_hi, n + 1)
            dve.tensor_tensor(gw_lo[:], gw_raw[:], gw_hi[:], ALU.subtract).then_inc(g_lo, 1)

        def ffn1_act(act, layer):
            base = HIDDEN[f"f{layer}"]
            cw = ROW["ffn_conv_w"] + 132 * layer
            cb = ROW["ffn_conv_b"] + 44 * layer
            for part in range(3):
                def up(i, p, g):
                    u = g + (base + 8 * part)
                    act.wait_ge(hid_l, g + (base + 8 * part) + 1)
                    for h in range(2):
                        t = g + (8 * part + 22 * h)
                        act.activation(S[:, h, :], G[:, 2 * p + h, :], ACT.Identity, bias=VT[:, ds(t + cb, 1)],
                                       scale=VT[:, ds(t + (cw + 88), 1)]).then_inc(f_a, 1)
                    act.wait_ge(f_d, u * 3 + 2)
                    act.activation(S[:, 2, :], S[:, 0, :], ACT.Gelu_apprx_tanh).then_inc(f_g, 1)
                    act.wait_ge(f_m, u + 1)
                    act.activation(hid_hi[:, ds(g, 1), :], S[:, 3:4, :], ACT.Copy).then_inc(hid_h, 1)

                groups(act, f"f{layer}_up{part}", split_hi, up)

                def down(i, p, g):
                    act.activation(two(Y, g), G[:, 2 * p:2 * p + 2, :], ACT.Copy).then_inc(freed_a, 1)

                groups(act, f"f{layer}_down{part}", split_hi, down if part == 0 else None)

        def ffn1_dve(dve, layer):
            base = HIDDEN[f"f{layer}"]
            cw = ROW["ffn_conv_w"] + 132 * layer
            for part in range(3):
                freed = plan[f"f{layer}_up{part}"]["freed"]

                def up(i, p, g):
                    u = g + (base + 8 * part)

                    def tap(h, j):
                        w = VT[:, ds(g + (8 * part + 22 * h + cw + 44 * j), 1)]
                        k = 2 - j
                        return dve.scalar_tensor_tensor(S[:, h, k:T], G[:, 2 * p + h, 0:T - k], w, S[:, h, k:T],
                                                        ALU.mult, ALU.add)

                    dve.wait_ge(f_a, u * 2 + 1)
                    tap(0, 1).then_inc(f_d, 1)
                    dve.wait_ge(f_d, u * 3 + 1)
                    tap(0, 0).then_inc(f_d, 1)
                    dve.wait_ge(f_a, u * 2 + 2)
                    tap(1, 1).then_inc(f_d, 1)
                    dve.wait_ge(f_d, u * 3 + 3)
                    tap(1, 0).then_inc(freed_d, 1)
                    dve.wait_ge(freed_d, g + (2 + freed + 1))
                    dve.wait_ge(f_g, u + 1)
                    dve.tensor_tensor(S[:, 3, :], S[:, 1, :], S[:, 2, :], ALU.mult).then_inc(f_m, 1)
                    dve.wait_ge(hid_h, u + 1)
                    dve.tensor_tensor(hid_lo[:, ds(g, 1), :], S[:, 3:4, :], hid_hi[:, ds(g, 1), :],
                                      ALU.subtract).then_inc(hid_l, 1)

                groups(dve, f"f{layer}_up{part}", split_lo, up)

                def down(i, p, g):
                    y = two(Y, g)
                    dve.tensor_tensor(y, G[:, 2 * p:2 * p + 2, :], y, ALU.add).then_inc(freed_d, 1)

                if part:
                    dve.wait_ge(freed_a, 2 + plan[f"f{layer}_down0"]["totals"][0])
                    if part == 2:
                        dve.wait_ge(freed_d, 2 + plan[f"f{layer}_down1"]["totals"][1])
                groups(dve, f"f{layer}_down{part}", split_lo, down if part else None)

        w_mod, MCH = a["w_mod_2"], 256

        def pool_mod(pool):
            pool.wait_ge(cs_ready, 1)
            pool.tensor_tensor(cs[:], cs[:], VT[:, ROW["c_2"]:ROW["c_2"] + 16], ALU.mult).then_inc(pool_c, 1)
            pool.wait_ge(pool_c, 1)
            n = [1]
            lands = [0]

            def load(layer, half, first, g):
                src = w_mod[layer].rearrange("(k p) n -> p k n", p=P)[:, 4 * half:4 * half + 4,
                                                                      ds(g * MCH + first, MCH)]
                pool.dma_start(mod_w[:, half], src).then_inc(mod_landed[half], 16)

            def run(layer, vec, count, acc):
                for half in range(2):
                    load(layer, half, 0, 0)

                def body(i, more):
                    def step(ins, k):
                        ins.then_inc(pool_c, 1)
                        pool.wait_ge(pool_c, i * 7 + (n[0] + k))

                    for half in range(2):
                        w = mod_w[:, half]
                        pool.wait_ge(mod_landed[half], i * 16 + 16 * (lands[0] + 1))
                        col = cs[:, 8 * vec + 4 * half:8 * vec + 4 * half + 4].unsqueeze(2).to_broadcast([P, 4, MCH])
                        step(pool.tensor_tensor(w, w, col, ALU.mult), 3 * half + 1)
                        step(pool.tensor_tensor(w[:, 0:2], w[:, 0:2], w[:, 2:4], ALU.add), 3 * half + 2)
                        dst = mod_t[:] if half == 0 else w[:, 0]
                        step(pool.tensor_tensor(dst, w[:, 0], w[:, 1], ALU.add), 3 * half + 3)
                        if more and half == 0:
                            load(layer, 0, MCH, i)
                    step(pool.tensor_tensor(acc[:, ds(i * MCH, MCH)], mod_t[:], mod_w[:, 1, 0], ALU.add), 7)
                    if more:
                        load(layer, 1, MCH, i)

                with pool.Fori(0, count - 1) as i:
                    body(i, True)
                body(count - 1, False)
                n[0] += 7 * count
                lands[0] += count

            run(0, 0, 24, mod_acc)
            run(0, 1, 8, ctx_acc)
            pool.memset(tok[:, 0:1], 0.0).then_inc(mod_done, 1)
            pool.wait_ge(chunk_used, used_after("f1_up2"))
            pool.memset(rp[:], NEG).then_inc(setup_p, 1)
            pool.wait_ge(setup_p, 3)
            for c in (0, 32):
                pool.dma_start(rp[:, c:c + 31], a["rpb_2"].rearrange("a h r c -> (a h r) c")).then_inc(rp_dma, 16)
            for q in range(4):
                pool.wait_ge(tb_mm, q + 1)
                pool.dma_start(sel[:, q % 2, :], consts["sel"][:, q * 16 * P:(q + 1) * 16 * P]
                               ).then_inc(sel_dma[q % 2], 16)
            pool.wait_ge(x_ready, RESIDS["fpost1"] + 8)
            pool.dma_start(ctx_tm[:], a["ctx_2"].rearrange("a (b p) d -> p (a b) d", p=P)).then_inc(ctx_dma, 16)
            pool.wait_ge(h_lo, FILL["even"] + 8)
            pool.dma_start(S[:, 0, :].rearrange("p (g q) -> p g q", g=4),
                           a["w_sp_2"][0].rearrange("g p q -> p g q")).then_inc(wsp_dma, 16)
            pool.wait_ge(aux_free, 1)
            run(1, 0, 24, mod_acc)
            pool.memset(tok[:, 1:2], 0.0).then_inc(mod_done, 1)

        def mod_pe(pe, layer):
            pe.wait_ge(mod_done, layer + 1)
            for j in range(48):
                mm = pe.matmul(M[:, 3, j:j + 1], mod_acc[:, j * P:j * P + P], ones[:, 0:1], start=(j == 0),
                               stop=False, skip_group_check=True)
            for j in range(16 if layer == 0 else 0):
                mm = pe.matmul(M[:, 3, 48 + j:49 + j], ctx_acc[:, j * P:j * P + P], ones[:, 0:1], start=False,
                               stop=True, skip_group_check=True)
            mm.then_inc(mod_s, 1)

        def mod_dve(dve, link, layer):
            dve.wait_ge(mod_s, layer + 1)
            b = ROW["b_mod_2"] + 48 * layer
            gr = ROW["norm_g_2"] + 16 * layer
            if layer == 0:
                link(dve.tensor_tensor(cmod[:], M[:, 3, 48:64], VT[:, b:b + 16], ALU.add))
                link(dve.scalar_tensor_tensor(cgain[:], cmod[:, 8:16], 1.0, VT[:, gr:gr + 8], ALU.add, ALU.mult))
            link(dve.tensor_tensor(mod[:], M[:, 3, 0:48], VT[:, b:b + 48], ALU.add))
            link(dve.scalar_tensor_tensor(gain1[:], mod[:, 8:16], 1.0, VT[:, gr:gr + 8], ALU.add, ALU.mult))
            link(dve.scalar_tensor_tensor(gain2[:], mod[:, 32:40], 1.0, VT[:, gr + 8:gr + 16], ALU.add, ALU.mult))
            if layer == 1:
                link(dve.tensor_tensor(gb[:], mod[:, 16:24], VT[:, ROW["b_pw2_2"]:ROW["b_pw2_2"] + 8], ALU.mult))
            dve.memset(tok[:, 2 + layer:3 + layer], 0.0).then_inc(mod_ok, 1)

        HP = 64

        def mlstm_pe(pe, spread):
            pe.wait_ge(row_c, 2)
            for q, r in enumerate((5, 6, 10)):
                for b in range(TB):
                    mm = pe.transpose(M[:, 3, (q * TB + b) * 8:(q * TB + b) * 8 + 8], rows[0:8, r, b * P:b * P + P],
                                      ident[0:8, 0:8])
            mm.then_inc(row_t, 1)
            pe.wait_ge(freed_a, 2 + plan["m_o"]["totals"][0])
            with pe.Fori(0, 4) as i:
                for e in range(2):
                    h = i * 2 + e
                    hs = slice(HP * e, HP * e + HP)
                    pe.wait_ge(ml["n0"], h + 1)
                    pe.wait_ge(ml["n1"], h + 1)
                    pe.wait_ge(ml["dg"], h + 1)
                    pe.matmul(M[:, 1, :], ones[:], Dg[:].rearrange("p b n -> p (b n)"), start=True,
                              stop=True).then_inc(ml["bc"], 1)
                    if e == 0:
                        pe.wait_ge(ml["stg"], i + 1)
                    for s in range(TB):
                        pe.wait_ge(ml["p"], h * 4 + (s + 1))
                        pe.matmul(G[:, s, 0:T - s * P], Kp[hs, s * P:s * P + P], Qp[hs, s * P:T], start=True,
                                  stop=True).then_inc(ml["s"], 1)
                    pe.wait_ge(ml["y"], h + 1)
                    pe.wait_ge(ml["sq"], h + 1)
                    for s in range(TB):
                        pe.wait_ge(ml["p"], h * 4 + (s + 5))
                        mm = pe.matmul(M[:, 2, s * P:T], Vp[:, 256 * s + P * e:256 * s + P * e + P],
                                       PT[:, s, s * P:T], start=(s == 0), stop=(s == 3), skip_group_check=True)
                    mm.then_inc(ml["num"], 1)
                    pe.wait_ge(ml["st"], h + 1)
                    for b in range(TB):
                        for s in range(b + 1):
                            pe.matmul(M[:, 3, b:b + 1], PT[:, s, b * P:b * P + P], ones[:, 0:1],
                                      start=(b == 0 and s == 0), stop=False, skip_group_check=True)
                    pe.wait_ge(ml["sq"], h + 2)
                    for b in range(TB):
                        mm = pe.matmul(M[:, 3, 4 + b:5 + b], SQ[:, 0, b * P:b * P + P], ones[:, 0:1], start=False,
                                       stop=(b == 3), skip_group_check=True)
                    mm.then_inc(ml["ss"], 1)
            for t in range(DT):
                spread(ml["dg"], 8 + t + 1, ml["bc"])

        def mlstm_act(act):
            act.wait_ge(g_mm, 1)
            act.wait_ge(chunk_used, used_after("m_o"))
            act.wait_ge(h_lo, FILL["pre0"] + 8)
            act.activation(rows[0:8, 0, :], M[0:8, 2, :], ACT.Identity, bias=b_m[:, 0:1]).then_inc(row_a, 1)
            act.activation(rows[0:8, 1, :], M[32:40, 2, :], ACT.Copy).then_inc(row_a, 1)
            act.wait_ge(row_d, 1)
            act.activation(rows[0:8, 2, :], rows[0:8, 2, :], ACT.Exp).then_inc(row_a, 1)
            act.wait_ge(row_a, 3)
            act.activation(rows[0:8, 9, :], rows[0:8, 2, :], ACT.Ln, bias=1.0).then_inc(row_a, 1)
            act.wait_ge(row_c, 1)
            act.activation(rows[0:8, 10, :], rows[0:8, 7, :], ACT.Exp, scale=-1.0).then_inc(row_c, 1)
            with act.Fori(0, 4) as i:
                for e in range(2):
                    h = i * 2 + e
                    act.wait_ge(ml["e"], h * 4 + 1)
                    act.wait_ge(ml["bc"], h + 2)
                    act.activation(N0, M[:, 1, :], ACT.Copy, scale=-1.0).then_inc(ml["n0"], 1)
                    act.wait_ge(ml["n0"], h + 2)
                    act.wait_ge(ml["n1"], h + 2)
                    for s in range(TB):
                        act.wait_ge(ml["p"], h * 4 + (s + 3))
                        bias = gates_T[:, 0, s, ds(h, 1)]
                        one = act.activation(Lg[:, s % 2, 0:P], N1[:, s * P:s * P + P], ACT.Exp, bias=bias)
                        if s < 3:
                            one = act.activation(Lg[:, s % 2, P:T - s * P], N0[:, (s + 1) * P:T], ACT.Exp, bias=bias)
                        one.then_inc(ml["e"], 1)
                    act.wait_ge(ml["ss"], h + 1)
                    act.wait_ge(ml["num"], h + 2)
                    act.activation(SQ[:, 0, :], M[:, 2, :], ACT.Square).then_inc(ml["sq"], 1)
            act.wait_ge(ml["nar"], 1)
            act.activation(n3[:], n3[:], ACT.Sqrt, bias=eps[:], scale=1.0 / P).then_inc(ml["nar"], 1)
            fill_act(act, "mlstm", None, None, None)

        def mlstm_dve(dve, link):
            dve.wait_ge(chunk_used, used_after("m_o"))
            link(dve.memset(rows[0:8, 8, :], 1.0))
            dve.wait_ge(row_a, 2)
            link(dve.tensor_scalar(rows[0:8, 1, :], rows[0:8, 1, :], b_m[:, 1:2], None, ALU.add))
            dve.scalar_tensor_tensor(rows[0:8, 2, :], rows[0:8, 1, :], -1.0, rows[0:8, 1, :], ALU.mult,
                                     ALU.min).then_inc(row_d, 1)
            dve.wait_ge(row_a, 4)
            link(dve.scalar_tensor_tensor(rows[0:8, 3, :], rows[0:8, 1, :], 0.0, rows[0:8, 9, :], ALU.min,
                                          ALU.subtract))
            link(dve.tensor_tensor_scan(rows[0:8, 4, :], rows[0:8, 8, :], rows[0:8, 3, :], 0.0, ALU.mult, ALU.add))
            link(dve.tensor_tensor(rows[0:8, 5, :], rows[0:8, 0, :], rows[0:8, 4, :], ALU.subtract))
            link(dve.tensor_tensor_scan(rows[0:8, 6, :], rows[0:8, 8, :], rows[0:8, 5, :], 0.0, ALU.mult, ALU.max))
            dve.tensor_tensor(rows[0:8, 7, :], rows[0:8, 4, :], rows[0:8, 6, :], ALU.add).then_inc(row_c, 1)
            dve.wait_ge(row_t, 1)
            link(dve.tensor_copy(gates_T[:].rearrange("p q b h -> p (q b h)"), M[:, 3, 0:96]))
            dve.wait_ge(freed_a, 2 + plan["m_o"]["totals"][0])
            with dve.Fori(0, 4) as i:
                dve.wait_ge(ml["num"], i * 2 + 1)
                dve.tensor_copy(Kp[:, 0:T], mK[:, ds(i, 1), :].rearrange("p a n -> p (a n)"))
                dve.tensor_copy(Qp[:, 0:T], mQ[:, ds(i, 1), :].rearrange("p a n -> p (a n)"))
                dve.tensor_copy(Vp.rearrange("p (b n) -> p b n", b=4),
                                mV[:, :, ds(i * 256, 256)]).then_inc(ml["stg"], 1)
                for e in range(2):
                    h = i * 2 + e
                    dve.wait_ge(ml["bc"], h + 1)
                    dve.tensor_tensor(Dg[:], ident4, gates_T[:, 1, :, ds(h, 1)].to_broadcast([P, TB, P]),
                                      ALU.mult).then_inc(ml["dg"], 1)
                    dve.wait_ge(ml["e"], h * 4 + 1)
                    dve.wait_ge(ml["n0"], h + 2)
                    dve.tensor_tensor(N1.rearrange("p (b n) -> p b n", b=4),
                                      mask_st[:].unsqueeze(1).to_broadcast([P, TB, P]),
                                      N0.rearrange("p (b n) -> p b n", b=4), ALU.add).then_inc(ml["n1"], 1)
                    dve.wait_ge(ml["ss"], h + 1)
                    for s in range(TB):
                        dve.wait_ge(ml["s"], h * 4 + (s + 1))
                        dve.wait_ge(ml["e"], h * 4 + (s + 2))
                        dve.tensor_tensor(PT[:, s, s * P:T], G[:, s, 0:T - s * P], Lg[:, s % 2, 0:T - s * P],
                                          ALU.mult).then_inc(ml["p"], 1)
                    dve.wait_ge(ml["sq"], h + 2)
                    yv = Y[:, ds(h, 1), :].rearrange("p a n -> p (a n)")
                    dve.tensor_tensor(yv, M[:, 2, :], yv, ALU.mult).then_inc(ml["y"], 1)
                    dve.wait_ge(ml["ss"], h + 2)
                    dve.tensor_copy(stat[:, ds(h, 1), :].rearrange("p a n -> p (a n)"),
                                    M[:, 3, 0:8]).then_inc(ml["st"], 1)
            dve.wait_ge(ml["st"], 9)
            den, ssq = stat[:, :, 0:4], stat[:, :, 4:8]
            link(dve.scalar_tensor_tensor(n1[:], den, -1.0, den, ALU.mult, ALU.max))
            link(dve.tensor_tensor(n1[:], n1[:], gates_T[:, 2, :, :].rearrange("p b h -> p h b"), ALU.max))
            link(dve.reciprocal(n2[:], n1[:]))
            link(dve.tensor_tensor(n3[:], n2[:], n2[:], ALU.mult))
            dve.tensor_tensor(n3[:], n3[:], ssq, ALU.mult).then_inc(ml["nar"], 1)
            dve.wait_ge(ml["nar"], 2)
            link(dve.reciprocal(n1[:], n3[:]))
            link(dve.tensor_tensor(n2[:], n2[:], n1[:], ALU.mult))

            def produce(t, dst):
                dve.wait_ge(ml["bc"], 8 + t + 1)
                dve.tensor_tensor(Dg[:], ident4, n2[:, t, :].unsqueeze(2).to_broadcast([P, TB, P]),
                                  ALU.mult).then_inc(ml["dg"], 1)
                dve.wait_ge(ml["bc"], 8 + t + 2)
                return dve.scalar_tensor_tensor(dst, Y[:, t, :], vt("mlstm_norm", t), M[:, 1, :], ALU.mult, ALU.mult)

            dve.wait_ge(ml["y"], 9)
            fill_dve(dve, "mlstm", produce, None, None)

        def fox_pe(pe):
            pe.wait_ge(row_c, 4)
            for b in range(TB):
                mm = pe.transpose(M[:, 3, b * 16:b * 16 + 16], rows[0:16, 4, b * P:b * P + P], ident[0:16, 0:16])
            mm.then_inc(row_t, 1)
            pe.wait_ge(freed_a, 2 + plan["x_g"]["totals"][0])
            with pe.Fori(0, 8) as i:
                for e in range(2):
                    h = i * 2 + e
                    hs = slice(HP * e, HP * e + HP)
                    pe.wait_ge(fx["n0"], h + 1)
                    pe.wait_ge(fx["dg"], h + 1)
                    pe.matmul(M[:, 1, :], ones[:], Dg[:].rearrange("p b n -> p (b n)"), start=True,
                              stop=True).then_inc(fx["bc"], 1)
                    if e == 0:
                        pe.wait_ge(fx["stg"], i + 1)
                    for b in range(TB):
                        pe.matmul(G[:, b, 0:(b + 1) * P], Qp[hs, b * P:b * P + P], Kp[hs, 0:(b + 1) * P], start=True,
                                  stop=True).then_inc(fx["s"], 1)
                    for b in range(TB):
                        pe.wait_ge(fx["pt"], h * 4 + (b + 1))
                        pe.wait_ge(fx["p"], h * 4 + (b + 1))
                        for s in range(b + 1):
                            mm = pe.transpose(M[:, 2 + b % 2, s * P:s * P + P], Lg[:, b % 2, s * P:s * P + P],
                                              ident[:])
                        mm.then_inc(fx["t"], 1)
                    pe.wait_ge(fx["pt"], h * 4 + 6)
                    pe.wait_ge(fx["y"], h + 1)
                    for s in range(TB):
                        mm = pe.matmul(M[0:HP, 0, s * P:T], Vp[:, P * s + HP * e:P * s + HP * e + HP],
                                       PT[:, s, s * P:T], start=(s == 0), stop=(s == 3), skip_group_check=True)
                    mm.then_inc(fx["o"], 1)

        def fox_act(act):
            act.wait_ge(g_mm, 2)
            act.wait_ge(chunk_used, used_after("x_g"))
            act.wait_ge(h_lo, FILL["pre1"] + 8)
            act.activation(rows[0:16, 1, :], M[0:16, 2, :], ACT.Identity, bias=b_x[:, 0:1]).then_inc(row_a, 1)
            act.wait_ge(row_d, 2)
            act.activation(rows[0:16, 2, :], rows[0:16, 2, :], ACT.Exp).then_inc(row_a, 1)
            act.wait_ge(row_a, 6)
            act.activation(rows[0:16, 9, :], rows[0:16, 2, :], ACT.Ln, bias=1.0).then_inc(row_a, 1)
            act.wait_ge(row_t, 2)
            with act.Fori(0, 8) as i:
                for e in range(2):
                    h = i * 2 + e

                    def exps(b):
                        n = (b + 1) * P
                        act.wait_ge(fx["m"], h * 4 + (b + 1))
                        act.activation(Lg[:, b % 2, 0:n], Lg[:, b % 2, 0:n], ACT.Exp, bias=mx[:, b % 2, 2:3],
                                       accum_out=rsum[:, b % 2, 0:1]).then_inc(fx["e"], 1)

                    def turned(b):
                        act.wait_ge(fx["t"], h * 4 + (b + 3))
                        act.activation(PT[:, 0:b + 1, b * P:b * P + P],
                                       M[:, 2 + b % 2, 0:(b + 1) * P].rearrange("p (s n) -> p s n", n=P),
                                       ACT.Copy).then_inc(fx["pt"], 1)

                    act.wait_ge(fx["bc"], h + 2)
                    act.activation(N0, M[:, 1, :], ACT.Copy).then_inc(fx["n0"], 1)
                    act.wait_ge(fx["o"], h + 1)
                    exps(0)
                    exps(1)
                    turned(0)
                    exps(2)
                    turned(1)
                    exps(3)
                    turned(2)
                    turned(3)
            split_act(act, "fox", lambda t: act.wait_ge(fx["y"], 17), Y)

        def fox_dve(dve, link):
            dve.wait_ge(chunk_used, used_after("x_g"))
            link(dve.memset(rows[0:16, 8, :], 1.0))
            dve.wait_ge(row_a, 5)
            dve.scalar_tensor_tensor(rows[0:16, 2, :], rows[0:16, 1, :], -1.0, rows[0:16, 1, :], ALU.mult,
                                     ALU.min).then_inc(row_d, 1)
            dve.wait_ge(row_a, 7)
            link(dve.scalar_tensor_tensor(rows[0:16, 3, :], rows[0:16, 1, :], 0.0, rows[0:16, 9, :], ALU.min,
                                          ALU.subtract))
            dve.tensor_tensor_scan(rows[0:16, 4, :], rows[0:16, 8, :], rows[0:16, 3, :], 0.0, ALU.mult,
                                   ALU.add).then_inc(row_c, 2)
            dve.wait_ge(row_t, 2)
            link(dve.tensor_copy(c_T[:].rearrange("p b h -> p (b h)"), M[:, 3, 0:64]))
            dve.wait_ge(freed_a, 2 + plan["x_g"]["totals"][0])
            with dve.Fori(0, 8) as i:
                link.enter(i, 24)
                dve.wait_ge(fx["o"], i * 2 + 1)
                dve.tensor_copy(Kp[:, 0:T], xK[:, ds(i, 1), :].rearrange("p a n -> p (a n)"))
                dve.tensor_copy(Qp[:, 0:T], xQ[:, ds(i, 1), :].rearrange("p a n -> p (a n)"))
                dve.tensor_copy(Vp[:, 0:T].rearrange("p (b n) -> p b n", b=4),
                                xV[:, :, ds(i * P, P)]).then_inc(fx["stg"], 1)
                for e in range(2):
                    h = i * 2 + e
                    hs = slice(HP * e, HP * e + HP)

                    def logits(b):
                        q, n = b % 2, b * P
                        dve.wait_ge(fx["s"], h * 4 + (b + 1))
                        dve.wait_ge(fx["t"], h * 4 + (b + 1))
                        dve.memset(tok[:, 40 + b:41 + b], 0.0)
                        first = -3.0e38
                        if b:
                            link(dve.tensor_tensor_reduce(Lg[:, q, 0:n], G[:, b, 0:n], N0[:, 0:n], 1.0, first, ALU.add,
                                                          ALU.max, mx[:, q, 0:1]))
                            dve.memset(tok[:, 43 + b:44 + b], 0.0)
                            first = mx[:, q, 0:1]
                        link(dve.tensor_tensor_reduce(Lg[:, q, n:n + P], G[:, b, n:n + P], N1[:, n:n + P], 1.0, first,
                                                      ALU.add, ALU.max, mx[:, q, 1:2]))
                        dve.tensor_scalar(mx[:, q, 2:3], mx[:, q, 1:2], -1.0, None, ALU.mult).then_inc(fx["m"], 1)

                    def scaled(b):
                        q = b % 2
                        dve.wait_ge(fx["e"], h * 4 + (b + 1))
                        link(dve.reciprocal(rsum[:, q, 1:2], rsum[:, q, 0:1]))
                        dve.tensor_scalar(Lg[:, q, 0:(b + 1) * P], Lg[:, q, 0:(b + 1) * P], rsum[:, q, 1:2], None,
                                          ALU.mult).then_inc(fx["p"], 1)

                    dve.wait_ge(fx["bc"], h + 1)
                    dve.scalar_tensor_tensor(Dg[:], c_T[:, :, ds(h, 1)].to_broadcast([P, TB, P]), -1.0, ident4,
                                             ALU.mult, ALU.mult).then_inc(fx["dg"], 1)
                    dve.wait_ge(fx["n0"], h + 2)
                    link(dve.tensor_tensor(N1.rearrange("p (b n) -> p b n", b=4),
                                           N0.rearrange("p (b n) -> p b n", b=4),
                                           mask_ts[:].unsqueeze(1).to_broadcast([P, TB, P]), ALU.add))
                    logits(0)
                    logits(1)
                    scaled(0)
                    logits(2)
                    scaled(1)
                    logits(3)
                    scaled(2)
                    scaled(3)
                    dve.wait_ge(fx["o"], h + 2)
                    yv = Y[hs, ds(i, 1), :].rearrange("p a n -> p (a n)")
                    dve.tensor_tensor(yv, M[0:HP, 0, :], yv, ALU.mult).then_inc(fx["y"], 1)
            link.leave(8)
            split_dve(dve, "fox", Y)
        def second_loads(sp, load_stage, cols, pairs):
            w_in = a["w_in_2"][0]
            load_stage("c_k", cols(w_in, 1536))
            load_stage("c_v", cols(w_in, 2048))
            load_stage("n_u", cols(w_in, 0))
            load_stage("n_g", cols(w_in, 512))
            load_stage("n_q", cols(w_in, 1024))
            load_stage("n_k", cols(w_in, 1536))
            load_stage("n_v", cols(w_in, 2048))
            load_stage("n_out", cols(a["w_out_2"][0], 0))

            def ffn2(layer):
                for part in range(4):
                    load_stage(f"s{layer}_up{part}", cols(a["w_ff1_2"][layer], D * part))
                    load_stage(f"s{layer}_down{part}", cols(a["w_ff2_2"][layer][D * part:D * part + D, :], 0))

            ffn2(0)
            load_stage("p_1", pairs(a["w_pw1_2"][0], 0, D))
            load_stage("p_2", cols(a["w_pw2_2"][0], 0))
            ffn2(1)
            sp.wait_ge(fin_c, 8)
            out_v = out.rearrange("a (b p) d -> p (a b) d", p=P)
            sp.dma_start(out_v, x_tm[:]).then_inc(done, 16)
            sp.wait_ge(done, 16)

        def bias_pe(pe):
            pe.wait_ge(rp_dma, 32)
            pe.wait_ge(setup_p, 3)
            pe.wait_ge(freed_d, 2 + plan["f1_down2"]["totals"][1])
            pe.transpose(M[0:64, 2, 0:120], rp[:], ident[0:120, 0:120]).then_inc(tb_t, 1)
            pe.wait_ge(tb_r, 2)
            with pe.Fori(0, 2) as i:
                for q in range(2):
                    pe.wait_ge(sel_dma[q], i * 16 + 16)
                    for r in range(4):
                        pe.wait_ge(tb_e, i * 8 + (4 * q + r + 1))
                        for k in range(4):
                            mm = pe.matmul(G[:, r, k * 112:k * 112 + 112],
                                           sel[:, q, (4 * r + k) * P:(4 * r + k) * P + P],
                                           rm[:].rearrange("p h x -> p (h x)"), start=(k == 0), stop=(k == 3),
                                           skip_group_check=True)
                        if r < 3:
                            mm.then_inc(tb_b, 1)
                    mm.then_inc(tb_mm, 1)

        def bias_act(act):
            act.wait_ge(tb_t, 1)
            act.wait_ge(chunk_used, used_after("f1_up2"))
            t = M[:, 2, 0:120].rearrange("p (h r) -> p h r", r=15)
            act.activation(rm[0:32], t[0:32, :, 1:15], ACT.Copy).then_inc(tb_r, 1)
            act.activation(rm[32:64], t[32:64, :, 0:14], ACT.Copy).then_inc(tb_r, 1)
            act.wait_ge(mod_s, 1)
            act.wait_ge(fx["stg"], 8)
            act.wait_ge(fx["o"], 17)
            tv = tbias[:].rearrange("p h x k -> p (h x) k").rearrange("p y k -> p k y")
            with act.Fori(0, 2) as i:
                for q in range(2):
                    for r in range(4):
                        if r < 3:
                            act.wait_ge(tb_b, i * 6 + (3 * q + r + 1))
                        else:
                            act.wait_ge(tb_mm, i * 2 + (q + 3))
                        act.activation(tv[:, ds(i * 32 + (16 * q + 4 * r), 4), :],
                                       G[:, r, 0:448].rearrange("p (k y) -> p k y", y=112),
                                       ACT.Copy).then_inc(tb_e, 1)

        def even_pe(pe, spread):
            pe.wait_ge(wsp_dma, 16)
            for g in range(4):
                mm = pe.transpose(M[:, 2, g * P:g * P + P], S[:, 0, g * P:g * P + P], ident[:])
            mm.then_inc(sg_t, 1)
            spread(sg_dg, 1, sg_bc)
            pe.wait_ge(sg_n, 1)
            pe.wait_ge(sg_w, 1)
            pe.wait_ge(freed_a, 2 + plan["n_v"]["totals"][0])
            for g in range(4):
                for b in range(TB):
                    mm = pe.matmul(G[:, g, b * P:b * P + P], g_tm[:, b, g * P:g * P + P],
                                   S[:, 1, g * P:g * P + P], start=(b == 0), stop=(b == 3),
                                   skip_group_check=True)
                mm.then_inc(sg_m, 1)
            with pe.Fori(0, 4) as i:
                for e in range(2):
                    h = i * 2 + e
                    hs = slice(HP * e, HP * e + HP)
                    if e == 0:
                        pe.wait_ge(na["stg"], i + 1)
                    for b in range(TB + 1):
                        if b < TB:
                            pe.wait_ge(na["e"], h * 4 + (b + 1))
                            q = 2 * (b % 2)
                            pe.matmul(G[:, q, :], Qp[hs, b * P:b * P + P], Kp[hs, 0:T], start=True, stop=True)
                            pe.matmul(G[:, q + 1, 0:CTX], Qp[hs, b * P:b * P + P], Kp[hs, T:T + CTX], start=True,
                                      stop=True).then_inc(na["s"], 1)
                        if b:
                            pe.wait_ge(na["pt"], h * 4 + b)
                            pe.wait_ge(na["p"], h * 4 + b)
                            for s in range(6):
                                mm = pe.transpose(M[:, 2 + s // 4, (s % 4) * P:(s % 4) * P + P],
                                                  Lg[:, (b - 1) % 2, s * P:s * P + P], ident[:])
                            mm.then_inc(na["t"], 1)
                    pe.wait_ge(na["pt"], h * 4 + 5)
                    pe.wait_ge(na["y"], h + 1)
                    for s in range(6):
                        mm = pe.matmul(M[0:HP, 0, :], Vp[:, P * s + HP * e:P * s + HP * e + HP], PT[:, s, :],
                                       start=(s == 0), stop=(s == 5))
                    mm.then_inc(na["o"], 1)

        def even_act(act):
            act.wait_ge(sg_t, 1)
            act.activation(S[:, 1, :], M[:, 2, :], ACT.Copy).then_inc(sg_w, 1)
            act.wait_ge(sg_bc, 1)
            act.wait_ge(chunk_used, used_after("n_v"))
            act.activation(N0, M[:, 1, :], ACT.Copy).then_inc(sg_b, 1)
            act.wait_ge(sg_v, 1)
            act.activation(bn[:, :, 1:2], bn[:, :, 1:2], ACT.Sqrt, bias=eps[:, 0:1]).then_inc(sg_r, 1)
            with act.Fori(0, 4) as i:
                for e in range(2):
                    h = i * 2 + e
                    for b in range(TB + 1):
                        q = b % 2
                        if b < TB:
                            act.wait_ge(na["m"], h * 4 + (b + 1))
                            act.activation(Lg[:, q, 0:T], Lg[:, q, 0:T], ACT.Exp, bias=mx[:, q, 2:3],
                                           accum_out=rsum[:, q, 0:1])
                            act.activation(Lg[:, q, T:T + CTX], G[:, 2 * q + 1, 0:CTX], ACT.Exp,
                                           bias=mx[:, q, 2:3], accum_out=rsum[:, q, 1:2]).then_inc(na["e"], 1)
                        if b:
                            act.wait_ge(na["t"], h * 4 + (b + 2))
                            if b == 1:
                                act.wait_ge(na["o"], h + 1)
                            act.activation(PT[:, :, (b - 1) * P:b * P],
                                           M[:, 2:4, :].rearrange("p a n -> p (a n)")[:, 0:6 * P].rearrange(
                                               "p (s n) -> p s n", n=P), ACT.Copy).then_inc(na["pt"], 1)
            split_act(act, "mix", lambda t: act.wait_ge(na["y"], 9), Y)

        def even_dve(dve, link):
            dve.wait_ge(n_bc, NORM["even"] + 1)
            dve.tensor_tensor(Dg[:], ident4, VT[:, ROW["b_sp_2"]:ROW["b_sp_2"] + 4].unsqueeze(2).to_broadcast(
                [P, 4, P]), ALU.mult).then_inc(sg_dg, 1)
            dve.wait_ge(freed_a, 2 + plan["n_v"]["totals"][0])
            dve.wait_ge(chunk_used, used_after("n_v"))
            st = att[:, 7936:8032].rearrange("p (j k) -> p j k", k=6)
            for j in range(16):
                one = dve.bn_stats(st[:, j, :], g_tm[:, j // 4, (j % 4) * P:(j % 4) * P + P])
            link(one)
            for j in range(16):
                one = dve.bn_aggr(bn[:, j, :], st[:, j, :])
            one.then_inc(sg_v, 1)
            dve.wait_ge(sg_r, 1)
            link(dve.reciprocal(bn[:, :, 1:2], bn[:, :, 1:2]))
            for j in range(16):
                v = g_tm[:, j // 4, (j % 4) * P:(j % 4) * P + P]
                one = dve.tensor_scalar(v, v, bn[:, j, 0:1], bn[:, j, 1:2], ALU.subtract, ALU.mult)
            one.then_inc(sg_n, 1)
            dve.wait_ge(sg_b, 1)
            for g in range(4):
                dve.wait_ge(sg_m, g + 1)
                link(dve.scalar_tensor_tensor(S[:, 2 + g % 2, :].rearrange("p (b n) -> p b n", b=4),
                                              G[:, g, :].rearrange("p (b n) -> p b n", b=4), vt("ln_v_g_2", g),
                                              N0[:, g * P:g * P + P].unsqueeze(1).to_broadcast([P, 4, P]),
                                              ALU.mult, ALU.add))
                link(dve.tensor_tensor(Y[:, g, :], S[:, 2 + g % 2, :], Y[:, g, :], ALU.mult))
            tb_head = S[:, 0:2, :].rearrange("p a n -> p (a n)")[:, 0:14 * 64]
            dve.wait_ge(tb_e, 20)
            with dve.Fori(0, 4) as i:
                link.enter(i, 26)
                dve.wait_ge(na["o"], i * 2 + 1)
                for dst, src in ((Kp[:, 0:T], nK), (Kp[:, T:T + CTX], cK), (Qp, nQ)):
                    dve.tensor_copy(dst, src[:, ds(i, 1), :].rearrange("p a n -> p (a n)"))
                dve.tensor_copy(Vp[:, 0:T].rearrange("p (b n) -> p b n", b=4), nV[:, :, ds(i * P, P)])
                dve.tensor_copy(Vp[:, T:T + CTX].rearrange("p (b n) -> p b n", b=2),
                                cV[:, :, ds(i * P, P)]).then_inc(na["stg"], 1)
                for e in range(2):
                    h = i * 2 + e
                    hs = slice(HP * e, HP * e + HP)
                    link(dve.tensor_copy(tb_head, tbias[:, ds(h, 1)].rearrange("p a x k -> p (a x k)")))
                    for b in range(TB + 1):
                        if b < TB:
                            q = b % 2
                            dve.wait_ge(na["s"], h * 4 + (b + 1))
                            dve.wait_ge(na["t"], h * 4 + (b + 1))
                            tb_ = tb_head[:, 64 * (6 - 2 * b):64 * (14 - 2 * b)]
                            dve.memset(tok[:, 40 + b:41 + b], 0.0)
                            dve.tensor_tensor_reduce(Lg[:, q, 0:T], G[:, 2 * q, :], tb_, 1.0, -3.0e38, ALU.add,
                                                     ALU.max, mx[:, q, 0:1])
                            link(dve.reduce_max(mx[:, q, 1:2], G[:, 2 * q + 1, 0:CTX], AX.X))
                            dve.tensor_scalar(mx[:, q, 2:3], mx[:, q, 0:1], mx[:, q, 1:2], -1.0, ALU.max,
                                              ALU.mult).then_inc(na["m"], 1)
                        if b:
                            q = (b - 1) % 2
                            dve.wait_ge(na["e"], h * 4 + (b + 2))
                            link(dve.tensor_scalar(rsum[:, q, 2:3], rsum[:, q, 0:1], rsum[:, q, 1:2], None, ALU.add))
                            link(dve.reciprocal(rsum[:, q, 3:4], rsum[:, q, 2:3]))
                            dve.tensor_scalar(Lg[:, q, :], Lg[:, q, :], rsum[:, q, 3:4], None,
                                              ALU.mult).then_inc(na["p"], 1)
                    dve.wait_ge(na["o"], h + 2)
                    dve.tensor_copy(Y[hs, ds(i + 4, 1), :].rearrange("p a n -> p (a n)"),
                                    M[0:HP, 0, :]).then_inc(na["y"], 1)
            link.leave(4)
            dve.memset(tok[:, 4:5], 0.0).then_inc(aux_free, 1)
            split_dve(dve, "mix", Y)

        def add_to_x(dve, name, first):
            dve.wait_ge(freed_d, 2 + plan[name]["before"][1])

            def evacuate(i, p, g):
                for m in range(2):
                    x = X[:, ds(g * 2 + m, 1), :]
                    one = dve.scalar_tensor_tensor(x, G[:, 2 * p + m:2 * p + m + 1, :], mod[:, ds(g * 2 + (m + first), 1)],
                                                   x, ALU.mult, ALU.add)
                one.then_inc(freed_d, 1)
            groups(dve, name, split_lo, evacuate)

        def ffn2_act(act, layer):
            for part in range(4):
                base = HIDDEN[f"s{layer}"] + 4 * part

                def up(i, p, g):
                    act.wait_ge(hid_l, g + (base + 1))
                    act.activation(S[:, 0:2, :], G[:, 2 * p:2 * p + 2, :], ACT.Relu).then_inc(freed_a, 1)
                    act.wait_ge(f_m, g + (base + 1))
                    act.activation(two(hid_hi, g), S[:, 2:4, :], ACT.Copy).then_inc(hid_h, 1)

                groups(act, f"s{layer}_up{part}", split_hi, up)
                groups(act, f"s{layer}_down{part}", split_hi, None)

        def ffn2_dve(dve, layer):
            for part in range(4):
                base = HIDDEN[f"s{layer}"] + 4 * part
                freed = plan[f"s{layer}_up{part}"]["freed"]

                def up(i, p, g):
                    dve.wait_ge(freed_a, g + (2 + freed + 1))
                    dve.tensor_tensor(S[:, 2:4, :], S[:, 0:2, :], S[:, 0:2, :], ALU.mult).then_inc(f_m, 1)
                    dve.wait_ge(hid_h, g + (base + 1))
                    dve.tensor_tensor(two(hid_lo, g), S[:, 2:4, :], two(hid_hi, g), ALU.subtract).then_inc(hid_l, 1)

                groups(dve, f"s{layer}_up{part}", split_lo, up)
                add_to_x(dve, f"s{layer}_down{part}", 40)

        def second_pe(pe, linear, norm, from_h, spread):
            bias_pe(pe)
            pe.wait_ge(ctx_dma, 16)
            for t in range(DT):
                if t >= 2:
                    pe.wait_ge(ct_c, t - 1)
                if t == 0:
                    pe.wait_ge(tb_r, 2)
                for b in range(2):
                    mm = pe.transpose(M[:, 2 + t % 2, b * P:b * P + P], ctx_tm[:, b, t * P:t * P + P], ident[:])
                mm.then_inc(ct_t, 1)
            norm("ctx", 2)
            pe.wait_ge(tb_e, 20)
            linear("c_k", H_hi, H_lo, need=from_h("ctx"), n=CTX)
            linear("c_v", H_hi, H_lo, "T", need=from_h("ctx"), n=CTX)
            norm("even")
            for name, mode in (("n_u", "F"), ("n_g", "T"), ("n_q", "F"), ("n_k", "F"), ("n_v", "T")):
                linear(name, H_hi, H_lo, mode, need=from_h("even"))
            even_pe(pe, spread)
            linear("n_out", H_hi, H_lo, need=from_h("mix"))

            def ffn2(layer):
                for part in range(4):
                    base = HIDDEN[f"s{layer}"] + 4 * part
                    linear(f"s{layer}_up{part}", H_hi, H_lo, need=from_h(f"mlp{layer}"))
                    linear(f"s{layer}_down{part}", hid_hi, hid_lo,
                           need=lambda t, base=base: pe.wait_ge(hid_l, base + t // 2 + 2))

            norm("mlp0")
            ffn2(0)
            mod_pe(pe, 1)
            norm("odd")
            linear("p_1", H_hi, H_lo, need=from_h("odd"))
            for t in range(DT):
                pe.wait_ge(cv_d, t + 1)
                for b in range(TB):
                    mm = pe.matmul(M[:, 0, b:b + 1], Y[:, t, b * P:b * P + P], ones[:, 0:1],
                                   start=(t == 0 and b == 0), stop=(t == 7), skip_group_check=True)
            mm.then_inc(cv_s, 1)
            spread(cv_dg, 1, cv_bc)
            norm("conf")
            linear("p_2", H_hi, H_lo, need=from_h("conf"))
            norm("mlp1")
            ffn2(1)
            norm("final")
            for t in range(DT):
                pe.wait_ge(fin_t, t + 1)
                if t >= 4:
                    pe.wait_ge(fin_c, t - 3)
                for b in range(TB):
                    mm = pe.transpose(G[:, t % 4, b * P:b * P + P], S[:, t % 4, b * P:b * P + P], ident[:])
                mm.then_inc(fin_m, 1)

        def after_x(eng, name):
            st = plan[name]
            return lambda t: eng.wait_ge(freed_d, 2 + st["freed"] + t // 2 + 1)

        def second_act(act):
            bias_act(act)
            act.wait_ge(mod_ok, 1)
            norm_act(act, "ctx", ct, lambda t: act.wait_ge(ct_c, t + 1), 2)
            fill_act(act, "ctx", None, lambda t: cmod[:, t:t + 1], used_after("f1_up2"), CTX)
            act.wait_ge(tb_mm, 6)
            plain(act, "c_k", lambda g: two(cK, g), lambda p: G[:, 2 * p:2 * p + 2, 0:CTX])
            plain(act, "c_v", lambda g: cV[:, :, ds(g * GC, GC)],
                  lambda p: G[:, 2 * p, :].rearrange("p (b n) -> p b n", b=2))
            act.wait_ge(x_ready, RESIDS["fpost1"] + 8)
            norm_act(act, "even", X, lambda t: None)
            fill_act(act, "even", None, lambda t: mod[:, t:t + 1], used_after("c_v"))
            tokens_out = lambda p: G[:, 2 * p:2 * p + 2, :].rearrange("p a (b n) -> p (a b) n", b=2)
            plain(act, "n_u", lambda g: two(Y, g), None, ACT.Gelu_apprx_tanh)
            plain(act, "n_g", lambda g: g_tm[:, :, ds(g * GC, GC)], tokens_out, ACT.Gelu_apprx_tanh)
            plain(act, "n_q", lambda g: two(nQ, g), None, ACT.Copy, 0.125)
            plain(act, "n_k", lambda g: two(nK, g))
            plain(act, "n_v", lambda g: nV[:, :, ds(g * GC, GC)], tokens_out)
            even_act(act)
            groups(act, "n_out", split_hi, None)
            norm_act(act, "mlp0", X, after_x(act, "n_out"))
            fill_act(act, "mlp0", None, lambda t: mod[:, 24 + t:25 + t], used_after("n_out"))
            ffn2_act(act, 0)
            norm_act(act, "odd", X, after_x(act, "s0_down3"))
            act.wait_ge(mod_ok, 2)
            fill_act(act, "odd", None, lambda t: mod[:, t:t + 1], used_after("s0_up3"))

            def glu(i, p, g):
                act.wait_ge(freed_d, g + (plan["p_1"]["freed"] + 1))
                act.activation(S[:, p, :], G[:, 2 * p + 1, :], ACT.Sigmoid,
                               bias=VT[:, ds(g + (ROW["b_pw1_2"] + 8), 1)]).then_inc(glu_a, 1)

            groups(act, "p_1", split_hi, glu)
            norm_act(act, "conf", Y, lambda t: act.wait_ge(cv_m, t + 1))
            for t in range(DT):
                act.wait_ge(cv_t, t + 1)
                act.activation(Y[:, t, :], S[:, t % 4, :], ACT.Silu, bias=vt("ln_c_b_2", t)).then_inc(cv_y, 1)
                if t:
                    split_one(act, t - 1)
            split_one(act, 7)
            groups(act, "p_2", split_hi, None)
            norm_act(act, "mlp1", X, after_x(act, "p_2"))
            fill_act(act, "mlp1", None, lambda t: mod[:, 24 + t:25 + t], used_after("p_2"))
            ffn2_act(act, 1)
            norm_act(act, "final", X, after_x(act, "s1_down3"))
            for t in range(DT):
                act.wait_ge(fin_m, t + 1)
                act.activation(x_tm[:, :, t * P:t * P + P], G[:, t % 4, :].rearrange("p (b n) -> p b n", b=4),
                               ACT.Copy).then_inc(fin_c, 1)

        def split_one(act, t):
            act.wait_ge(cv_y, t + 1)
            act.activation(H_hi[:, t, :], Y[:, t, :], ACT.Copy).then_inc(h_hi, 1)

        def plain(act, name, dst, src=None, func=ACT.Copy, scale=1.0):
            def evacuate(i, p, g):
                s = src(p) if src else G[:, 2 * p:2 * p + 2, :]
                act.activation(dst(g), s, func, scale=scale).then_inc(freed_a, 1)
            groups(act, name, split_hi, evacuate)

        def second_dve(dve, link):
            for t in range(DT):
                dve.wait_ge(ct_t, t + 1)
                dve.tensor_copy(ct[:, t, :], M[:, 2 + t % 2, 0:CTX]).then_inc(ct_c, 1)
            dve.wait_ge(mod_ok, 1)
            dve.wait_ge(x_ready, RESIDS["fpost1"] + 8)
            pre_dve(dve, "ctx", ct, lambda t: cgain[:, t:t + 1], lambda t: cmod[:, t:t + 1], used_after("f1_up2"), 2)
            for name in ("c_k", "c_v"):
                groups(dve, name, split_lo, None)
            pre_dve(dve, "even", X, lambda t: gain1[:, t:t + 1], lambda t: mod[:, t:t + 1], used_after("c_v"))
            for name in ("n_u", "n_g", "n_q", "n_k", "n_v"):
                groups(dve, name, split_lo, None)
            even_dve(dve, link)
            add_to_x(dve, "n_out", 16)
            pre_dve(dve, "mlp0", X, lambda t: gain2[:, t:t + 1], lambda t: mod[:, 24 + t:25 + t],
                    used_after("n_out"))
            ffn2_dve(dve, 0)
            dve.wait_ge(freed_d, 2 + plan["s0_down3"]["totals"][1])
            mod_dve(dve, link, 1)
            dve.wait_ge(chunk_used, used_after("s0_down3"))
            link(dve.memset(yp[:], 0.0))
            pre_dve(dve, "odd", X, lambda t: gain1[:, t:t + 1], lambda t: mod[:, t:t + 1], used_after("s0_up3"))
            dve.wait_ge(n_bc, NORM["odd"] + 1)

            def glu(i, p, g):
                if p == 0:
                    link.enter(i, 2 * (CONV_K - 1))
                dve.wait_ge(glu_a, g + 1)
                dve.scalar_tensor_tensor(yp[:, ds(g, 1), PAD:PAD + T], G[:, 2 * p:2 * p + 1, :],
                                         VT[:, ds(g + ROW["b_pw1_2"], 1)], S[:, p:p + 1, :], ALU.add,
                                         ALU.mult).then_inc(freed_d, 1)
                dve.wait_ge(freed_d, g + (2 + plan["p_1"]["freed"] + 1))
                y = Y[:, ds(g, 1), :]
                tap = lambda j: VT[:, ds(g + (ROW["w_dw_2"] + 8 * j), 1)]
                link(dve.tensor_scalar(y, yp[:, ds(g, 1), 0:T], tap(0), VT[:, ds(g + ROW["b_dw_2"], 1)], ALU.mult,
                                       ALU.add))
                for j in range(1, CONV_K):
                    one = dve.scalar_tensor_tensor(y, yp[:, ds(g, 1), j:j + T], tap(j), y, ALU.mult, ALU.add)
                    if j < CONV_K - 1:
                        link(one)
                one.then_inc(cv_d, 1)

            groups(dve, "p_1", split_lo, glu)
            link.leave(4)
            dve.wait_ge(cv_s, 1)
            dve.tensor_scalar(rs[:], M[:, 0, 0:4], 1.0 / D, None, ALU.mult).then_inc(cv_r, 1)
            dve.wait_ge(cv_r, 1)
            dve.tensor_tensor(Dg[:], ident4, rs[:].unsqueeze(2).to_broadcast([P, TB, P]), ALU.mult).then_inc(cv_dg, 1)
            dve.wait_ge(cv_bc, 1)
            for t in range(DT):
                dve.tensor_tensor(Y[:, t, :], Y[:, t, :], M[:, 1, :], ALU.subtract).then_inc(cv_m, 1)
            for t in range(DT):
                one = dve.tensor_scalar(X[:, t, :], X[:, t, :], gb[:, t:t + 1], None, ALU.add)
            link(one)
            row = norm_dve(dve, "conf")

            def low(t):
                dve.wait_ge(h_hi, FILL["conf"] + t + 1)
                dve.tensor_tensor(H_lo[:, t, :], Y[:, t, :], H_hi[:, t, :], ALU.subtract).then_inc(h_lo, 1)

            for t in range(DT):
                if t >= 4:
                    dve.wait_ge(cv_y, t - 3)
                dve.scalar_tensor_tensor(S[:, t % 4, :], Y[:, t, :], vt("ln_c_g_2", t), row, ALU.mult,
                                         ALU.mult).then_inc(cv_t, 1)
                if t >= 2:
                    low(t - 2)
            low(6)
            low(7)
            add_to_x(dve, "p_2", 16)
            pre_dve(dve, "mlp1", X, lambda t: gain2[:, t:t + 1], lambda t: mod[:, 24 + t:25 + t], used_after("p_2"))
            ffn2_dve(dve, 1)
            row = norm_dve(dve, "final")
            for t in range(DT):
                if t >= 4:
                    dve.wait_ge(fin_m, t - 3)
                dve.scalar_tensor_tensor(S[:, t % 4, :], X[:, t, :], vt("final_g_2", t), row, ALU.mult,
                                         ALU.mult).then_inc(fin_t, 1)

        @block.sync
        def _(sp):
            sp.dma_start(x_tm[:], a["x"].rearrange("b (t p) d -> p (b t) d", p=P)).then_inc(x_dma, 16)
            sp.dma_start(ident[:], consts["ident"]).then_inc(c_dma, 16)
            sp.dma_start(mask_ts[:], consts["mask"]).then_inc(c_dma, 16)
            sp.dma_start(mask_st[:], consts["mask_t"]).then_inc(c_dma, 16)
            sp.dma_start(b_m[:], a["mlstm_b_gate"].rearrange("a (g h) -> (a h) g", g=2),
                         allow_slow_non_contiguous=True).then_inc(c_dma, 16)
            sp.dma_start(b_x[:], a["kv_b_f"].rearrange("(h a) -> h a", a=1),
                         allow_slow_non_contiguous=True).then_inc(c_dma, 16)

            def load_chunk(src, j, n=KC):
                dst = raw[:, j, :].rearrange("p (k n) -> p k n", k=KC)[:, 0:n, :]
                if len(src.shape) == 4:
                    for h in range(2):
                        sp.dma_start(dst[:, :, h * P:h * P + P], src[:, :, h, :]).then_inc(raw_landed[j], 16)
                else:
                    sp.dma_start(dst, src).then_inc(raw_landed[j], 32)

            def load_stage(name, source):
                st = plan[name]
                with sp.Fori(0, st["groups"] // 2) as i:
                    for p in range(2):
                        src = source(i * 2 + p)
                        for j in range(2):
                            c = 2 * p + j
                            k1 = min(KC, st["ktiles"] - KC * j)
                            sp.wait_ge(lo_done, i * 4 + (st["chunk"] + c + 1))
                            load_chunk(src[:, KC * j:KC * j + k1], c, k1)

            def cols(w, first):
                wv = w.rearrange("(k p) n -> p k n", p=P)
                return lambda g: wv[:, :, ds(g * GC + first, GC)]

            def pairs(w, first, half):
                wv = w.rearrange("(k p) (h n) -> p k h n", p=P, h=2)
                return lambda g: wv[:, :, :, ds(g * P + first, P)]

            sp.wait_ge(setup_p, 1)
            for name, n, r, m in vector_dmas():
                names = " ".join("abcd"[:len(a[name].shape)])
                flat = a[name].rearrange(f"{names} -> ({names})").rearrange("(r p) -> r p", p=P)
                sp.dma_start(v_rows[r % P:r % P + m, r // P, :], flat[n:n + m, :]).then_inc(v_dma, 16)
            w_in = a["mlstm_w_in"].rearrange("a d n -> (a d) n")
            load_stage("m_q", cols(w_in, 0))
            sp.wait_ge(setup_p, 2)
            for i in range(2):
                sp.dma_start(gw_raw[:, :, 32 * i:32 * i + 8],
                             w_in.rearrange("(k p) n -> p k n", p=P)[:, :, 3072 + 8 * i:3080 + 8 * i],
                             allow_slow_non_contiguous=True).then_inc(g_dma, 16)
            load_stage("m_k", cols(w_in, 512))
            load_stage("m_v", cols(w_in, 1024))
            load_stage("m_o", cols(w_in, 2048))
            load_stage("m_out", cols(a["mlstm_w_out"].rearrange("a d n -> (a d) n"), 0))

            def ffn1(layer):
                for part, n in enumerate((8, 8, 6)):
                    load_stage(f"f{layer}_up{part}", pairs(a["ffn_w_up"][layer], 8 * P * part, FF1))
                    down = a["ffn_w_down"][layer][8 * P * part:8 * P * part + n * P, :]
                    load_stage(f"f{layer}_down{part}", cols(down, 0))

            ffn1(0)
            load_stage("kv_k", cols(a["kv_w"], 0))
            load_stage("kv_v", cols(a["kv_w"], 1024))
            load_stage("x_q", cols(a["fox_w_qg"][0], 0))
            load_stage("x_g", cols(a["fox_w_qg"][0], 1024))
            load_stage("x_out", cols(a["fox_w_out"][0], 0))
            ffn1(1)
            second_loads(sp, load_stage, cols, pairs)

        @block.gpsimd
        def _(pool):
            pool.memset(v_rows[:], 0.0).then_inc(setup_p, 1)
            pool.memset(ones[:], 1.0).then_inc(chunk_used, 4)
            pool.memset(eps[:], EPS).then_inc(lo_done, 4)
            pool.wait_ge(setup_t, 9)
            pool.memset(gw_raw[:], 0.0).then_inc(setup_p, 1)
            pool_mod(pool)

        @block.tensor
        def _(pe):
            def linear(name, hi, lo, mode="F", need=None, n=T):
                st = plan[name]
                sem_, base = (freed_a, st["freed"]) if st["by"] == "A" else (freed_d, st["freed"])
                pe.wait_ge(freed_a, 2 + st["before"][0])
                pe.wait_ge(freed_d, 2 + st["before"][1])
                with pe.Fori(0, st["groups"] // 2) as i:
                    for p in range(2):
                        pe.wait_ge(sem_, i * 2 + (base + p + 1))
                        for j in range(2):
                            c = 2 * p + j
                            pe.wait_ge(lo_done, i * 4 + (st["chunk"] + c + 5))
                            nk = min(KC, st["ktiles"] - KC * j)
                            wh = w_hi[:, c, :].rearrange("p (k n) -> p k n", k=KC)
                            wl = w_lo[:, c, :].rearrange("p (k n) -> p k n", k=KC)
                            if mode == "F":
                                for m in range(2):
                                    for k in range(nk):
                                        t = KC * j + k
                                        if p == 0 and m == 0:
                                            need(t)
                                        ms = slice(m * P, m * P + P)
                                        for q, (lw, rh) in enumerate(((wh, hi), (wh, lo), (wl, hi))):
                                            mm = pe.matmul(G[:, 2 * p + m, 0:n], lw[:, k, ms], rh[:, t, 0:n],
                                                           start=(t == 0 and q == 0),
                                                           stop=(t == st["ktiles"] - 1 and q == 2),
                                                           skip_group_check=True)
                            else:
                                for b in range(n // P):
                                    bs = slice(b * P, b * P + P)
                                    for k in range(nk):
                                        t = KC * j + k
                                        if p == 0 and b == 0:
                                            need(t)
                                        for q, (lh, rw) in enumerate(((hi, wh), (lo, wh), (hi, wl))):
                                            mm = pe.matmul(G[:, 2 * p + b // 2, (b % 2) * GC:(b % 2) * GC + GC],
                                                           lh[:, t, bs], rw[:, k, :],
                                                           start=(t == 0 and q == 0 and b % 2 == 0),
                                                           stop=(t == st["ktiles"] - 1 and q == 2 and b % 2 == 1),
                                                           skip_group_check=True)
                            mm.then_inc(chunk_used, 1)

            def from_h(fill):
                return lambda t: pe.wait_ge(h_lo, FILL[fill] + t + 1)

            def norm(name, blocks=TB):
                i = NORM[name]
                for t in range(DT):
                    pe.wait_ge(n_sq, 8 * i + t + 1)
                    if t == 0 and i:
                        pe.wait_ge(n_sd, i)
                    for b in range(blocks):
                        mm = pe.matmul(M[:, 0, b:b + 1], SQ[:, t % 2, b * P:b * P + P], ones[:, 0:1],
                                       start=(t == 0 and b == 0), stop=(t == 7), skip_group_check=True)
                    mm.then_inc(n_ss, 1)
                spread(n_dg, i + 1, n_bc, blocks)

            def spread(diag_ready, value, sent, blocks=TB):
                pe.wait_ge(diag_ready, value)
                pe.matmul(M[:, 1, 0:blocks * P], ones[:], Dg[:, 0:blocks, :].rearrange("p b n -> p (b n)"),
                          start=True, stop=True).then_inc(sent, 1)

            def gate_rows(first, fill):
                pe.wait_ge(g_lo, first + 1)
                for t in range(DT):
                    pe.wait_ge(h_lo, FILL[fill] + t + 1)
                    for q, (lw, rh) in enumerate(((gw_hi, H_hi), (gw_hi, H_lo), (gw_lo, H_hi))):
                        mm = pe.matmul(M[:, 2, :], lw[:, t, :], rh[:, t, :], start=(t == 0 and q == 0),
                                       stop=(t == 7 and q == 2))
                mm.then_inc(g_mm, 1)

            pe.wait_ge(c_dma, 80)
            pe.wait_ge(chunk_used, 4)
            pe.wait_ge(v_dma, 16 * VECTOR_DMAS)
            for r in range(VBLOCKS):
                mm = pe.transpose(G[:, r // 4, (r % 4) * P:(r % 4) * P + P], v_rows[:, r, :], ident[:])
            mm.then_inc(setup_t, 1)
            pe.wait_ge(x_dma, 16)
            for t in range(DT):
                if t >= 2:
                    pe.wait_ge(x_ready, t - 1)
                for b in range(TB):
                    mm = pe.transpose(M[:, 2 + t % 2, b * P:b * P + P], x_tm[:, b, t * P:t * P + P], ident[:])
                mm.then_inc(setup_t, 1)

            norm("pre0")
            pe.wait_ge(setup_c, 1)
            h0 = from_h("pre0")
            linear("m_q", H_hi, H_lo, need=h0)
            linear("m_k", H_hi, H_lo, need=h0)
            gate_rows(0, "pre0")
            linear("m_v", H_hi, H_lo, "T", need=h0)
            linear("m_o", H_hi, H_lo, need=h0)
            mlstm_pe(pe, spread)
            linear("m_out", H_hi, H_lo, need=from_h("mlstm"))

            def ffn1(layer):
                base = HIDDEN[f"f{layer}"]
                for part in range(3):
                    linear(f"f{layer}_up{part}", H_hi, H_lo, need=from_h(f"ffn{layer}"))
                    linear(f"f{layer}_down{part}", hid_hi, hid_lo,
                           need=lambda t, part=part: pe.wait_ge(hid_l, base + 8 * part + t + 2))

            norm("post0")
            norm("ffn0")
            ffn1(0)
            mod_pe(pe, 0)
            norm("fpost0")
            norm("kv")
            gate_rows(1, "kv")
            linear("kv_k", H_hi, H_lo, need=from_h("kv"))
            linear("kv_v", H_hi, H_lo, "T", need=from_h("kv"))
            norm("pre1")
            linear("x_q", H_hi, H_lo, need=from_h("pre1"))
            linear("x_g", H_hi, H_lo, need=from_h("pre1"))
            fox_pe(pe)
            linear("x_out", H_hi, H_lo, need=from_h("fox"))
            norm("post1")
            norm("ffn1")
            ffn1(1)
            norm("fpost1")
            second_pe(pe, linear, norm, from_h, spread)
        @block.scalar
        def _(act):
            act.wait_ge(c_dma, 80)
            act.wait_ge(lo_done, 4)
            act.wait_ge(setup_t, 1)
            act.activation(VT[:], G[:, 0:2, :].rearrange("p a n -> p (a n)")[:, 0:VBLOCKS * P],
                           ACT.Copy).then_inc(setup_c, 1)
            act.wait_ge(setup_c, 1)
            act.activation(cs[:], VT[:, ROW["c_2"]:ROW["c_2"] + 16], ACT.Sigmoid).then_inc(cs_ready, 1)
            for j in range(SLOTS):
                split_hi(act, 0, 0, j)
            norm_act(act, "pre0", X, lambda t: act.wait_ge(x_ready, t + 1))
            fill_act(act, "pre0", None, None, None)
            plain(act, "m_q", lambda g: two(mQ, g), None, ACT.Copy, 0.125)
            plain(act, "m_k", lambda g: two(mK, g))
            tokens_out = lambda p: G[:, 2 * p:2 * p + 2, :].rearrange("p a (b n) -> p (a b) n", b=2)
            gate_weights_act(act, 0)
            plain(act, "m_v", lambda g: mV[:, :, ds(g * GC, GC)], tokens_out)
            act.wait_ge(g_mm, 1)
            plain(act, "m_o", lambda g: two(Y, g), None, ACT.Sigmoid)
            mlstm_act(act)
            plain(act, "m_out", lambda g: two(Y, g))

            def y_ready(name):
                st = plan[name]
                s, n = (freed_a, st["freed"]) if st["by"] == "A" else (freed_d, st["freed"])
                return lambda t: act.wait_ge(s, 2 + n + t // 2 + 1)

            def x_from(name):
                return lambda t: act.wait_ge(x_ready, RESIDS[name] + t + 1)

            norm_act(act, "post0", Y, y_ready("m_out"))
            norm_act(act, "ffn0", X, x_from("post0"))
            fill_act(act, "ffn0", None, None, used_after("m_out"))
            ffn1_act(act, 0)
            norm_act(act, "fpost0", Y, y_ready("f0_down2"))
            norm_act(act, "kv", X, x_from("fpost0"))
            act.wait_ge(g_zero, 1)
            act.dma_start(gw_raw[:, :, 0:16], a["kv_w"].rearrange("(k p) n -> p k n", p=P)[:, :, 2048:2064],
                          allow_slow_non_contiguous=True).then_inc(g_dma, 16)
            fill_act(act, "kv", None, None, used_after("f0_up2"))
            gate_weights_act(act, 1)
            plain(act, "kv_k", lambda g: two(xK, g))
            plain(act, "kv_v", lambda g: xV[:, :, ds(g * GC, GC)], tokens_out)
            norm_act(act, "pre1", X, lambda t: None)
            fill_act(act, "pre1", None, None, used_after("kv_v"))
            act.wait_ge(mod_s, 1)
            plain(act, "x_q", lambda g: two(xQ, g), None, ACT.Copy, 0.125)
            plain(act, "x_g", lambda g: two(Y, g), None, ACT.Sigmoid)
            fox_act(act)
            plain(act, "x_out", lambda g: two(Y, g))
            norm_act(act, "post1", Y, y_ready("x_out"))
            norm_act(act, "ffn1", X, x_from("post1"))
            fill_act(act, "ffn1", None, None, used_after("x_out"))
            ffn1_act(act, 1)
            norm_act(act, "fpost1", Y, y_ready("f1_down2"))
            second_act(act)

        @block.vector
        def _(dve):
            link = Chain(dve, chain_d)
            for n, (s, v) in enumerate(TOKENS):
                dve.memset(tok[:, 8 + n:9 + n], 0.0).then_inc(s, v)
            dve.wait_ge(c_dma, 80)
            for t in range(DT):
                dve.wait_ge(setup_t, t + 2)
                dve.tensor_copy(X[:, t, :], M[:, 2 + t % 2, :]).then_inc(x_ready, 1)
            for j in range(SLOTS):
                split_lo(dve, 0, 0, j)
            dve.wait_ge(setup_c, 1)
            pre_dve(dve, "pre0", X, lambda t: vt("norm_mix_pre", t), None, None)
            groups(dve, "m_q", split_lo, None)
            groups(dve, "m_k", split_lo, None)
            gate_weights_dve(dve, 0)
            groups(dve, "m_v", split_lo, None)
            groups(dve, "m_o", split_lo, None)
            mlstm_dve(dve, link)
            groups(dve, "m_out", split_lo, None)
            residual_dve(dve, "post0", lambda t: vt("norm_mix_post", t))
            pre_dve(dve, "ffn0", X, lambda t: vt("norm_ffn_pre", t), None, used_after("m_out"))
            ffn1_dve(dve, 0)
            mod_dve(dve, link, 0)
            residual_dve(dve, "fpost0", lambda t: vt("norm_ffn_post", t))
            dve.wait_ge(x_ready, RESIDS["fpost0"] + 8)
            dve.memset(gw_raw[:], 0.0).then_inc(g_zero, 1)
            pre_dve(dve, "kv", X, lambda t: vt("kv_norm", t), None, used_after("f0_up2"))
            gate_weights_dve(dve, 1)
            groups(dve, "kv_k", split_lo, None)
            groups(dve, "kv_v", split_lo, None)
            pre_dve(dve, "pre1", X, lambda t: vt("norm_mix_pre", 8 + t), None, used_after("kv_v"))
            groups(dve, "x_q", split_lo, None)
            groups(dve, "x_g", split_lo, None)
            fox_dve(dve, link)
            groups(dve, "x_out", split_lo, None)
            residual_dve(dve, "post1", lambda t: vt("norm_mix_post", 8 + t))
            pre_dve(dve, "ffn1", X, lambda t: vt("norm_ffn_pre", 8 + t), None, used_after("x_out"))
            ffn1_dve(dve, 1)
            residual_dve(dve, "fpost1", lambda t: vt("norm_ffn_post", 8 + t))
            second_dve(dve, link)


class Chain:

    def __init__(self, engine, semaphore):
        self.engine, self.semaphore, self.n, self.i, self.per, self.k = engine, semaphore, 0, None, 0, 0

    def __call__(self, ins):
        ins.then_inc(self.semaphore, 1)
        if self.i is None:
            self.n += 1
            self.engine.wait_ge(self.semaphore, self.n)
        else:
            self.k += 1
            self.engine.wait_ge(self.semaphore, self.i * self.per + (self.n + self.k))

    def enter(self, i, per):
        self.i, self.per, self.k = i, per, 0

    def leave(self, times):
        assert self.k == self.per, (self.k, self.per)
        self.n += self.per * times
        self.i = None


_NAMES = ["x"] + [n for n, _ in VECTORS] + [
    "mlstm_w_in", "mlstm_b_gate", "mlstm_w_out", "kv_w", "kv_b_f", "fox_w_qg", "fox_w_out", "ffn_w_up",
    "ffn_w_down", "ctx_2", "w_mod_2", "w_in_2", "w_out_2", "w_sp_2", "rpb_2", "w_pw1_2", "w_pw2_2", "w_ff1_2",
    "w_ff2_2"]


def shape_constants():
    import numpy as np

    r = np.arange(P)
    mask = np.where(r[None, :] <= r[:, None], 0.0, NEG).astype(np.float32)
    sel = np.zeros((64, 64, P), np.float32)
    for kc in range(64):
        for qc in range(64):
            start = min(max(qc - 8, 0), 48)
            row = kc - qc + 15 if start <= kc < start + 16 else 31
            sel[row, kc, qc] = 1.0
            sel[32 + row, kc, 64 + qc] = 1.0
    return {"ident": np.eye(P, dtype=np.float32), "mask": mask, "mask_t": np.ascontiguousarray(mask.T),
            "sel": sel.reshape(64, 64 * P)}


def kernel(**inputs):
    import numpy as np
    import concourse.bacc as bacc
    from concourse.bass_utils import run_bass_kernel_spmd

    nc = bacc.Bacc("TRN2", target_bir_lowering=False, num_devices=1)
    arrays, views, consts = {}, {}, {}
    for name in _NAMES:
        v = np.ascontiguousarray(inputs[name])
        arrays[f"in_{name}"] = v
        views[name] = nc.dram_tensor(f"in_{name}", v.shape, F32, kind="ExternalInput").ap()
    for name, v in shape_constants().items():
        arrays[f"const_{name}"] = v
        consts[name] = nc.dram_tensor(f"const_{name}", v.shape, F32, kind="ExternalInput").ap()
    out = nc.dram_tensor("out", (1, T, D), F32, kind="ExternalOutput").ap()
    build(nc, views, out, consts)
    r = run_bass_kernel_spmd(nc, [arrays], core_ids=[0])
    return r.results[0]["out"]
```

```python
from contextlib import ExitStack

import concourse.bass as bass
from concourse import mybir

ALU = mybir.AluOpType
ACT = mybir.ActivationFunctionType
AX = mybir.AxisListType
F32 = mybir.dt.float32
F32R = mybir.dt.float32r

P = 128
T = 512
TB = T // P
D = 1024
DT = D // P
CTX = 256
EPS = 1e-6
NEG = -1e30
FF1 = 2816
FF1_T = FF1 // P
FF2 = 4096
SLOTS = 4
KC = 4
GC = 256
CONV_K = 31
PAD = CONV_K // 2
PE_TAPS = 10
V_TAPS = CONV_K - PE_TAPS


def ds(a, n):
    return bass.ds(a, n)


VECTORS = [
    ("norm_mix_pre", 16), ("norm_mix_post", 16), ("norm_ffn_pre", 16), ("norm_ffn_post", 16),
    ("mlstm_norm", 8), ("kv_norm", 8), ("ffn_conv_w", 264), ("ffn_conv_b", 88), ("norm_g_2", 32),
    ("ln_v_g_2", 4), ("b_pw1_2", 16), ("w_dw_2", 248), ("b_dw_2", 8), ("ln_c_g_2", 8), ("ln_c_b_2", 8),
    ("b_pw2_2", 8), ("final_g_2", 8), ("b_mod_2", 96), ("c_2", 8), ("c_ctx_2", 8), ("b_sp_2", 4),
]
ROW = {}
_n = 0
for _name, _rows in VECTORS:
    ROW[_name] = _n
    _n += _rows
VROWS = _n
VBLOCKS = -(-VROWS // P)


def vector_dmas():
    found = []
    for name, count in VECTORS:
        n = 0
        while n < count:
            r = ROW[name] + n
            m = min(count - n, P - r % P)
            found.append((name, n, r, m))
            n += m
    return found


VECTOR_DMAS = len(vector_dmas())


def linear_plan():
    stages = [("m_q", 2, 8), ("m_k", 2, 8), ("m_v", 4, 8), ("m_o", 4, 8), ("m_out", 4, 8)]

    def ffn1(layer):
        for part, n in enumerate((8, 8, 6)):
            stages.append((f"f{layer}_up{part}", n, 8))
            stages.append((f"f{layer}_down{part}", 4, n))

    def ffn2(layer):
        for part in range(4):
            stages.append((f"s{layer}_up{part}", 4, 8))
            stages.append((f"s{layer}_down{part}", 4, 8))

    ffn1(0)
    stages.extend([("kv_k", 4, 8), ("kv_v", 4, 8), ("x_q", 4, 8), ("x_g", 4, 8), ("x_out", 4, 8)])
    ffn1(1)
    stages.extend([("c_k", 2, 8), ("c_v", 2, 8), ("n_u", 2, 8), ("n_g", 2, 8), ("n_q", 2, 8), ("n_k", 2, 8),
                   ("n_v", 2, 8), ("n_out", 4, 8)])
    ffn2(0)
    stages.extend([("p_1", 8, 8), ("p_2", 4, 8)])
    ffn2(1)
    plan, c, g = {}, 0, 0
    for name, n, k in stages:
        plan[name] = dict(name=name, groups=n, ktiles=k, chunk=c, group=g)
        c += 2 * n
        g += n
    return plan, c


FILLS = ["pre0", "mlstm", "ffn0", "kv", "pre1", "fox", "ffn1", "ctx", "even", "mix", "mlp0", "odd", "conf", "mlp1"]
FILL = {name: 8 * i for i, name in enumerate(FILLS)}
NORMS = ["pre0", "post0", "ffn0", "fpost0", "kv", "pre1", "post1", "ffn1", "fpost1", "ctx", "even", "mlp0",
         "odd", "conf", "mlp1", "final"]
NORM = {name: i for i, name in enumerate(NORMS)}
RESIDS = {"post0": 8, "fpost0": 16, "post1": 24, "fpost1": 32}
READY = {name: 8 * i for i, name in enumerate(f for f in FILLS if f not in ("fox", "mix", "conf"))}
HIDDEN = {"f0": 0, "f1": 22, "s0": 44, "s1": 60}


def build(nc, a, out, consts):
    plan, chunks = linear_plan()
    with ExitStack() as ctx:
        arena = ctx.enter_context(nc.sbuf_tensor("arena", [P, 212736 // 4], F32))
        origin = 16512

        def at(name, offset, shape, dt=F32):
            return nc.alloc_sbuf_tensor_at(name, shape, dt, offset=origin + offset)

        def sem(name):
            return ctx.enter_context(nc.semaphore(name))

        K = 1024
        X = at("X", 0, [P, DT, T])
        Y = at("Y", 16 * K, [P, DT, T])
        H_hi = at("H_hi", 32 * K, [P, DT, T], F32R)
        H_lo = at("H_lo", 48 * K, [P, DT, T], F32R)
        raw = at("raw", 64 * K, [P, SLOTS, KC * GC])
        w_hi = at("w_hi", 80 * K, [P, SLOTS, KC * GC], F32R)
        w_lo = at("w_lo", 96 * K, [P, SLOTS, KC * GC], F32R)
        hid_hi = at("hid_hi", 112 * K, [P, DT, T], F32R)
        hid_lo = at("hid_lo", 128 * K, [P, DT, T], F32R)
        mod_acc = at("mod_acc", 144 * K, [P, 6 * D])
        ctx_acc = at("ctx_acc", 168 * K, [P, 2 * D])
        mod_w = at("mod_w", 176 * K, [P, 2, 4, 256])
        VT = at("VT", 184 * K, [P, VBLOCKS * P])
        S = at("S", 188 * K, [P, 4, T])
        SQ = at("SQ", 196 * K, [P, 2, T])
        Dg = at("Dg", 200 * K, [P, TB, P])
        root = Dg[:].rearrange("p b n -> p (b n)")
        o = [202 * K]

        def small(name, shape, dt=F32):
            n = 4
            for s in shape[1:]:
                n *= s
            t = at(name, o[0], shape, dt)
            o[0] += -(-n // 32) * 32
            return t

        ident = small("ident", [P, P])
        mask_ts = small("mask_ts", [P, P])
        mask_st = small("mask_st", [P, P])
        ones = small("ones", [P, P])
        eps = small("eps", [P, 1])
        gates_T = small("gates_T", [P, 3, TB, 8])
        c_T = small("c_T", [P, TB, 16])
        stat = small("stat", [P, 8, 8])
        n1 = small("n1", [P, 8, 4])
        n2 = small("n2", [P, 8, 4])
        n3 = small("n3", [P, 8, 4])
        mx = small("mx", [P, 4, 4])
        rsum = small("rsum", [P, 4, 4])
        cs = small("cs", [P, 16])
        mods = [small(f"mod{layer}", [P, 48]) for layer in range(2)]
        cmod = small("cmod", [P, 16])
        gain1 = small("gain1", [P, 8])
        gain2 = small("gain2", [P, 8])
        cgain = small("cgain", [P, 8])
        gb = small("gb", [P, 8])
        bn = small("bn", [P, 16, 2])
        b_m = small("b_m", [8, 2])
        b_x = small("b_x", [16, 1])
        tok = small("tok", [P, 48])
        mod_t = small("mod_t", [P, 256])
        assert o[0] <= 212736, o[0]

        x_tm = at("x_tm", 16 * K, [P, TB, D])
        v_rows = at("v_rows", 112 * K, [P, VBLOCKS, P])
        gw_raw = at("gw_raw", 16 * K, [P, DT, P])
        gw_hi = at("gw_hi", 20 * K, [P, DT, P], F32R)
        gw_lo = at("gw_lo", 24 * K, [P, DT, P], F32R)
        mQ = at("mQ", 112 * K, [P, 4, T])
        mK = at("mK", 120 * K, [P, 4, T])
        mV = at("mV", 128 * K, [P, TB, D])
        xK = at("xK", 112 * K, [P, DT, T])
        xV = at("xV", 128 * K, [P, TB, D])
        xQ = at("xQ", 144 * K, [P, DT, T])
        att = at("att", 32 * K, [P, 8192])
        Kp = att[:, 0:768]
        Qp = att[:, 768:1280]
        Vp = att[:, 1280:2304]
        N0 = att[:, 2304:2816]
        N1 = att[:, 2816:3328]
        Lg = att[:, 3328:4864].rearrange("p (b n) -> p b n", b=2)
        PT = att[:, 4864:7936].rearrange("p (s n) -> p s n", s=6)
        rows = att[:, 0:8192].rearrange("p (j n) -> p j n", n=T)

        xPT0 = at("xPT0", 160 * K, [P, TB, T])
        xPT1 = at("xPT1", 168 * K, [P, TB, T])
        ctx_tm = at("ctx_tm", 16 * K, [P, 2, D])
        ct = at("ct", 24 * K, [P, DT, CTX])
        g_tm = at("g_tm", 24 * K, [P, TB, 512])
        nK = at("nK", 112 * K, [P, 4, T])
        nV = at("nV", 120 * K, [P, TB, 512])
        cK = at("cK", 128 * K, [P, 4, CTX])
        cV = at("cV", 132 * K, [P, 2, 512])
        nQ = at("nQ", 136 * K, [P, 4, T])
        tbias = at("tbias", 144 * K, [P, 8, 14, 64])
        tb_head = at("tb_head", 172 * K, [P, 14 * 64])
        nPT1 = at("nPT1", 188 * K, [P, 6, T])
        sel = at("sel", 32 * K, [64, 2, 16 * P])
        rp = at("rp", 48 * K, [120, 64])
        rm = at("rm", 49 * K, [64, 8, 14])
        yp = at("yp", 112 * K, [P, 2, T + 2 * PAD])
        tap_diag = at("tap_diag", 117 * K, [P, 2, PE_TAPS, P])

        G = ctx.enter_context(nc.psum_tensor("G", [P, 4, 512], F32))
        M = ctx.enter_context(nc.psum_tensor("M", [P, 4, 512], F32))

        raw_landed = [sem(f"raw_landed{i}") for i in range(SLOTS)]
        hi_done = sem("hi_done")
        lo_done = sem("lo_done")
        chunk_used = sem("chunk_used")
        freed_a = sem("freed_a")
        freed_d = sem("freed_d")
        h_ready = sem("h_ready")
        h_hi = sem("h_hi")
        h_lo = sem("h_lo")
        n_sq = sem("n_sq")
        n_ss = sem("n_ss")
        n_sd = sem("n_sd")
        n_row = sem("n_row")
        r_t = sem("r_t")
        x_ready = sem("x_ready")
        x_dma = sem("x_dma")
        v_dma = sem("v_dma")
        c_dma = sem("c_dma")
        cs_ready = sem("cs_ready")
        pool_c = sem("pool_c")
        mod_landed = [sem(f"mod_landed{i}") for i in range(2)]
        mod_done = sem("mod_done")
        mod_s = sem("mod_s")
        mod_ok = sem("mod_ok")
        aux_free = sem("aux_free")
        chain_d = sem("chain_d")
        sel_dma = [sem(f"sel_dma{i}") for i in range(2)]
        setup_p = sem("setup_p")
        setup_t = sem("setup_t")
        setup_c = sem("setup_c")
        g_dma = sem("g_dma")
        g_zero = sem("g_zero")
        g_hi = sem("g_hi")
        g_lo = sem("g_lo")
        g_mm = sem("g_mm")
        f_a = sem("f_a")
        f_d = sem("f_d")
        f_g = sem("f_g")
        f_m = sem("f_m")
        hid_h = sem("hid_h")
        hid_l = sem("hid_l")
        row_a = sem("row_a")
        row_d = sem("row_d")
        row_t = sem("row_t")
        row_c = sem("row_c")
        ml = {k: sem(f"ml_{k}") for k in ("stg", "dg", "bc", "n0", "n1", "s", "e", "p", "num", "sq", "ss", "st",
                                          "y", "nar")}
        fx = {k: sem(f"fx_{k}") for k in ("stg", "dg", "bc", "n0", "s", "m", "e", "p", "t", "pt", "o", "y", "stv")}
        na = {k: sem(f"na_{k}") for k in ("stg", "stv", "s", "m", "e", "p", "t", "pt", "o", "y")}
        (rp_dma, tb_t, tb_r, tb_b, tb_mm, tb_e, ctx_dma, ct_t, ct_c, wsp_dma, sg_t, sg_w, sg_dg, sg_bc, sg_b, sg_v,
         sg_r, sg_n, sg_m, glu_a, cv_d, cv_s, cv_m, cv_t, cv_y, cv_w, cv_pe, cv_v, fin_t, fin_m, fin_c) = [
            sem(k) for k in ("rp_dma tb_t tb_r tb_b tb_mm tb_e ctx_dma ct_t ct_c wsp_dma sg_t sg_w sg_dg sg_bc sg_b "
                             "sg_v sg_r sg_n sg_m glu_a cv_d cv_s cv_m cv_t cv_y cv_w cv_pe cv_v fin_t fin_m "
                             "fin_c").split()]
        TOKENS = [(freed_a, 2), (freed_d, 2), (hid_l, 1), (tb_mm, 2), (tb_e, 4), (cv_pe, 2), (cv_d, 2), (ml["p"], 4)]
        TOKENS += [(ml[k], 1) for k in ("n0", "n1", "bc", "y", "sq", "st", "ss", "num", "e")]
        TOKENS += [(fx[k], 1) for k in ("n0", "bc")]
        for d in (fx, na):
            TOKENS += [(d["t"], 4), (d["m"], 4), (d["pt"], 2), (d["e"], 2), (d["o"], 2), (d["y"], 1)]
        done = sem("done")

        block = ctx.enter_context(nc.Block())
        vt = lambda name, t: VT[:, ROW[name] + t:ROW[name] + t + 1]

        by = {}
        read_a = read_d = 0
        for name, st in plan.items():
            kind = "A"
            if "down" in name and (name[0] == "s" or not name.endswith("down0")):
                kind = "D"
            if name[0] == "f" and "up" in name or name in ("n_out", "p_1", "p_2"):
                kind = "D"
            st["by"] = kind
            st["freed"] = read_a if kind == "A" else read_d
            if kind == "A":
                read_a += st["groups"]
            else:
                read_d += st["groups"]
            st["totals"] = (read_a, read_d)
        order = list(plan)
        for prev, name in zip([None] + order, order):
            plan[name]["before"] = plan[prev]["totals"] if prev else (0, 0)
        used_after = lambda name: 4 + 2 * (plan[name]["group"] + plan[name]["groups"])

        ident4 = ident[:].unsqueeze(1).to_broadcast([P, TB, P])

        def h_ready_wait(eng, name, t):
            eng.wait_ge(h_ready, READY[name] + t + 1)

        def fill_act(act, name, ready, shift, after, n=T):
            if after:
                act.wait_ge(chunk_used, after)
            for t in range(DT):
                h_ready_wait(act, name, t)
                if shift:
                    ins = act.activation(H_hi[:, t, 0:n], S[:, t % 4, 0:n], ACT.Identity, bias=shift(t))
                else:
                    ins = act.activation(H_hi[:, t, 0:n], S[:, t % 4, 0:n], ACT.Copy)
                ins.then_inc(h_hi, 1)

        def fill_dve(dve, name, produce, shift, after, n=T):
            def low(t):
                dve.wait_ge(h_hi, FILL[name] + t + 1)
                if shift:
                    ins = dve.scalar_tensor_tensor(H_lo[:, t, 0:n], S[:, t % 4, 0:n], shift(t), H_hi[:, t, 0:n],
                                                   ALU.add, ALU.subtract)
                else:
                    ins = dve.tensor_tensor(H_lo[:, t, 0:n], S[:, t % 4, 0:n], H_hi[:, t, 0:n], ALU.subtract)
                ins.then_inc(h_lo, 1)

            if after:
                dve.wait_ge(chunk_used, after)
            for t in range(DT):
                if FILL[name] + t - 3 > 0:
                    dve.wait_ge(h_lo, FILL[name] + t - 3)
                produce(t, S[:, t % 4, 0:n]).then_inc(h_ready, 1)
                if t:
                    low(t - 1)
            low(7)

        def split_act(act, name, ready, src):
            for t in range(DT):
                ready(t)
                act.activation(H_hi[:, t, :], src[:, t, :], ACT.Copy).then_inc(h_hi, 1)

        def split_dve(dve, name, src):
            for t in range(DT):
                dve.wait_ge(h_hi, FILL[name] + t + 1)
                dve.tensor_tensor(H_lo[:, t, :], src[:, t, :], H_hi[:, t, :], ALU.subtract).then_inc(h_lo, 1)

        def squares_act(act, name, src, stage):
            st = plan[stage]
            written = freed_a if st["by"] == "A" else freed_d
            first = 8 * NORM[name]

            def evacuate(i, p, g):
                act.wait_ge(written, g + (2 + st["freed"] + 1))
                for m in range(2):
                    if first + m - 1 > 0:
                        act.wait_ge(n_ss, g * 2 + (first + m - 1))
                        act.activation(tok[:, 44 + m:45 + m], eps[:, 0:1], ACT.Copy)
                    act.activation(SQ[:, m:m + 1, :], src[:, ds(g * 2 + m, 1), :], ACT.Square).then_inc(n_sq, 1)
            return evacuate

        def norm_act(act, name, src, ready, blocks=TB):
            i, n = NORM[name], blocks * P
            for t in range(DT if src is not None else 0):
                ready(t)
                if 8 * i + t - 1 > 0:
                    act.wait_ge(n_ss, 8 * i + t - 1)
                act.activation(SQ[:, t % 2, 0:n], src[:, t, 0:n], ACT.Square).then_inc(n_sq, 1)
            act.wait_ge(n_ss, 8 * i + 8)
            act.activation(root[:, 0:n], M[:, 0, 0:n], ACT.Ln, bias=eps[:, 0:1], scale=1.0 / D).then_inc(n_sd, 1)
            act.wait_ge(n_sd, i + 1)
            act.activation(root[:, 0:n], root[:, 0:n], ACT.Exp, scale=-0.5).then_inc(n_row, 1)

        def norm_dve(dve, name, blocks=TB):
            dve.wait_ge(n_row, NORM[name] + 1)
            return root[:, 0:blocks * P]

        def pre_dve(dve, name, src, gain, shift, after, blocks=TB):
            row = norm_dve(dve, name, blocks)
            n = blocks * P
            fill_dve(dve, name, lambda t, dst: dve.scalar_tensor_tensor(dst, src[:, t, 0:n], gain(t), row, ALU.mult,
                                                                        ALU.mult), shift, after, n)

        def residual_dve(dve, name, gain):
            row = norm_dve(dve, name)
            b = RESIDS[name]
            def add(t):
                dve.wait_ge(r_t, b - 8 + t + 1)
                dve.tensor_tensor(X[:, t, :], X[:, t, :], S[:, t % 4, :], ALU.add).then_inc(x_ready, 1)

            for t in range(DT):
                if t >= 4:
                    dve.wait_ge(x_ready, b + t - 3)
                dve.scalar_tensor_tensor(S[:, t % 4, :], Y[:, t, :], gain(t), row, ALU.mult, ALU.mult).then_inc(r_t, 1)
                if t:
                    add(t - 1)
            add(7)

        def split_hi(act, chunk, i, j):
            act.wait_ge(raw_landed[j], i * 32 + 32 * (chunk // 4 + 1))
            act.wait_ge(chunk_used, i * 4 + (chunk + j + 1))
            act.activation(w_hi[:, j, :], raw[:, j, :], ACT.Copy).then_inc(hi_done, 1)

        def split_lo(dve, chunk, i, j):
            dve.wait_ge(hi_done, i * 4 + (chunk + j + 1))
            dve.tensor_tensor(w_lo[:, j, :], raw[:, j, :], w_hi[:, j, :], ALU.subtract).then_inc(lo_done, 1)

        def groups(eng, name, split, evacuate, peel=False):
            st = plan[name]

            def body(i, more):
                for p in range(2):
                    if more:
                        split(eng, st["chunk"] + 4, i, 2 * p)
                        split(eng, st["chunk"] + 4, i, 2 * p + 1)
                    if evacuate:
                        eng.wait_ge(chunk_used, i * 4 + (2 * st["group"] + 2 * p + 6))
                        evacuate(i, p, i * 2 + p)

            n = st["groups"] // 2
            if name == order[-1]:
                for i in range(n):
                    body(i, i < n - 1)
            elif peel:
                body(0, True)
                with eng.Fori(0, n - 1) as i:
                    body(i + 1, True)
            else:
                with eng.Fori(0, n) as i:
                    body(i, True)

        def two(tile, g):
            return tile[:, ds(g * 2, 2), :]

        def gate_weights_act(act, n):
            act.wait_ge(g_dma, 32 if n == 0 else 48)
            act.activation(gw_hi[:], gw_raw[:], ACT.Copy).then_inc(g_hi, 1)

        def gate_weights_dve(dve, n):
            dve.wait_ge(g_hi, n + 1)
            dve.tensor_tensor(gw_lo[:], gw_raw[:], gw_hi[:], ALU.subtract).then_inc(g_lo, 1)

        def ffn1_act(act, layer):
            base = HIDDEN[f"f{layer}"]
            cw = ROW["ffn_conv_w"] + 132 * layer
            cb = ROW["ffn_conv_b"] + 44 * layer
            for part in range(3):
                def up(i, p, g):
                    u = g + (base + 8 * part)
                    act.wait_ge(hid_l, g + (base + 8 * part) + 1)
                    for h in range(2):
                        t = g + (8 * part + 22 * h)
                        act.activation(S[:, h, :], G[:, 2 * p + h, :], ACT.Identity, bias=VT[:, ds(t + cb, 1)],
                                       scale=VT[:, ds(t + (cw + 88), 1)]).then_inc(f_a, 1)
                    act.wait_ge(f_d, u * 3 + 2)
                    act.activation(S[:, 2, :], S[:, 0, :], ACT.Gelu_apprx_tanh).then_inc(f_g, 1)
                    act.wait_ge(f_m, u + 1)
                    act.activation(hid_hi[:, ds(g, 1), :], S[:, 3:4, :], ACT.Copy).then_inc(hid_h, 1)

                groups(act, f"f{layer}_up{part}", split_hi, up)

                def down(i, p, g):
                    act.activation(two(Y, g), G[:, 2 * p:2 * p + 2, :], ACT.Copy).then_inc(freed_a, 1)

                groups(act, f"f{layer}_down{part}", split_hi,
                       (down, None, squares_act(act, f"fpost{layer}", Y, f"f{layer}_down2"))[part])

        def ffn1_dve(dve, link, layer):
            base = HIDDEN[f"f{layer}"]
            cw = ROW["ffn_conv_w"] + 132 * layer
            for part in range(3):
                freed = plan[f"f{layer}_up{part}"]["freed"]

                def up(i, p, g):
                    u = g + (base + 8 * part)

                    def tap(h, j):
                        w = VT[:, ds(g + (8 * part + 22 * h + cw + 44 * j), 1)]
                        k = 2 - j
                        return dve.scalar_tensor_tensor(S[:, h, k:T], G[:, 2 * p + h, 0:T - k], w, S[:, h, k:T],
                                                        ALU.mult, ALU.add)

                    dve.wait_ge(f_a, u * 2 + 1)
                    tap(0, 1).then_inc(f_d, 1)
                    dve.wait_ge(f_d, u * 3 + 1)
                    tap(0, 0).then_inc(f_d, 1)
                    dve.wait_ge(f_a, u * 2 + 2)
                    tap(1, 1).then_inc(f_d, 1)
                    dve.wait_ge(f_d, u * 3 + 3)
                    tap(1, 0).then_inc(freed_d, 1)
                    dve.wait_ge(freed_d, g + (2 + freed + 1))
                    dve.wait_ge(f_g, u + 1)
                    dve.tensor_tensor(S[:, 3, :], S[:, 1, :], S[:, 2, :], ALU.mult).then_inc(f_m, 1)
                    dve.wait_ge(hid_h, u + 1)
                    dve.tensor_tensor(hid_lo[:, ds(g, 1), :], S[:, 3:4, :], hid_hi[:, ds(g, 1), :],
                                      ALU.subtract).then_inc(hid_l, 1)

                groups(dve, f"f{layer}_up{part}", split_lo, up)

                def down(i, p, g):
                    y = two(Y, g)
                    dve.tensor_tensor(y, G[:, 2 * p:2 * p + 2, :], y, ALU.add).then_inc(freed_d, 1)

                if layer == 0 and part == 2:
                    mod_dve(dve, link, 0)
                if part:
                    dve.wait_ge(freed_a, 2 + plan[f"f{layer}_down0"]["totals"][0])
                    if part == 2:
                        dve.wait_ge(freed_d, 2 + plan[f"f{layer}_down1"]["totals"][1])
                groups(dve, f"f{layer}_down{part}", split_lo, down if part else None)

        w_mod, MCH = a["w_mod_2"], 256

        def pool_mod(pool):
            pool.wait_ge(cs_ready, 1)
            pool.tensor_tensor(cs[:], cs[:], VT[:, ROW["c_2"]:ROW["c_2"] + 16], ALU.mult).then_inc(pool_c, 1)
            pool.wait_ge(pool_c, 1)
            n = [1]
            lands = [0]

            def load(layer, half, first, g):
                src = w_mod[layer].rearrange("(k p) n -> p k n", p=P)[:, 4 * half:4 * half + 4,
                                                                      ds(g * MCH + first, MCH)]
                pool.dma_start(mod_w[:, half], src).then_inc(mod_landed[half], 16)

            def run(layer, vec, count, acc):
                for half in range(2):
                    load(layer, half, 0, 0)

                def body(i, more):
                    def step(ins, k):
                        ins.then_inc(pool_c, 1)
                        pool.wait_ge(pool_c, i * 7 + (n[0] + k))

                    for half in range(2):
                        w = mod_w[:, half]
                        pool.wait_ge(mod_landed[half], i * 16 + 16 * (lands[0] + 1))
                        col = cs[:, 8 * vec + 4 * half:8 * vec + 4 * half + 4].unsqueeze(2).to_broadcast([P, 4, MCH])
                        step(pool.tensor_tensor(w, w, col, ALU.mult), 3 * half + 1)
                        step(pool.tensor_tensor(w[:, 0:2], w[:, 0:2], w[:, 2:4], ALU.add), 3 * half + 2)
                        dst = mod_t[:] if half == 0 else w[:, 0]
                        step(pool.tensor_tensor(dst, w[:, 0], w[:, 1], ALU.add), 3 * half + 3)
                        if more and half == 0:
                            load(layer, 0, MCH, i)
                    step(pool.tensor_tensor(acc[:, ds(i * MCH, MCH)], mod_t[:], mod_w[:, 1, 0], ALU.add), 7)
                    if more:
                        load(layer, 1, MCH, i)

                with pool.Fori(0, count - 1) as i:
                    body(i, True)
                body(count - 1, False)
                n[0] += 7 * count
                lands[0] += count

            run(0, 0, 24, mod_acc)
            run(0, 1, 8, ctx_acc)
            pool.memset(tok[:, 0:1], 0.0).then_inc(mod_done, 1)
            pool.wait_ge(chunk_used, used_after("f1_up2"))
            pool.memset(rp[:], NEG).then_inc(setup_p, 1)
            pool.wait_ge(setup_p, 3)
            for c in (0, 32):
                pool.dma_start(rp[:, c:c + 31], a["rpb_2"].rearrange("a h r c -> (a h r) c")).then_inc(rp_dma, 16)
            for q in range(4):
                pool.wait_ge(tb_mm, q + 1)
                pool.dma_start(sel[:, q % 2, :], consts["sel"][:, q * 16 * P:(q + 1) * 16 * P]
                               ).then_inc(sel_dma[q % 2], 16)
            pool.wait_ge(x_ready, RESIDS["fpost1"] + 8)
            pool.dma_start(ctx_tm[:], a["ctx_2"].rearrange("a (b p) d -> p (a b) d", p=P)).then_inc(ctx_dma, 16)
            pool.wait_ge(h_lo, FILL["even"] + 8)
            pool.dma_start(S[:, 0, :].rearrange("p (g q) -> p g q", g=4),
                           a["w_sp_2"][0].rearrange("g p q -> p g q")).then_inc(wsp_dma, 16)
            pool.wait_ge(aux_free, 1)
            run(1, 0, 24, mod_acc)
            pool.memset(tok[:, 1:2], 0.0).then_inc(mod_done, 1)

        def mod_pe(pe, layer):
            pe.wait_ge(mod_done, layer + 1)
            for j in range(48):
                mm = pe.matmul(M[:, 3, j:j + 1], mod_acc[:, j * P:j * P + P], ones[:, 0:1], start=(j == 0),
                               stop=False, skip_group_check=True)
            for j in range(16 if layer == 0 else 0):
                mm = pe.matmul(M[:, 3, 48 + j:49 + j], ctx_acc[:, j * P:j * P + P], ones[:, 0:1], start=False,
                               stop=True, skip_group_check=True)
            mm.then_inc(mod_s, 1)

        def mod_dve(dve, link, layer):
            dve.wait_ge(mod_s, layer + 1)
            mod = mods[layer]
            b = ROW["b_mod_2"] + 48 * layer
            gr = ROW["norm_g_2"] + 16 * layer
            if layer == 0:
                link(dve.tensor_tensor(cmod[:], M[:, 3, 48:64], VT[:, b:b + 16], ALU.add))
                link(dve.scalar_tensor_tensor(cgain[:], cmod[:, 8:16], 1.0, VT[:, gr:gr + 8], ALU.add, ALU.mult))
            link(dve.tensor_tensor(mod[:], M[:, 3, 0:48], VT[:, b:b + 48], ALU.add))
            link(dve.scalar_tensor_tensor(gain1[:], mod[:, 8:16], 1.0, VT[:, gr:gr + 8], ALU.add, ALU.mult))
            link(dve.scalar_tensor_tensor(gain2[:], mod[:, 32:40], 1.0, VT[:, gr + 8:gr + 16], ALU.add, ALU.mult))
            if layer == 1:
                link(dve.tensor_tensor(gb[:], mod[:, 16:24], VT[:, ROW["b_pw2_2"]:ROW["b_pw2_2"] + 8], ALU.mult))
            dve.memset(tok[:, 2 + layer:3 + layer], 0.0).then_inc(mod_ok, 1)

        HP = 64

        def mlstm_pe(pe, spread):
            pe.wait_ge(row_c, 2)
            for q, r in enumerate((5, 6, 10)):
                for b in range(TB):
                    mm = pe.transpose(M[:, 3, (q * TB + b) * 8:(q * TB + b) * 8 + 8], rows[0:8, r, b * P:b * P + P],
                                      ident[0:8, 0:8])
            mm.then_inc(row_t, 1)
            pe.wait_ge(freed_a, 2 + plan["m_o"]["totals"][0])
            with pe.Fori(0, 4) as i:
                for e in range(2):
                    h = i * 2 + e
                    hs = slice(HP * e, HP * e + HP)
                    pe.wait_ge(ml["n0"], h + 1)
                    pe.wait_ge(ml["n1"], h + 1)
                    pe.wait_ge(ml["dg"], h + 1)
                    pe.matmul(M[:, 1, :], ones[:], Dg[:].rearrange("p b n -> p (b n)"), start=True,
                              stop=True).then_inc(ml["bc"], 1)
                    if e == 0:
                        pe.wait_ge(ml["stg"], i + 1)
                    for s in range(TB):
                        pe.wait_ge(ml["p"], h * 4 + (s + 1))
                        pe.matmul(G[:, s, 0:T - s * P], Kp[hs, s * P:s * P + P], Qp[hs, s * P:T], start=True,
                                  stop=True).then_inc(ml["s"], 1)
                    pe.wait_ge(ml["y"], h + 1)
                    pe.wait_ge(ml["sq"], h + 1)
                    for s in range(TB):
                        pe.wait_ge(ml["p"], h * 4 + (s + 5))
                        mm = pe.matmul(M[:, 2, s * P:T], Vp[:, 256 * s + P * e:256 * s + P * e + P],
                                       PT[:, s, s * P:T], start=(s == 0), stop=(s == 3), skip_group_check=True)
                    mm.then_inc(ml["num"], 1)
                    pe.wait_ge(ml["st"], h + 1)
                    for b in range(TB):
                        for s in range(b + 1):
                            pe.matmul(M[:, 3, b:b + 1], PT[:, s, b * P:b * P + P], ones[:, 0:1],
                                      start=(b == 0 and s == 0), stop=False, skip_group_check=True)
                    pe.wait_ge(ml["sq"], h + 2)
                    for b in range(TB):
                        mm = pe.matmul(M[:, 3, 4 + b:5 + b], SQ[:, 0, b * P:b * P + P], ones[:, 0:1], start=False,
                                       stop=(b == 3), skip_group_check=True)
                    mm.then_inc(ml["ss"], 1)
            for t in range(DT):
                spread(ml["dg"], 8 + t + 1, ml["bc"])

        def mlstm_act(act):
            act.wait_ge(g_mm, 1)
            act.wait_ge(chunk_used, used_after("m_o"))
            act.wait_ge(h_lo, FILL["pre0"] + 8)
            act.activation(rows[0:8, 0, :], M[0:8, 2, :], ACT.Identity, bias=b_m[:, 0:1]).then_inc(row_a, 1)
            act.activation(rows[0:8, 1, :], M[32:40, 2, :], ACT.Copy).then_inc(row_a, 1)
            act.wait_ge(row_d, 1)
            act.activation(rows[0:8, 2, :], rows[0:8, 2, :], ACT.Exp).then_inc(row_a, 1)
            act.wait_ge(row_a, 3)
            act.activation(rows[0:8, 9, :], rows[0:8, 2, :], ACT.Ln, bias=1.0).then_inc(row_a, 1)
            act.wait_ge(row_c, 1)
            act.activation(rows[0:8, 10, :], rows[0:8, 7, :], ACT.Exp, scale=-1.0).then_inc(row_c, 1)
            with act.Fori(0, 4) as i:
                for e in range(2):
                    h = i * 2 + e
                    act.wait_ge(ml["e"], h * 4 + 1)
                    act.wait_ge(ml["bc"], h + 2)
                    act.activation(N0, M[:, 1, :], ACT.Copy, scale=-1.0).then_inc(ml["n0"], 1)
                    act.wait_ge(ml["n0"], h + 2)
                    act.wait_ge(ml["n1"], h + 2)
                    for s in range(TB):
                        act.wait_ge(ml["p"], h * 4 + (s + 3))
                        bias = gates_T[:, 0, s, ds(h, 1)]
                        one = act.activation(Lg[:, s % 2, 0:P], N1[:, s * P:s * P + P], ACT.Exp, bias=bias)
                        if s < 3:
                            one = act.activation(Lg[:, s % 2, P:T - s * P], N0[:, (s + 1) * P:T], ACT.Exp, bias=bias)
                        one.then_inc(ml["e"], 1)
                    act.wait_ge(ml["ss"], h + 1)
                    act.wait_ge(ml["num"], h + 2)
                    act.activation(SQ[:, 0, :], M[:, 2, :], ACT.Square).then_inc(ml["sq"], 1)
            act.wait_ge(ml["nar"], 1)
            act.activation(n3[:], n3[:], ACT.Sqrt, bias=eps[:], scale=1.0 / P).then_inc(ml["nar"], 1)
            fill_act(act, "mlstm", None, None, None)

        def mlstm_dve(dve, link):
            dve.wait_ge(chunk_used, used_after("m_o"))
            link(dve.memset(rows[0:8, 8, :], 1.0))
            dve.wait_ge(row_a, 2)
            link(dve.tensor_scalar(rows[0:8, 1, :], rows[0:8, 1, :], b_m[:, 1:2], None, ALU.add))
            dve.scalar_tensor_tensor(rows[0:8, 2, :], rows[0:8, 1, :], -1.0, rows[0:8, 1, :], ALU.mult,
                                     ALU.min).then_inc(row_d, 1)
            dve.wait_ge(row_a, 4)
            link(dve.scalar_tensor_tensor(rows[0:8, 3, :], rows[0:8, 1, :], 0.0, rows[0:8, 9, :], ALU.min,
                                          ALU.subtract))
            link(dve.tensor_tensor_scan(rows[0:8, 4, :], rows[0:8, 8, :], rows[0:8, 3, :], 0.0, ALU.mult, ALU.add))
            link(dve.tensor_tensor(rows[0:8, 5, :], rows[0:8, 0, :], rows[0:8, 4, :], ALU.subtract))
            link(dve.tensor_tensor_scan(rows[0:8, 6, :], rows[0:8, 8, :], rows[0:8, 5, :], 0.0, ALU.mult, ALU.max))
            dve.tensor_tensor(rows[0:8, 7, :], rows[0:8, 4, :], rows[0:8, 6, :], ALU.add).then_inc(row_c, 1)
            dve.wait_ge(row_t, 1)
            link(dve.tensor_copy(gates_T[:].rearrange("p q b h -> p (q b h)"), M[:, 3, 0:96]))
            dve.wait_ge(freed_a, 2 + plan["m_o"]["totals"][0])
            with dve.Fori(0, 4) as i:
                dve.wait_ge(ml["num"], i * 2 + 1)
                dve.tensor_copy(Kp[:, 0:T], mK[:, ds(i, 1), :].rearrange("p a n -> p (a n)"))
                dve.tensor_copy(Qp[:, 0:T], mQ[:, ds(i, 1), :].rearrange("p a n -> p (a n)"))
                dve.tensor_copy(Vp.rearrange("p (b n) -> p b n", b=4),
                                mV[:, :, ds(i * 256, 256)]).then_inc(ml["stg"], 1)
                for e in range(2):
                    h = i * 2 + e
                    dve.wait_ge(ml["bc"], h + 1)
                    dve.tensor_tensor(Dg[:], ident4, gates_T[:, 1, :, ds(h, 1)].to_broadcast([P, TB, P]),
                                      ALU.mult).then_inc(ml["dg"], 1)
                    dve.wait_ge(ml["e"], h * 4 + 1)
                    dve.wait_ge(ml["n0"], h + 2)
                    dve.tensor_tensor(N1.rearrange("p (b n) -> p b n", b=4),
                                      mask_st[:].unsqueeze(1).to_broadcast([P, TB, P]),
                                      N0.rearrange("p (b n) -> p b n", b=4), ALU.add).then_inc(ml["n1"], 1)
                    dve.wait_ge(ml["ss"], h + 1)
                    for s in range(TB):
                        dve.wait_ge(ml["s"], h * 4 + (s + 1))
                        dve.wait_ge(ml["e"], h * 4 + (s + 2))
                        dve.tensor_tensor(PT[:, s, s * P:T], G[:, s, 0:T - s * P], Lg[:, s % 2, 0:T - s * P],
                                          ALU.mult).then_inc(ml["p"], 1)
                    dve.wait_ge(ml["sq"], h + 2)
                    yv = Y[:, ds(h, 1), :].rearrange("p a n -> p (a n)")
                    dve.tensor_tensor(yv, M[:, 2, :], yv, ALU.mult).then_inc(ml["y"], 1)
                    dve.wait_ge(ml["ss"], h + 2)
                    dve.tensor_copy(stat[:, ds(h, 1), :].rearrange("p a n -> p (a n)"),
                                    M[:, 3, 0:8]).then_inc(ml["st"], 1)
            dve.wait_ge(ml["st"], 9)
            den, ssq = stat[:, :, 0:4], stat[:, :, 4:8]
            link(dve.scalar_tensor_tensor(n1[:], den, -1.0, den, ALU.mult, ALU.max))
            link(dve.tensor_tensor(n1[:], n1[:], gates_T[:, 2, :, :].rearrange("p b h -> p h b"), ALU.max))
            link(dve.reciprocal(n2[:], n1[:]))
            link(dve.tensor_tensor(n3[:], n2[:], n2[:], ALU.mult))
            dve.tensor_tensor(n3[:], n3[:], ssq, ALU.mult).then_inc(ml["nar"], 1)
            dve.wait_ge(ml["nar"], 2)
            link(dve.reciprocal(n1[:], n3[:]))
            link(dve.tensor_tensor(n2[:], n2[:], n1[:], ALU.mult))

            def produce(t, dst):
                dve.wait_ge(ml["bc"], 8 + t + 1)
                dve.tensor_tensor(Dg[:], ident4, n2[:, t, :].unsqueeze(2).to_broadcast([P, TB, P]),
                                  ALU.mult).then_inc(ml["dg"], 1)
                dve.wait_ge(ml["bc"], 8 + t + 2)
                return dve.scalar_tensor_tensor(dst, Y[:, t, :], vt("mlstm_norm", t), M[:, 1, :], ALU.mult, ALU.mult)

            dve.wait_ge(ml["y"], 9)
            fill_dve(dve, "mlstm", produce, None, None)

        fox = dict(d=fx, pairs=8, Kp=att[:, 0:512], Qp=att[:, 512:1024],
                   Vp=att[:, 1024:1536], N0=att[:, 1536:2560].rearrange("p (e n) -> p e n", e=2),
                   N1=att[:, 2560:3584].rearrange("p (e n) -> p e n", e=2),
                   Lg=att[:, 3584:5632].rearrange("p (q n) -> p q n", q=4), PT=(xPT0, xPT1))
        near = dict(d=na, pairs=4, Kp=att[:, 0:768], Qp=att[:, 768:1280], Vp=att[:, 1280:2048],
                    Lg=att[:, 2048:5120].rearrange("p (q n) -> p q n", q=4),
                    PT=(att[:, 5120:8192].rearrange("p (s n) -> p s n", s=6), nPT1))

        def skewed(pairs, loop, body, tail):
            body(0, True, False)
            with loop(0, pairs - 2) as i:
                body(i + 1, False, False)
            body(pairs - 1, False, True)
            tail()

        def soft_pe(pe, c):
            d, ctx_keys = c["d"], c is near

            def scores(h, e, b):
                hs = slice(HP * e, HP * e + HP)
                if ctx_keys:
                    pe.wait_ge(d["e"], h * 4 + (b + 1))
                    q = 2 * (b % 2)
                    pe.matmul(G[:, q, :], c["Qp"][hs, b * P:b * P + P], c["Kp"][hs, 0:T], start=True, stop=True)
                    one = pe.matmul(G[:, q + 1, 0:CTX], c["Qp"][hs, b * P:b * P + P], c["Kp"][hs, T:T + CTX],
                                    start=True, stop=True)
                else:
                    pe.wait_ge(d["m"], h * 4 + (b + 1))
                    one = pe.matmul(G[:, b, 0:(b + 1) * P], c["Qp"][hs, b * P:b * P + P],
                                    c["Kp"][hs, 0:(b + 1) * P], start=True, stop=True)
                one.then_inc(d["s"], 1)

            def turn(h, b):
                pe.wait_ge(d["pt"], h * 4 + (b + (2 if ctx_keys else 1)))
                pe.wait_ge(d["p"], h * 4 + (b + 1))
                for s in range(6 if ctx_keys else b + 1):
                    bank = 2 + s // 4 if ctx_keys else 2 + b % 2
                    mm = pe.transpose(M[:, bank, (s % 4) * P:(s % 4) * P + P], c["Lg"][:, b, s * P:s * P + P],
                                      ident[:])
                mm.then_inc(d["t"], 1)

            def values(h, e):
                pe.wait_ge(d["pt"], h * 4 + 6)
                pe.wait_ge(d["y"], h + 1)
                n = 6 if ctx_keys else TB
                for s in range(n):
                    t0 = 0 if ctx_keys else s * P
                    mm = pe.matmul(M[0:HP, 0, t0:T], c["Vp"][:, P * s + HP * e:P * s + HP * e + HP],
                                   c["PT"][e][:, s, t0:T], start=(s == 0), stop=(s == n - 1),
                                   skip_group_check=True)
                mm.then_inc(d["o"], 1)

            def row(h):
                pe.wait_ge(d["n0"], h + 1)
                pe.wait_ge(d["dg"], h + 1)
                pe.matmul(M[:, 1, :], ones[:], Dg[:].rearrange("p b n -> p (b n)"), start=True,
                          stop=True).then_inc(d["bc"], 1)

            def body(i, first, last):
                if first:
                    pe.wait_ge(d["stg"], 1)
                    scores(0, 0, 0)
                for e in range(2):
                    h = i * 2 + e
                    for b in range(TB):
                        if b < 3:
                            scores(h, e, b + 1)
                        elif e == 0:
                            scores(h + 1, 1, 0)
                        elif not last:
                            pe.wait_ge(d["stg"], i + 2)
                            scores(h + 1, 0, 0)
                        if b == 2 and not ctx_keys and not (last and e == 1):
                            row(h + 1)
                        if b == 3:
                            turn(h, 0)
                        elif not (first and e == 0):
                            turn(h + (-1), b + 1)
                        if b == 3 and not (first and e == 0):
                            if e == 1:
                                pe.wait_ge(d["stv"], i + 1)
                            values(h + (-1), 1 - e)

            def tail():
                h = 2 * c["pairs"] - 1
                for b in range(1, TB):
                    turn(h, b)
                values(h, 1)

            if not ctx_keys:
                row(0)
            skewed(c["pairs"], pe.Fori, body, tail)

        def soft_act(act, c):
            d, ctx_keys = c["d"], c is near

            def exps(h, b):
                act.wait_ge(d["m"], h * 4 + (b + 5))
                lg = c["Lg"]
                if ctx_keys:
                    act.activation(lg[:, b, 0:T], lg[:, b, 0:T], ACT.Exp, bias=mx[:, b, 1:2], scale=-1.0,
                                   accum_out=rsum[:, b, 0:1])
                    one = act.activation(lg[:, b, T:T + CTX], G[:, 2 * (b % 2) + 1, 0:CTX], ACT.Exp,
                                         bias=mx[:, b, 1:2], accum_out=rsum[:, b, 1:2])
                else:
                    one = act.activation(lg[:, b, 0:(b + 1) * P], lg[:, b, 0:(b + 1) * P], ACT.Exp,
                                         bias=mx[:, b, 1:2], scale=-1.0, accum_out=rsum[:, b, 0:1])
                one.then_inc(d["e"], 1)

            def turned(h, e, b):
                if b == 0:
                    act.wait_ge(d["o"], h + 1)
                act.wait_ge(d["t"], h * 4 + (b + 5))
                n = 6 if ctx_keys else b + 1
                src = (M[:, 2:4, :].rearrange("p a n -> p (a n)") if ctx_keys else M[:, 2 + b % 2, :])
                act.activation(c["PT"][e][:, 0:n, b * P:b * P + P],
                               src[:, 0:n * P].rearrange("p (s n) -> p s n", n=P), ACT.Copy).then_inc(d["pt"], 1)

            def row(h, e):
                act.wait_ge(d["bc"], h + 2)
                act.activation(c["N0"][:, e, :], M[:, 1, :], ACT.Copy).then_inc(d["n0"], 1)

            def body(i, first, last):
                for e in range(2):
                    h = i * 2 + e
                    for b in range(TB):
                        exps(h, b)
                        if b == 3:
                            turned(h, e, 0)
                        elif not (first and e == 0):
                            turned(h + (-1), 1 - e, b + 1)
                        if b == 2 and not ctx_keys and not (last and e == 1):
                            row(h + 1, 1 - e)

            def tail():
                for b in range(1, TB):
                    turned(2 * c["pairs"] - 1, 1, b)

            if not ctx_keys:
                row(0, 0)
            skewed(c["pairs"], act.Fori, body, tail)

        def soft_dve(dve, link, c, keys_queries, values_in, out_tile, first_tile):
            d, ctx_keys = c["d"], c is near
            lg = c["Lg"]

            def logits(h, e, b):
                dve.wait_ge(d["s"], h * 4 + (b + 1))
                dve.wait_ge(d["t"], h * 4 + (b + 1))
                dve.memset(tok[:, 32 + b:33 + b], 0.0)
                if ctx_keys:
                    dve.tensor_tensor_reduce(lg[:, b, 0:T], G[:, 2 * (b % 2), :],
                                             tb_head[:, 64 * (6 - 2 * b):64 * (14 - 2 * b)], -1.0, 3.0e38, ALU.add,
                                             ALU.min, mx[:, b, 0:1])
                    link(dve.reduce_max(mx[:, b, 2:3], G[:, 2 * (b % 2) + 1, 0:CTX], AX.X))
                    one = dve.scalar_tensor_tensor(mx[:, b, 1:2], mx[:, b, 2:3], -1.0, mx[:, b, 0:1], ALU.mult,
                                                   ALU.min)
                else:
                    n, least = b * P, 3.0e38
                    if b:
                        link(dve.tensor_tensor_reduce(lg[:, b, 0:n], G[:, b, 0:n], c["N0"][:, e, 0:n], -1.0, least,
                                                      ALU.add, ALU.min, mx[:, b, 0:1]))
                        dve.memset(tok[:, 36 + b:37 + b], 0.0)
                        least = mx[:, b, 0:1]
                    one = dve.tensor_tensor_reduce(lg[:, b, n:n + P], G[:, b, n:n + P], c["N1"][:, e, n:n + P], -1.0,
                                                   least, ALU.add, ALU.min, mx[:, b, 1:2])
                one.then_inc(d["m"], 1)

            def scaled(h, b):
                dve.wait_ge(d["e"], h * 4 + (b + 3))
                n = T + CTX if ctx_keys else (b + 1) * P
                if ctx_keys:
                    link(dve.tensor_scalar(rsum[:, b, 0:1], rsum[:, b, 0:1], rsum[:, b, 1:2], None, ALU.add))
                link(dve.reciprocal(rsum[:, b, 2:3], rsum[:, b, 0:1]))
                dve.tensor_scalar(lg[:, b, 0:n], lg[:, b, 0:n], rsum[:, b, 2:3], None, ALU.mult).then_inc(d["p"], 1)

            def diagonal(h):
                dve.wait_ge(d["bc"], h + 1)
                dve.scalar_tensor_tensor(Dg[:], c_T[:, :, ds(h, 1)].to_broadcast([P, TB, P]), -1.0, ident4,
                                         ALU.mult, ALU.mult).then_inc(d["dg"], 1)

            def masked(h, e):
                dve.wait_ge(d["n0"], h + 2)
                link(dve.tensor_tensor(c["N1"][:, e, :].rearrange("p (b n) -> p b n", b=4),
                                       c["N0"][:, e, :].rearrange("p (b n) -> p b n", b=4),
                                       mask_ts[:].unsqueeze(1).to_broadcast([P, TB, P]), ALU.add))

            def biases(h):
                link(dve.tensor_copy(tb_head[:], tbias[:, ds(h, 1)].rearrange("p a x k -> p (a x k)")))

            def output(h, e, i):
                dve.wait_ge(d["o"], h + 3)
                out_tile(e, i).then_inc(d["y"], 1)

            def body(i, first, last):
                for e in range(2):
                    h = i * 2 + e
                    for b in range(TB):
                        logits(h, e, b)
                        if b >= 2:
                            scaled(h, b - 2)
                        elif not (first and e == 0):
                            scaled(h + (-1), b + 2)
                        if not (last and e == 1):
                            if b == 1 and not ctx_keys:
                                diagonal(h + 1)
                            if b == 3 and not ctx_keys:
                                masked(h + 1, 1 - e)
                            if b == 3 and ctx_keys:
                                biases(h + 1)
                        if b == 3 and e == 1 and not last:
                            dve.wait_ge(d["s"], i * 8 + 8)
                            keys_queries(i + 1).then_inc(d["stg"], 1)
                        if b == 3 and not (first and e == 0):
                            output(h + (-1), 1 - e, i if e else i + (-1))
                        if b == 3 and e == 0:
                            dve.wait_ge(d["o"], i * 2 + 2)
                            values_in(i).then_inc(d["stv"], 1)

            def tail():
                h = 2 * c["pairs"] - 1
                scaled(h, 2)
                scaled(h, 3)
                output(h, 1, c["pairs"] - 1)

            if ctx_keys:
                biases(0)
            else:
                diagonal(0)
            keys_queries(0).then_inc(d["stg"], 1)
            if not ctx_keys:
                masked(0, 0)

            def counted(i, first, last):
                if not first and not last:
                    link.enter(i + (-1), 2 * (13 if ctx_keys else 8))
                body(i, first, last)
                if not first and not last:
                    link.leave(c["pairs"] - 2)

            skewed(c["pairs"], dve.Fori, counted, tail)

        def fox_pe(pe):
            pe.wait_ge(row_c, 4)
            for b in range(TB):
                mm = pe.transpose(M[:, 3, b * 16:b * 16 + 16], rows[0:16, 4, b * P:b * P + P], ident[0:16, 0:16])
            mm.then_inc(row_t, 1)
            pe.wait_ge(freed_a, 2 + plan["x_g"]["totals"][0])
            soft_pe(pe, fox)

        def fox_act(act):
            act.wait_ge(g_mm, 2)
            act.wait_ge(chunk_used, used_after("x_g"))
            act.wait_ge(h_lo, FILL["pre1"] + 8)
            act.activation(rows[0:16, 1, :], M[0:16, 2, :], ACT.Identity, bias=b_x[:, 0:1]).then_inc(row_a, 1)
            act.wait_ge(row_d, 2)
            act.activation(rows[0:16, 2, :], rows[0:16, 2, :], ACT.Exp).then_inc(row_a, 1)
            act.wait_ge(row_a, 6)
            act.activation(rows[0:16, 9, :], rows[0:16, 2, :], ACT.Ln, bias=1.0).then_inc(row_a, 1)
            act.wait_ge(row_t, 2)
            soft_act(act, fox)
            split_act(act, "fox", lambda t: act.wait_ge(fx["y"], 17), Y)

        def fox_dve(dve, link):
            dve.wait_ge(chunk_used, used_after("x_g"))
            link(dve.memset(rows[0:16, 8, :], 1.0))
            dve.wait_ge(row_a, 5)
            dve.scalar_tensor_tensor(rows[0:16, 2, :], rows[0:16, 1, :], -1.0, rows[0:16, 1, :], ALU.mult,
                                     ALU.min).then_inc(row_d, 1)
            dve.wait_ge(row_a, 7)
            link(dve.scalar_tensor_tensor(rows[0:16, 3, :], rows[0:16, 1, :], 0.0, rows[0:16, 9, :], ALU.min,
                                          ALU.subtract))
            dve.tensor_tensor_scan(rows[0:16, 4, :], rows[0:16, 8, :], rows[0:16, 3, :], 0.0, ALU.mult,
                                   ALU.add).then_inc(row_c, 2)
            dve.wait_ge(row_t, 2)
            link(dve.tensor_copy(c_T[:].rearrange("p b h -> p (b h)"), M[:, 3, 0:64]))
            dve.wait_ge(freed_a, 2 + plan["x_g"]["totals"][0])
            def keys_queries(i):
                dve.tensor_copy(fox["Kp"], xK[:, ds(i, 1), :].rearrange("p a n -> p (a n)"))
                return dve.tensor_copy(fox["Qp"], xQ[:, ds(i, 1), :].rearrange("p a n -> p (a n)"))

            def values_in(i):
                return dve.tensor_copy(fox["Vp"].rearrange("p (b n) -> p b n", b=4), xV[:, :, ds(i * P, P)])

            def out_tile(e, i):
                yv = Y[HP * e:HP * e + HP, ds(i, 1), :].rearrange("p a n -> p (a n)")
                return dve.tensor_tensor(yv, M[0:HP, 0, :], yv, ALU.mult)

            soft_dve(dve, link, fox, keys_queries, values_in, out_tile, 0)
            split_dve(dve, "fox", Y)

        def second_loads(sp, load_stage, cols, pairs):
            w_in = a["w_in_2"][0]
            load_stage("c_k", cols(w_in, 1536))
            load_stage("c_v", cols(w_in, 2048))
            load_stage("n_u", cols(w_in, 0))
            load_stage("n_g", cols(w_in, 512))
            load_stage("n_q", cols(w_in, 1024))
            load_stage("n_k", cols(w_in, 1536))
            load_stage("n_v", cols(w_in, 2048))
            load_stage("n_out", cols(a["w_out_2"][0], 0))

            def ffn2(layer):
                for part in range(4):
                    load_stage(f"s{layer}_up{part}", cols(a["w_ff1_2"][layer], D * part))
                    load_stage(f"s{layer}_down{part}", cols(a["w_ff2_2"][layer][D * part:D * part + D, :], 0))

            ffn2(0)
            load_stage("p_1", pairs(a["w_pw1_2"][0], 0, D))
            load_stage("p_2", cols(a["w_pw2_2"][0], 0))
            ffn2(1)
            sp.wait_ge(fin_c, 8)
            out_v = out.rearrange("a (b p) d -> p (a b) d", p=P)
            sp.dma_start(out_v, x_tm[:]).then_inc(done, 16)
            sp.wait_ge(done, 16)

        def bias_pe(pe):
            pe.wait_ge(rp_dma, 32)
            pe.wait_ge(setup_p, 3)
            pe.wait_ge(freed_d, 2 + plan["f1_down2"]["totals"][1])
            pe.transpose(M[0:64, 2, 0:120], rp[:], ident[0:120, 0:120]).then_inc(tb_t, 1)
            pe.wait_ge(tb_r, 2)
            with pe.Fori(0, 2) as i:
                for q in range(2):
                    pe.wait_ge(sel_dma[q], i * 16 + 16)
                    for r in range(4):
                        pe.wait_ge(tb_e, i * 8 + (4 * q + r + 1))
                        for k in range(4):
                            mm = pe.matmul(G[:, r, k * 112:k * 112 + 112],
                                           sel[:, q, (4 * r + k) * P:(4 * r + k) * P + P],
                                           rm[:].rearrange("p h x -> p (h x)"), start=(k == 0), stop=(k == 3),
                                           skip_group_check=True)
                        if r < 3:
                            mm.then_inc(tb_b, 1)
                    mm.then_inc(tb_mm, 1)

        def bias_act(act):
            act.wait_ge(tb_t, 1)
            act.wait_ge(chunk_used, used_after("f1_up2"))
            t = M[:, 2, 0:120].rearrange("p (h r) -> p h r", r=15)
            act.activation(rm[0:32], t[0:32, :, 1:15], ACT.Copy).then_inc(tb_r, 1)
            act.activation(rm[32:64], t[32:64, :, 0:14], ACT.Copy).then_inc(tb_r, 1)
            act.wait_ge(mod_s, 1)
            act.wait_ge(fx["stg"], 8)
            act.wait_ge(fx["o"], 18)
            tv = tbias[:].rearrange("p h x k -> p (h x) k").rearrange("p y k -> p k y")
            with act.Fori(0, 2) as i:
                for q in range(2):
                    for r in range(4):
                        if r < 3:
                            act.wait_ge(tb_b, i * 6 + (3 * q + r + 1))
                        else:
                            act.wait_ge(tb_mm, i * 2 + (q + 3))
                        act.activation(tv[:, ds(i * 32 + (16 * q + 4 * r), 4), :],
                                       G[:, r, 0:448].rearrange("p (k y) -> p k y", y=112),
                                       ACT.Copy).then_inc(tb_e, 1)

        def even_pe(pe, spread):
            pe.wait_ge(wsp_dma, 16)
            for g in range(4):
                mm = pe.transpose(M[:, 2, g * P:g * P + P], S[:, 0, g * P:g * P + P], ident[:])
            mm.then_inc(sg_t, 1)
            spread(sg_dg, 1, sg_bc)
            pe.wait_ge(sg_n, 1)
            pe.wait_ge(sg_w, 1)
            pe.wait_ge(freed_a, 2 + plan["n_v"]["totals"][0])
            for g in range(4):
                for b in range(TB):
                    mm = pe.matmul(G[:, g, b * P:b * P + P], g_tm[:, b, g * P:g * P + P],
                                   S[:, 1, g * P:g * P + P], start=(b == 0), stop=(b == 3),
                                   skip_group_check=True)
                mm.then_inc(sg_m, 1)
            soft_pe(pe, near)

        def even_act(act):
            act.wait_ge(sg_t, 1)
            act.activation(S[:, 1, :], M[:, 2, :], ACT.Copy).then_inc(sg_w, 1)
            act.wait_ge(sg_bc, 1)
            act.wait_ge(chunk_used, used_after("n_v"))
            act.activation(N0, M[:, 1, :], ACT.Copy).then_inc(sg_b, 1)
            act.wait_ge(sg_v, 1)
            act.activation(bn[:, :, 1:2], bn[:, :, 1:2], ACT.Sqrt, bias=eps[:, 0:1]).then_inc(sg_r, 1)
            soft_act(act, near)
            split_act(act, "mix", lambda t: act.wait_ge(na["y"], 9), Y)

        def even_dve(dve, link):
            dve.tensor_tensor(Dg[:], ident4, VT[:, ROW["b_sp_2"]:ROW["b_sp_2"] + 4].unsqueeze(2).to_broadcast(
                [P, 4, P]), ALU.mult).then_inc(sg_dg, 1)
            dve.wait_ge(freed_a, 2 + plan["n_v"]["totals"][0])
            dve.wait_ge(chunk_used, used_after("n_v"))
            st = att[:, 7936:8032].rearrange("p (j k) -> p j k", k=6)
            for j in range(16):
                one = dve.bn_stats(st[:, j, :], g_tm[:, j // 4, (j % 4) * P:(j % 4) * P + P])
            link(one)
            for j in range(16):
                one = dve.bn_aggr(bn[:, j, :], st[:, j, :])
            one.then_inc(sg_v, 1)
            dve.wait_ge(sg_r, 1)
            link(dve.reciprocal(bn[:, :, 1:2], bn[:, :, 1:2]))
            for j in range(16):
                v = g_tm[:, j // 4, (j % 4) * P:(j % 4) * P + P]
                one = dve.tensor_scalar(v, v, bn[:, j, 0:1], bn[:, j, 1:2], ALU.subtract, ALU.mult)
            one.then_inc(sg_n, 1)
            dve.wait_ge(sg_b, 1)
            for g in range(4):
                dve.wait_ge(sg_m, g + 1)
                link(dve.scalar_tensor_tensor(S[:, 2 + g % 2, :].rearrange("p (b n) -> p b n", b=4),
                                              G[:, g, :].rearrange("p (b n) -> p b n", b=4), vt("ln_v_g_2", g),
                                              N0[:, g * P:g * P + P].unsqueeze(1).to_broadcast([P, 4, P]),
                                              ALU.mult, ALU.add))
                link(dve.tensor_tensor(Y[:, g, :], S[:, 2 + g % 2, :], Y[:, g, :], ALU.mult))
            dve.wait_ge(tb_e, 20)

            def keys_queries(i):
                for dst, src in ((Kt[:, 0:T], nK), (Kt[:, T:T + CTX], cK), (near["Qp"], nQ)):
                    one = dve.tensor_copy(dst, src[:, ds(i, 1), :].rearrange("p a n -> p (a n)"))
                return one

            def values_in(i):
                dve.tensor_copy(near["Vp"][:, 0:T].rearrange("p (b n) -> p b n", b=4), nV[:, :, ds(i * P, P)])
                return dve.tensor_copy(near["Vp"][:, T:T + CTX].rearrange("p (b n) -> p b n", b=2),
                                       cV[:, :, ds(i * P, P)])

            def out_tile(e, i):
                return dve.tensor_copy(Y[HP * e:HP * e + HP, ds(i + 4, 1), :].rearrange("p a n -> p (a n)"),
                                       M[0:HP, 0, :])

            Kt = near["Kp"]
            soft_dve(dve, link, near, keys_queries, values_in, out_tile, 4)
            dve.memset(tok[:, 4:5], 0.0).then_inc(aux_free, 1)
            split_dve(dve, "mix", Y)

        def add_to_x(dve, name, mod, first):
            dve.wait_ge(freed_d, 2 + plan[name]["before"][1])

            def evacuate(i, p, g):
                for m in range(2):
                    x = X[:, ds(g * 2 + m, 1), :]
                    one = dve.scalar_tensor_tensor(x, G[:, 2 * p + m:2 * p + m + 1, :], mod[:, ds(g * 2 + (m + first), 1)],
                                                   x, ALU.mult, ALU.add)
                one.then_inc(freed_d, 1)
            groups(dve, name, split_lo, evacuate)

        def ffn2_act(act, layer, then):
            for part in range(4):
                base = HIDDEN[f"s{layer}"] + 4 * part

                def up(i, p, g):
                    act.wait_ge(hid_l, g + (base + 1))
                    act.activation(S[:, 0:2, :], G[:, 2 * p:2 * p + 2, :], ACT.Relu).then_inc(freed_a, 1)
                    act.wait_ge(f_m, g + (base + 1))
                    act.activation(two(hid_hi, g), S[:, 2:4, :], ACT.Copy).then_inc(hid_h, 1)

                groups(act, f"s{layer}_up{part}", split_hi, up)
                groups(act, f"s{layer}_down{part}", split_hi,
                       squares_act(act, then, X, f"s{layer}_down3") if part == 3 else None)

        def ffn2_dve(dve, link, layer):
            for part in range(4):
                base = HIDDEN[f"s{layer}"] + 4 * part
                freed = plan[f"s{layer}_up{part}"]["freed"]

                def up(i, p, g):
                    dve.wait_ge(freed_a, g + (2 + freed + 1))
                    dve.tensor_tensor(S[:, 2:4, :], S[:, 0:2, :], S[:, 0:2, :], ALU.mult).then_inc(f_m, 1)
                    dve.wait_ge(hid_h, g + (base + 1))
                    dve.tensor_tensor(two(hid_lo, g), S[:, 2:4, :], two(hid_hi, g), ALU.subtract).then_inc(hid_l, 1)

                groups(dve, f"s{layer}_up{part}", split_lo, up)
                if layer == 0 and part == 3:
                    mod_dve(dve, link, 1)
                add_to_x(dve, f"s{layer}_down{part}", mods[layer], 40)

        def second_pe(pe, linear, norm, from_h, spread, squares_behind):
            bias_pe(pe)
            pe.wait_ge(ctx_dma, 16)
            for t in range(DT):
                if t >= 2:
                    pe.wait_ge(ct_c, t - 1)
                if t == 0:
                    pe.wait_ge(tb_r, 2)
                for b in range(2):
                    mm = pe.transpose(M[:, 2 + t % 2, b * P:b * P + P], ctx_tm[:, b, t * P:t * P + P], ident[:])
                mm.then_inc(ct_t, 1)
            norm("ctx", 2)
            pe.wait_ge(tb_e, 20)
            linear("c_k", H_hi, H_lo, need=from_h("ctx"), n=CTX)
            linear("c_v", H_hi, H_lo, "T", need=from_h("ctx"), n=CTX)
            norm("even")
            for name, mode in (("n_u", "F"), ("n_g", "T"), ("n_q", "F"), ("n_k", "F"), ("n_v", "T")):
                linear(name, H_hi, H_lo, mode, need=from_h("even"))
            even_pe(pe, spread)
            linear("n_out", H_hi, H_lo, need=from_h("mix"), behind=squares_behind("mlp0"))

            def ffn2(layer, then):
                for part in range(4):
                    base = HIDDEN[f"s{layer}"] + 4 * part
                    linear(f"s{layer}_up{part}", H_hi, H_lo, need=from_h(f"mlp{layer}"))
                    if layer == 0 and part == 3:
                        mod_pe(pe, 1)
                    linear(f"s{layer}_down{part}", hid_hi, hid_lo,
                           need=lambda t, base=base: pe.wait_ge(hid_l, base + t // 2 + 2),
                           behind=squares_behind(then) if part == 3 else None)

            ffn2(0, "odd")

            def taps(g, p):
                pe.wait_ge(cv_w, g + 1)
                pe.wait_ge(freed_d, g + (2 + plan["p_1"]["freed"] + 1))
                pe.wait_ge(cv_d, g + 1)
                for j in range(PE_TAPS):
                    mm = pe.matmul(M[:, 2 + p, :], tap_diag[:, p, j, :], yp[:, p, V_TAPS + j:V_TAPS + j + T],
                                   start=(j == 0), stop=(j == PE_TAPS - 1))
                mm.then_inc(cv_pe, 1)

            linear("p_1", H_hi, H_lo, need=from_h("odd"), behind=taps)
            for t in range(DT):
                pe.wait_ge(cv_d, t + 3)
                mm = pe.matmul(M[:, 1, :], ones[:], Y[:, t, :], start=(t == 0), stop=(t == 7))
            mm.then_inc(cv_s, 1)
            norm("conf")
            linear("p_2", H_hi, H_lo, need=from_h("conf"), behind=squares_behind("mlp1"))
            ffn2(1, "final")
            for t in range(DT):
                pe.wait_ge(fin_t, t + 1)
                if t >= 4:
                    pe.wait_ge(fin_c, t - 3)
                for b in range(TB):
                    mm = pe.transpose(G[:, t % 4, b * P:b * P + P], S[:, t % 4, b * P:b * P + P], ident[:])
                mm.then_inc(fin_m, 1)

        def second_act(act):
            bias_act(act)
            act.wait_ge(mod_ok, 1)
            norm_act(act, "ctx", ct, lambda t: act.wait_ge(ct_c, t + 1), 2)
            fill_act(act, "ctx", None, lambda t: cmod[:, t:t + 1], used_after("f1_up2"), CTX)
            act.wait_ge(tb_mm, 6)
            plain(act, "c_k", lambda g: two(cK, g), lambda p: G[:, 2 * p:2 * p + 2, 0:CTX])
            plain(act, "c_v", lambda g: cV[:, :, ds(g * GC, GC)],
                  lambda p: G[:, 2 * p, :].rearrange("p (b n) -> p b n", b=2))
            act.wait_ge(x_ready, RESIDS["fpost1"] + 8)
            norm_act(act, "even", X, lambda t: None)
            fill_act(act, "even", None, lambda t: mods[0][:, t:t + 1], used_after("c_v"))
            tokens_out = lambda p: G[:, 2 * p:2 * p + 2, :].rearrange("p a (b n) -> p (a b) n", b=2)
            plain(act, "n_u", lambda g: two(Y, g), None, ACT.Gelu_apprx_tanh)
            plain(act, "n_g", lambda g: g_tm[:, :, ds(g * GC, GC)], tokens_out, ACT.Gelu_apprx_tanh)
            plain(act, "n_q", lambda g: two(nQ, g), None, ACT.Copy, 0.125)
            plain(act, "n_k", lambda g: two(nK, g))
            plain(act, "n_v", lambda g: nV[:, :, ds(g * GC, GC)], tokens_out)
            even_act(act)
            groups(act, "n_out", split_hi, squares_act(act, "mlp0", X, "n_out"))
            norm_act(act, "mlp0", None, None)
            fill_act(act, "mlp0", None, lambda t: mods[0][:, 24 + t:25 + t], used_after("n_out"))
            ffn2_act(act, 0, "odd")
            norm_act(act, "odd", None, None)
            act.wait_ge(mod_ok, 2)
            fill_act(act, "odd", None, lambda t: mods[1][:, t:t + 1], used_after("s0_up3"))

            def glu(i, p, g):
                act.wait_ge(freed_d, g + (plan["p_1"]["freed"] + 1))
                act.activation(S[:, p, :], G[:, 2 * p + 1, :], ACT.Sigmoid,
                               bias=VT[:, ds(g + (ROW["b_pw1_2"] + 8), 1)]).then_inc(glu_a, 1)

            groups(act, "p_1", split_hi, glu)
            norm_act(act, "conf", Y, lambda t: act.wait_ge(cv_m, t + 1))
            for t in range(DT):
                act.wait_ge(cv_t, t + 1)
                act.activation(Y[:, t, :], S[:, t % 4, :], ACT.Silu, bias=vt("ln_c_b_2", t)).then_inc(cv_y, 1)
                if t:
                    split_one(act, t - 1)
            split_one(act, 7)
            groups(act, "p_2", split_hi, squares_act(act, "mlp1", X, "p_2"))
            norm_act(act, "mlp1", None, None)
            fill_act(act, "mlp1", None, lambda t: mods[1][:, 24 + t:25 + t], used_after("p_2"))
            ffn2_act(act, 1, "final")
            norm_act(act, "final", None, None)
            for t in range(DT):
                act.wait_ge(fin_m, t + 1)
                act.activation(x_tm[:, :, t * P:t * P + P], G[:, t % 4, :].rearrange("p (b n) -> p b n", b=4),
                               ACT.Copy).then_inc(fin_c, 1)

        def split_one(act, t):
            act.wait_ge(cv_y, t + 1)
            act.activation(H_hi[:, t, :], Y[:, t, :], ACT.Copy).then_inc(h_hi, 1)

        def plain(act, name, dst, src=None, func=ACT.Copy, scale=1.0, then=None):
            def evacuate(i, p, g):
                s = src(p) if src else G[:, 2 * p:2 * p + 2, :]
                act.activation(dst(g), s, func, scale=scale).then_inc(freed_a, 1)
                if then:
                    then(i, p, g)
            groups(act, name, split_hi, evacuate)

        def second_dve(dve, link):
            for t in range(DT):
                dve.wait_ge(ct_t, t + 1)
                dve.tensor_copy(ct[:, t, :], M[:, 2 + t % 2, 0:CTX]).then_inc(ct_c, 1)
            dve.wait_ge(mod_ok, 1)
            dve.wait_ge(x_ready, RESIDS["fpost1"] + 8)
            pre_dve(dve, "ctx", ct, lambda t: cgain[:, t:t + 1], lambda t: cmod[:, t:t + 1], used_after("f1_up2"), 2)
            for name in ("c_k", "c_v"):
                groups(dve, name, split_lo, None)
            pre_dve(dve, "even", X, lambda t: gain1[:, t:t + 1], lambda t: mods[0][:, t:t + 1], used_after("c_v"))
            for name in ("n_u", "n_g", "n_q", "n_k", "n_v"):
                groups(dve, name, split_lo, None)
            even_dve(dve, link)
            add_to_x(dve, "n_out", mods[0], 16)
            pre_dve(dve, "mlp0", X, lambda t: gain2[:, t:t + 1], lambda t: mods[0][:, 24 + t:25 + t],
                    used_after("n_out"))
            ffn2_dve(dve, link, 0)
            dve.wait_ge(chunk_used, used_after("s0_down3"))
            link(dve.memset(yp[:], 0.0))
            pre_dve(dve, "odd", X, lambda t: gain1[:, t:t + 1], lambda t: mods[1][:, t:t + 1], used_after("s0_up3"))

            def total(g, p):
                dve.wait_ge(cv_pe, g + 3)
                y = Y[:, ds(g, 1), :]
                dve.tensor_tensor(y, y, M[:, 2 + p:3 + p, :], ALU.add).then_inc(cv_d, 1)

            def glu(i, p, g):
                looped = not isinstance(i, int)
                if p == 0 and looped:
                    link.enter(i + (-1), 2 * V_TAPS)
                dve.wait_ge(glu_a, g + 1)
                dve.wait_ge(cv_pe, g + 1)
                dve.scalar_tensor_tensor(yp[:, p:p + 1, PAD:PAD + T], G[:, 2 * p:2 * p + 1, :],
                                         VT[:, ds(g + ROW["b_pw1_2"], 1)], S[:, p:p + 1, :], ALU.add,
                                         ALU.mult).then_inc(freed_d, 1)
                dve.wait_ge(freed_d, g + (2 + plan["p_1"]["freed"] + 1))
                y, other = Y[:, ds(g, 1), :], S[:, 2:3, :]
                tap = lambda j: VT[:, ds(g + (ROW["w_dw_2"] + 8 * j), 1)]
                link.post(dve.tensor_scalar(y, yp[:, p:p + 1, 0:T], tap(0), VT[:, ds(g + ROW["b_dw_2"], 1)],
                                            ALU.mult, ALU.add))
                link.post(dve.tensor_scalar(other, yp[:, p:p + 1, 1:1 + T], tap(1), None, ALU.mult))
                for j in range(2, V_TAPS):
                    acc = other if j % 2 else y
                    link.wait(1)
                    link.post(dve.scalar_tensor_tensor(acc, yp[:, p:p + 1, j:j + T], tap(j), acc, ALU.mult, ALU.add))
                link.wait(0)
                if looped or p:
                    total(g + (-1), 1 - p)
                dve.tensor_tensor(y, y, other, ALU.add).then_inc(cv_v, 1)
                dve.wait_ge(cv_v, g + 1)

            groups(dve, "p_1", split_lo, glu, peel=True)
            link.leave(DT // 2 - 1)
            total(DT - 1, 1)
            dve.wait_ge(cv_s, 1)
            for t in range(DT):
                dve.scalar_tensor_tensor(Y[:, t, :], M[:, 1, :], -1.0 / D, Y[:, t, :], ALU.mult,
                                         ALU.add).then_inc(cv_m, 1)
            for t in range(DT):
                one = dve.tensor_scalar(X[:, t, :], X[:, t, :], gb[:, t:t + 1], None, ALU.add)
            link(one)
            row = norm_dve(dve, "conf")

            def low(t):
                dve.wait_ge(h_hi, FILL["conf"] + t + 1)
                dve.tensor_tensor(H_lo[:, t, :], Y[:, t, :], H_hi[:, t, :], ALU.subtract).then_inc(h_lo, 1)

            for t in range(DT):
                if t >= 4:
                    dve.wait_ge(cv_y, t - 3)
                dve.scalar_tensor_tensor(S[:, t % 4, :], Y[:, t, :], vt("ln_c_g_2", t), row, ALU.mult,
                                         ALU.mult).then_inc(cv_t, 1)
                if t >= 2:
                    low(t - 2)
            low(6)
            low(7)
            add_to_x(dve, "p_2", mods[1], 16)
            pre_dve(dve, "mlp1", X, lambda t: gain2[:, t:t + 1], lambda t: mods[1][:, 24 + t:25 + t], used_after("p_2"))
            ffn2_dve(dve, link, 1)
            row = norm_dve(dve, "final")
            for t in range(DT):
                if t >= 4:
                    dve.wait_ge(fin_m, t - 3)
                dve.scalar_tensor_tensor(S[:, t % 4, :], X[:, t, :], vt("final_g_2", t), row, ALU.mult,
                                         ALU.mult).then_inc(fin_t, 1)

        @block.sync
        def _(sp):
            sp.dma_start(x_tm[:], a["x"].rearrange("b (t p) d -> p (b t) d", p=P)).then_inc(x_dma, 16)
            sp.dma_start(ident[:], consts["ident"]).then_inc(c_dma, 16)
            sp.dma_start(mask_ts[:], consts["mask"]).then_inc(c_dma, 16)
            sp.dma_start(mask_st[:], consts["mask_t"]).then_inc(c_dma, 16)
            sp.dma_start(b_m[:], a["mlstm_b_gate"].rearrange("a (g h) -> (a h) g", g=2),
                         allow_slow_non_contiguous=True).then_inc(c_dma, 16)
            sp.dma_start(b_x[:], a["kv_b_f"].rearrange("(h a) -> h a", a=1),
                         allow_slow_non_contiguous=True).then_inc(c_dma, 16)

            def load_chunk(src, j, n=KC):
                dst = raw[:, j, :].rearrange("p (k n) -> p k n", k=KC)[:, 0:n, :]
                if len(src.shape) == 4:
                    for h in range(2):
                        sp.dma_start(dst[:, :, h * P:h * P + P], src[:, :, h, :]).then_inc(raw_landed[j], 16)
                else:
                    sp.dma_start(dst, src).then_inc(raw_landed[j], 32)

            def load_stage(name, source):
                st = plan[name]
                with sp.Fori(0, st["groups"] // 2) as i:
                    for p in range(2):
                        src = source(i * 2 + p)
                        for j in range(2):
                            c = 2 * p + j
                            k1 = min(KC, st["ktiles"] - KC * j)
                            sp.wait_ge(lo_done, i * 4 + (st["chunk"] + c + 1))
                            load_chunk(src[:, KC * j:KC * j + k1], c, k1)

            def cols(w, first):
                wv = w.rearrange("(k p) n -> p k n", p=P)
                return lambda g: wv[:, :, ds(g * GC + first, GC)]

            def pairs(w, first, half):
                wv = w.rearrange("(k p) (h n) -> p k h n", p=P, h=2)
                return lambda g: wv[:, :, :, ds(g * P + first, P)]

            sp.wait_ge(setup_p, 1)
            for name, n, r, m in vector_dmas():
                names = " ".join("abcd"[:len(a[name].shape)])
                flat = a[name].rearrange(f"{names} -> ({names})").rearrange("(r p) -> r p", p=P)
                sp.dma_start(v_rows[r % P:r % P + m, r // P, :], flat[n:n + m, :]).then_inc(v_dma, 16)
            w_in = a["mlstm_w_in"].rearrange("a d n -> (a d) n")
            load_stage("m_q", cols(w_in, 0))
            sp.wait_ge(setup_p, 2)
            for i in range(2):
                sp.dma_start(gw_raw[:, :, 32 * i:32 * i + 8],
                             w_in.rearrange("(k p) n -> p k n", p=P)[:, :, 3072 + 8 * i:3080 + 8 * i],
                             allow_slow_non_contiguous=True).then_inc(g_dma, 16)
            load_stage("m_k", cols(w_in, 512))
            load_stage("m_v", cols(w_in, 1024))
            load_stage("m_o", cols(w_in, 2048))
            load_stage("m_out", cols(a["mlstm_w_out"].rearrange("a d n -> (a d) n"), 0))

            def ffn1(layer):
                for part, n in enumerate((8, 8, 6)):
                    load_stage(f"f{layer}_up{part}", pairs(a["ffn_w_up"][layer], 8 * P * part, FF1))
                    down = a["ffn_w_down"][layer][8 * P * part:8 * P * part + n * P, :]
                    load_stage(f"f{layer}_down{part}", cols(down, 0))

            ffn1(0)
            load_stage("kv_k", cols(a["kv_w"], 0))
            load_stage("kv_v", cols(a["kv_w"], 1024))
            load_stage("x_q", cols(a["fox_w_qg"][0], 0))
            load_stage("x_g", cols(a["fox_w_qg"][0], 1024))
            load_stage("x_out", cols(a["fox_w_out"][0], 0))
            ffn1(1)
            second_loads(sp, load_stage, cols, pairs)

        @block.gpsimd
        def _(pool):
            pool.memset(v_rows[:], 0.0).then_inc(setup_p, 1)
            pool.memset(ones[:], 1.0).then_inc(chunk_used, 4)
            pool.memset(eps[:], EPS).then_inc(lo_done, 4)
            pool.wait_ge(setup_t, 9)
            pool.memset(gw_raw[:], 0.0).then_inc(setup_p, 1)
            pool_mod(pool)
            pool.wait_ge(chunk_used, used_after("s0_down3"))
            taps = VT[:, ROW["w_dw_2"]:ROW["w_dw_2"] + 8 * CONV_K].rearrange("p (j t) -> p j t", t=8)
            with pool.Fori(0, DT // 2) as i:
                for p in range(2):
                    pool.wait_ge(cv_pe, i * 2 + (p + 1))
                    pool.tensor_tensor(tap_diag[:, p], ident[:].unsqueeze(1).to_broadcast([P, PE_TAPS, P]),
                                       taps[:, V_TAPS:CONV_K, ds(i * 2 + p, 1)].to_broadcast([P, PE_TAPS, P]),
                                       ALU.mult).then_inc(cv_w, 1)

        @block.tensor
        def _(pe):
            def linear(name, hi, lo, mode="F", need=None, n=T, behind=None):
                st = plan[name]
                sem_, base = (freed_a, st["freed"]) if st["by"] == "A" else (freed_d, st["freed"])
                pe.wait_ge(freed_a, 2 + st["before"][0])
                pe.wait_ge(freed_d, 2 + st["before"][1])

                def body(i, first):
                    for p in range(2):
                        pe.wait_ge(sem_, i * 2 + (base + p + 1))
                        for j in range(2):
                            c = 2 * p + j
                            pe.wait_ge(lo_done, i * 4 + (st["chunk"] + c + 5))
                            nk = min(KC, st["ktiles"] - KC * j)
                            wh = w_hi[:, c, :].rearrange("p (k n) -> p k n", k=KC)
                            wl = w_lo[:, c, :].rearrange("p (k n) -> p k n", k=KC)
                            if mode == "F":
                                for k in range(nk):
                                    for m in range(2):
                                        t = KC * j + k
                                        if p == 0 and m == 0:
                                            need(t)
                                        ms = slice(m * P, m * P + P)
                                        for q, (lw, rh) in enumerate(((wh, hi), (wh, lo), (wl, hi))):
                                            mm = pe.matmul(G[:, 2 * p + m, 0:n], lw[:, k, ms], rh[:, t, 0:n],
                                                           start=(t == 0 and q == 0),
                                                           stop=(t == st["ktiles"] - 1 and q == 2),
                                                           skip_group_check=True)
                            else:
                                for b in range(n // P):
                                    bs = slice(b * P, b * P + P)
                                    for k in range(nk):
                                        t = KC * j + k
                                        if p == 0 and b == 0:
                                            need(t)
                                        for q, (lh, rw) in enumerate(((hi, wh), (lo, wh), (hi, wl))):
                                            mm = pe.matmul(G[:, 2 * p + b // 2, (b % 2) * GC:(b % 2) * GC + GC],
                                                           lh[:, t, bs], rw[:, k, :],
                                                           start=(t == 0 and q == 0 and b % 2 == 0),
                                                           stop=(t == st["ktiles"] - 1 and q == 2 and b % 2 == 1),
                                                           skip_group_check=True)
                            mm.then_inc(chunk_used, 1)
                        if behind and not (first and p == 0):
                            behind(i * 2 + (p - 1), 1 - p)

                if behind:
                    body(0, True)
                    with pe.Fori(0, st["groups"] // 2 - 1) as i:
                        body(i + 1, False)
                    behind(st["groups"] - 1, 1)
                else:
                    with pe.Fori(0, st["groups"] // 2) as i:
                        body(i, True)

            def from_h(fill):
                return lambda t: pe.wait_ge(h_lo, FILL[fill] + t + 1)

            def squares_behind(name):
                first = 8 * NORM[name]

                def behind(g, p):
                    start = isinstance(g, int) and g == 0
                    for m in range(2):
                        pe.wait_ge(n_sq, g * 2 + (first + m + 1))
                        if start and m == 0:
                            pe.wait_ge(n_sd, NORM[name])
                        pe.matmul(M[:, 0, :], ones[:], SQ[:, m, :], start=(start and m == 0),
                                  stop=(isinstance(g, int) and g == 3 and m == 1),
                                  skip_group_check=True).then_inc(n_ss, 1)
                return behind

            def norm(name, blocks=TB):
                i = NORM[name]
                for t in range(DT):
                    pe.wait_ge(n_sq, 8 * i + t + 1)
                    if t == 0 and i:
                        pe.wait_ge(n_sd, i)
                    pe.matmul(M[:, 0, 0:blocks * P], ones[:], SQ[:, t % 2, 0:blocks * P], start=(t == 0),
                              stop=(t == 7)).then_inc(n_ss, 1)

            def spread(diag_ready, value, sent, blocks=TB):
                pe.wait_ge(diag_ready, value)
                pe.matmul(M[:, 1, 0:blocks * P], ones[:], Dg[:, 0:blocks, :].rearrange("p b n -> p (b n)"),
                          start=True, stop=True).then_inc(sent, 1)

            def gate_rows(first, fill):
                pe.wait_ge(g_lo, first + 1)
                for t in range(DT):
                    pe.wait_ge(h_lo, FILL[fill] + t + 1)
                    for q, (lw, rh) in enumerate(((gw_hi, H_hi), (gw_hi, H_lo), (gw_lo, H_hi))):
                        mm = pe.matmul(M[:, 2, :], lw[:, t, :], rh[:, t, :], start=(t == 0 and q == 0),
                                       stop=(t == 7 and q == 2))
                mm.then_inc(g_mm, 1)

            pe.wait_ge(c_dma, 80)
            pe.wait_ge(chunk_used, 4)
            pe.wait_ge(v_dma, 16 * VECTOR_DMAS)
            for r in range(VBLOCKS):
                mm = pe.transpose(G[:, r // 4, (r % 4) * P:(r % 4) * P + P], v_rows[:, r, :], ident[:])
            mm.then_inc(setup_t, 1)
            pe.wait_ge(x_dma, 16)
            for t in range(DT):
                if t >= 2:
                    pe.wait_ge(x_ready, t - 1)
                for b in range(TB):
                    mm = pe.transpose(M[:, 2 + t % 2, b * P:b * P + P], x_tm[:, b, t * P:t * P + P], ident[:])
                mm.then_inc(setup_t, 1)

            norm("pre0")
            pe.wait_ge(setup_c, 1)
            h0 = from_h("pre0")
            linear("m_q", H_hi, H_lo, need=h0)
            linear("m_k", H_hi, H_lo, need=h0)
            gate_rows(0, "pre0")
            linear("m_v", H_hi, H_lo, "T", need=h0)
            linear("m_o", H_hi, H_lo, need=h0)
            mlstm_pe(pe, spread)
            linear("m_out", H_hi, H_lo, need=from_h("mlstm"), behind=squares_behind("post0"))

            def ffn1(layer):
                base = HIDDEN[f"f{layer}"]
                for part in range(3):
                    linear(f"f{layer}_up{part}", H_hi, H_lo, need=from_h(f"ffn{layer}"))
                    if layer == 0 and part == 2:
                        mod_pe(pe, 0)
                    linear(f"f{layer}_down{part}", hid_hi, hid_lo,
                           need=lambda t, part=part: pe.wait_ge(hid_l, base + 8 * part + t + 2),
                           behind=squares_behind(f"fpost{layer}") if part == 2 else None)

            norm("ffn0")
            ffn1(0)
            norm("kv")
            linear("kv_k", H_hi, H_lo, need=from_h("kv"))
            gate_rows(1, "kv")
            linear("kv_v", H_hi, H_lo, "T", need=from_h("kv"))
            norm("pre1")
            linear("x_q", H_hi, H_lo, need=from_h("pre1"))
            linear("x_g", H_hi, H_lo, need=from_h("pre1"))
            fox_pe(pe)
            linear("x_out", H_hi, H_lo, need=from_h("fox"), behind=squares_behind("post1"))
            norm("ffn1")
            ffn1(1)
            second_pe(pe, linear, norm, from_h, spread, squares_behind)
        @block.scalar
        def _(act):
            act.wait_ge(c_dma, 80)
            act.wait_ge(lo_done, 4)
            act.wait_ge(setup_t, 1)
            act.activation(VT[:], G[:, 0:2, :].rearrange("p a n -> p (a n)")[:, 0:VBLOCKS * P],
                           ACT.Copy).then_inc(setup_c, 1)
            act.wait_ge(setup_c, 1)
            act.activation(cs[:], VT[:, ROW["c_2"]:ROW["c_2"] + 16], ACT.Sigmoid).then_inc(cs_ready, 1)
            for j in range(SLOTS):
                split_hi(act, 0, 0, j)
            norm_act(act, "pre0", X, lambda t: act.wait_ge(x_ready, t + 1))
            fill_act(act, "pre0", None, None, None)
            plain(act, "m_q", lambda g: two(mQ, g), None, ACT.Copy, 0.125)
            plain(act, "m_k", lambda g: two(mK, g))
            tokens_out = lambda p: G[:, 2 * p:2 * p + 2, :].rearrange("p a (b n) -> p (a b) n", b=2)
            gate_weights_act(act, 0)
            plain(act, "m_v", lambda g: mV[:, :, ds(g * GC, GC)], tokens_out)
            act.wait_ge(g_mm, 1)
            plain(act, "m_o", lambda g: two(Y, g), None, ACT.Sigmoid)
            mlstm_act(act)
            plain(act, "m_out", lambda g: two(Y, g), then=squares_act(act, "post0", Y, "m_out"))

            def x_from(name):
                return lambda t: act.wait_ge(x_ready, RESIDS[name] + t + 1)

            norm_act(act, "post0", None, None)
            norm_act(act, "ffn0", X, x_from("post0"))
            fill_act(act, "ffn0", None, None, used_after("m_out"))
            ffn1_act(act, 0)
            norm_act(act, "fpost0", None, None)
            norm_act(act, "kv", X, x_from("fpost0"))
            act.wait_ge(g_zero, 1)
            act.dma_start(gw_raw[:, :, 0:16], a["kv_w"].rearrange("(k p) n -> p k n", p=P)[:, :, 2048:2064],
                          allow_slow_non_contiguous=True).then_inc(g_dma, 16)
            fill_act(act, "kv", None, None, used_after("f0_up2"))
            gate_weights_act(act, 1)
            plain(act, "kv_k", lambda g: two(xK, g))
            plain(act, "kv_v", lambda g: xV[:, :, ds(g * GC, GC)], tokens_out)
            norm_act(act, "pre1", X, lambda t: None)
            fill_act(act, "pre1", None, None, used_after("kv_v"))
            act.wait_ge(mod_s, 1)
            plain(act, "x_q", lambda g: two(xQ, g), None, ACT.Copy, 0.125)
            plain(act, "x_g", lambda g: two(Y, g), None, ACT.Sigmoid)
            fox_act(act)
            plain(act, "x_out", lambda g: two(Y, g), then=squares_act(act, "post1", Y, "x_out"))
            norm_act(act, "post1", None, None)
            norm_act(act, "ffn1", X, x_from("post1"))
            fill_act(act, "ffn1", None, None, used_after("x_out"))
            ffn1_act(act, 1)
            norm_act(act, "fpost1", None, None)
            second_act(act)

        @block.vector
        def _(dve):
            link = Chain(dve, chain_d)
            for n, (s, v) in enumerate(TOKENS):
                dve.memset(tok[:, 8 + n:9 + n], 0.0).then_inc(s, v)
            dve.wait_ge(c_dma, 80)
            for t in range(DT):
                dve.wait_ge(setup_t, t + 2)
                dve.tensor_copy(X[:, t, :], M[:, 2 + t % 2, :]).then_inc(x_ready, 1)
            for j in range(SLOTS):
                split_lo(dve, 0, 0, j)
            dve.wait_ge(setup_c, 1)
            pre_dve(dve, "pre0", X, lambda t: vt("norm_mix_pre", t), None, None)
            groups(dve, "m_q", split_lo, None)
            groups(dve, "m_k", split_lo, None)
            gate_weights_dve(dve, 0)
            groups(dve, "m_v", split_lo, None)
            groups(dve, "m_o", split_lo, None)
            mlstm_dve(dve, link)
            groups(dve, "m_out", split_lo, None)
            residual_dve(dve, "post0", lambda t: vt("norm_mix_post", t))
            pre_dve(dve, "ffn0", X, lambda t: vt("norm_ffn_pre", t), None, used_after("m_out"))
            ffn1_dve(dve, link, 0)
            residual_dve(dve, "fpost0", lambda t: vt("norm_ffn_post", t))
            dve.wait_ge(x_ready, RESIDS["fpost0"] + 8)
            dve.memset(gw_raw[:], 0.0).then_inc(g_zero, 1)
            pre_dve(dve, "kv", X, lambda t: vt("kv_norm", t), None, used_after("f0_up2"))
            gate_weights_dve(dve, 1)
            groups(dve, "kv_k", split_lo, None)
            groups(dve, "kv_v", split_lo, None)
            pre_dve(dve, "pre1", X, lambda t: vt("norm_mix_pre", 8 + t), None, used_after("kv_v"))
            groups(dve, "x_q", split_lo, None)
            groups(dve, "x_g", split_lo, None)
            fox_dve(dve, link)
            groups(dve, "x_out", split_lo, None)
            residual_dve(dve, "post1", lambda t: vt("norm_mix_post", 8 + t))
            pre_dve(dve, "ffn1", X, lambda t: vt("norm_ffn_pre", 8 + t), None, used_after("x_out"))
            ffn1_dve(dve, link, 1)
            residual_dve(dve, "fpost1", lambda t: vt("norm_ffn_post", 8 + t))
            second_dve(dve, link)


class Chain:

    def __init__(self, engine, semaphore):
        self.engine, self.semaphore, self.n, self.i, self.per, self.k = engine, semaphore, 0, None, 0, 0

    def __call__(self, ins):
        ins.then_inc(self.semaphore, 1)
        if self.i is None:
            self.n += 1
            self.engine.wait_ge(self.semaphore, self.n)
        else:
            self.k += 1
            self.engine.wait_ge(self.semaphore, self.i * self.per + (self.n + self.k))

    def post(self, ins):
        ins.then_inc(self.semaphore, 1)
        if self.i is None:
            self.n += 1
        else:
            self.k += 1

    def wait(self, behind):
        base = self.n + (0 if self.i is None else self.k) - behind
        self.engine.wait_ge(self.semaphore, base if self.i is None else self.i * self.per + base)

    def enter(self, i, per):
        self.i, self.per, self.k = i, per, 0

    def leave(self, times):
        assert self.k == self.per, (self.k, self.per)
        self.n += self.per * times
        self.i = None


_NAMES = ["x"] + [n for n, _ in VECTORS] + [
    "mlstm_w_in", "mlstm_b_gate", "mlstm_w_out", "kv_w", "kv_b_f", "fox_w_qg", "fox_w_out", "ffn_w_up",
    "ffn_w_down", "ctx_2", "w_mod_2", "w_in_2", "w_out_2", "w_sp_2", "rpb_2", "w_pw1_2", "w_pw2_2", "w_ff1_2",
    "w_ff2_2"]


def shape_constants():
    import numpy as np

    r = np.arange(P)
    mask = np.where(r[None, :] <= r[:, None], 0.0, NEG).astype(np.float32)
    sel = np.zeros((64, 64, P), np.float32)
    for kc in range(64):
        for qc in range(64):
            start = min(max(qc - 8, 0), 48)
            row = kc - qc + 15 if start <= kc < start + 16 else 31
            sel[row, kc, qc] = 1.0
            sel[32 + row, kc, 64 + qc] = 1.0
    return {"ident": np.eye(P, dtype=np.float32), "mask": mask, "mask_t": np.ascontiguousarray(mask.T),
            "sel": sel.reshape(64, 64 * P)}


def kernel(**inputs):
    import numpy as np
    import concourse.bacc as bacc
    from concourse.bass_utils import run_bass_kernel_spmd

    nc = bacc.Bacc("TRN2", target_bir_lowering=False, num_devices=1)
    arrays, views, consts = {}, {}, {}
    for name in _NAMES:
        v = np.ascontiguousarray(inputs[name])
        arrays[f"in_{name}"] = v
        views[name] = nc.dram_tensor(f"in_{name}", v.shape, F32, kind="ExternalInput").ap()
    for name, v in shape_constants().items():
        arrays[f"const_{name}"] = v
        consts[name] = nc.dram_tensor(f"const_{name}", v.shape, F32, kind="ExternalInput").ap()
    out = nc.dram_tensor("out", (1, T, D), F32, kind="ExternalOutput").ap()
    build(nc, views, out, consts)
    r = run_bass_kernel_spmd(nc, [arrays], core_ids=[0])
    return r.results[0]["out"]
```
